# Optimizing a Trainium2 kernel written in Bass

```python
import math
import jax
import jax.numpy as jnp
from jax import lax
import numpy as np

D_MODEL = 1024
BATCH = 1
SEQ = 1024
DEPTH = 1

DN_HEAD_DIM = 64
DN_WIDTH = D_MODEL // 4
DN_HEADS = DN_WIDTH // DN_HEAD_DIM
DN_CONV = 4
DN_CHUNK = 64
AT_HEAD_DIM = 64
AT_WIDTH = D_MODEL // 2
AT_HEADS = AT_WIDTH // AT_HEAD_DIM
WINDOWS = ((128, 1), (512, 4), (2048, 16))
AT_BLOCK = 128
N_BUCKETS = 32
MAX_DISTANCE = 2048
CV_WIDTH = D_MODEL // 4
CV_KERNEL = 31
MIX_WIDTH = DN_WIDTH + AT_WIDTH + CV_WIDTH
N_IN = 4 * DN_WIDTH + 2 * DN_HEADS + 3 * AT_WIDTH + 2 * CV_WIDTH
N_GROUPS = 4
EXPERTS_PER_GROUP = 8
N_EXPERTS = N_GROUPS * EXPERTS_PER_GROUP
TOP_K = 2
D_EXPERT = D_MODEL // 2
MOE_BLOCK = 128
NEG_INF = -1e30
EPS = 1e-6

kernel_name = 'hymba_style_deltanet_dilated_conformer_hmoe'

def _rms_norm(x, g):
    xf = x.astype(jnp.float32)
    return (xf * lax.rsqrt(jnp.mean(xf * xf, axis=-1, keepdims=True) + EPS) * g).astype(x.dtype)

def _layer_norm(x, g, b):
    xf = x.astype(jnp.float32)
    mu = jnp.mean(xf, axis=-1, keepdims=True)
    var = jnp.mean(jnp.square(xf - mu), axis=-1, keepdims=True)
    return ((xf - mu) * lax.rsqrt(var + EPS) * g + b).astype(x.dtype)

def _l2norm(x):
    return x * lax.rsqrt(jnp.sum(x * x, axis=-1, keepdims=True) + EPS)

def _causal_depthwise_conv(x, w):
    width, ch = w.shape
    return lax.conv_general_dilated(x, w[:, None, :], window_strides=(1,), padding=[(width - 1, 0)],
                                    dimension_numbers=('NWC', 'WIO', 'NWC'), feature_group_count=ch)

def _chunked_gated_delta_rule(q, k, v, g, beta):
    bsz, heads, seq, dk = q.shape
    dv = v.shape[-1]
    n = seq // DN_CHUNK
    q, k, v = (t.reshape(bsz, heads, n, DN_CHUNK, t.shape[-1]) for t in (q, k, v))
    g, beta = (t.reshape(bsz, heads, n, DN_CHUNK) for t in (g, beta))
    G = jnp.cumsum(g, axis=-1)
    idx = jnp.arange(DN_CHUNK)
    causal = idx[:, None] >= idx[None, :]
    strict = idx[:, None] > idx[None, :]
    decay = jnp.exp(jnp.where(causal, G[..., :, None] - G[..., None, :], -jnp.inf))
    kb = k * beta[..., None]
    a_mat = jnp.where(strict, jnp.einsum('bhnid,bhnjd->bhnij', kb, k) * decay, 0.0)
    eye = jnp.eye(DN_CHUNK, dtype=a_mat.dtype)
    t_mat = lax.linalg.triangular_solve(a_mat + eye, jnp.broadcast_to(eye, a_mat.shape),
                                        left_side=True, lower=True, unit_diagonal=True)
    e_g = jnp.exp(G)[..., None]
    w_mat = t_mat @ (kb * e_g)
    u_mat = t_mat @ (v * beta[..., None])
    qk = jnp.einsum('bhnid,bhnjd->bhnij', q, k) * decay
    q_dec = q * e_g
    k_dec = k * jnp.exp(G[..., -1:] - G)[..., None]
    g_last = jnp.exp(G[..., -1])[..., None, None]

    def step(state, xs):
        w_c, u_c, qk_c, qd_c, kd_c, gl_c = xs
        v_new = u_c - w_c @ state
        o_c = qd_c @ state + qk_c @ v_new
        state = state * gl_c + jnp.swapaxes(kd_c, -1, -2) @ v_new
        return state, o_c

    xs = tuple(jnp.moveaxis(t, 2, 0) for t in (w_mat, u_mat, qk, q_dec, k_dec, g_last))
    state0 = jnp.zeros((bsz, heads, dk, dv), q.dtype)
    _, o = lax.scan(step, state0, xs)
    return jnp.moveaxis(o, 0, 2).reshape(bsz, heads, seq, dv)

def _gated_deltanet(q, k, v, z, a, b, conv_w, a_log, dt_bias, out_norm):
    out_dtype = q.dtype
    bsz, seq, _ = q.shape
    qkv = jax.nn.silu(_causal_depthwise_conv(jnp.concatenate([q, k, v], axis=-1), conv_w))
    q, k, v = jnp.split(qkv, 3, axis=-1)

    def heads(t):
        return t.reshape(bsz, seq, DN_HEADS, DN_HEAD_DIM).transpose(0, 2, 1, 3).astype(jnp.float32)

    q, k, v = heads(q), heads(k), heads(v)
    q = _l2norm(q) * (DN_HEAD_DIM ** -0.5)
    k = _l2norm(k)
    beta = jnp.swapaxes(jax.nn.sigmoid(b.astype(jnp.float32)), 1, 2)
    g = -jnp.exp(a_log.astype(jnp.float32)) * jax.nn.softplus(a.astype(jnp.float32) + dt_bias.astype(jnp.float32))
    g = jnp.swapaxes(g, 1, 2)
    o = jnp.swapaxes(_chunked_gated_delta_rule(q, k, v, g, beta), 1, 2)
    zf = z.reshape(bsz, seq, DN_HEADS, DN_HEAD_DIM).astype(jnp.float32)
    o = _rms_norm(o, out_norm.astype(jnp.float32)) * jax.nn.silu(zf)
    return o.reshape(bsz, seq, DN_WIDTH).astype(out_dtype)

def _t5_bucket(dist):
    max_exact = N_BUCKETS // 2
    d = jnp.maximum(dist, 1).astype(jnp.float32)
    log_bucket = max_exact + (jnp.log(d / max_exact) / math.log(MAX_DISTANCE / max_exact)
                              * (N_BUCKETS - max_exact)).astype(jnp.int32)
    return jnp.where(dist < max_exact, dist, jnp.minimum(log_bucket, N_BUCKETS - 1))

def _dilated_band_attention(q, k, v, rel_bias, window, dilation):
    bsz, seq, heads, hd = q.shape
    n_back = window // dilation
    length = seq // dilation
    padded = -(-length // AT_BLOCK) * AT_BLOCK
    nb = padded // AT_BLOCK
    bs = bsz * dilation

    def strided(t):
        t = t.reshape(bsz, length, dilation, heads, hd).transpose(0, 2, 1, 3, 4)
        return t.reshape(bs, length, heads, hd)

    qs = jnp.pad(strided(q), ((0, 0), (0, padded - length), (0, 0), (0, 0))).reshape(bs, nb, AT_BLOCK, heads, hd)

    def band(t):
        t = jnp.pad(strided(t), ((0, 0), (AT_BLOCK, padded - length), (0, 0), (0, 0)))
        t = t.reshape(bs, nb + 1, AT_BLOCK, heads, hd)
        return jnp.concatenate([t[:, :-1], t[:, 1:]], axis=2)

    kb, vb = band(k), band(v)
    rel = jnp.arange(AT_BLOCK)[:, None] + AT_BLOCK - jnp.arange(2 * AT_BLOCK)[None, :]
    key_idx = (jnp.arange(nb)[:, None] - 1) * AT_BLOCK + jnp.arange(2 * AT_BLOCK)[None, :]
    valid = ((rel >= 0) & (rel <= n_back))[None] & (key_idx >= 0)[:, None, :]
    bias = rel_bias[_t5_bucket(dilation * jnp.clip(rel, 0, n_back))]
    scores = jnp.einsum('bnqhd,bnkhd->bnhqk', qs, kb) + jnp.transpose(bias, (2, 0, 1))
    scores = jnp.where(valid[None, :, None], scores, NEG_INF)
    m = jnp.max(scores, axis=-1, keepdims=True)
    p = jnp.exp(scores - m)
    s = jnp.sum(p, axis=-1)
    o = jnp.einsum('bnhqk,bnkhd->bnqhd', p, vb) / jnp.swapaxes(s, 2, 3)[..., None]
    lse = jnp.swapaxes(m[..., 0] + jnp.log(s), 2, 3)

    def unstrided(t):
        t = t.reshape(bsz, dilation, padded, *t.shape[3:])[:, :, :length]
        t = jnp.swapaxes(t, 1, 2)
        return t.reshape(bsz, seq, *t.shape[3:])

    return unstrided(o), unstrided(lse)

def _dilated_attention(q, k, v, q_norm, k_norm, rel_bias):
    out_dtype = q.dtype
    bsz, seq, _ = q.shape

    def heads(t):
        return t.reshape(bsz, seq, AT_HEADS, AT_HEAD_DIM)

    q = _rms_norm(heads(q), q_norm).astype(jnp.float32) * (AT_HEAD_DIM ** -0.5)
    k = _rms_norm(heads(k), k_norm).astype(jnp.float32)
    v = heads(v).astype(jnp.float32)
    table = rel_bias.astype(jnp.float32)
    outs, lses = [], []
    for window, dilation in WINDOWS:
        o_g, lse_g = _dilated_band_attention(q, k, v, table, window, dilation)
        outs.append(o_g)
        lses.append(lse_g)
    weights = jax.nn.softmax(jnp.stack(lses), axis=0)
    o = jnp.einsum('gbsh,gbshd->bshd', weights, jnp.stack(outs))
    return o.reshape(bsz, seq, AT_WIDTH).astype(out_dtype)

def _conformer_conv(u, dw, dw_b, ln_g, ln_b):
    a, gate = jnp.split(u, 2, axis=-1)
    y = a * jax.nn.sigmoid(gate)
    y = _causal_depthwise_conv(y, dw) + dw_b
    y = _layer_norm(y, ln_g, ln_b)
    return jax.nn.silu(y)

def _hierarchical_moe(h, rg_w, rg_b, re_w, re_b, w_gate, w_up, w_down):
    bsz, seq, d = h.shape
    xt = h.reshape(-1, d)
    n_tok = xt.shape[0]
    g_logits = (xt @ rg_w).astype(jnp.float32) + rg_b.astype(jnp.float32)
    g_sel = jnp.argmax(g_logits, axis=-1)
    p_group = jnp.take_along_axis(jax.nn.softmax(g_logits, axis=-1), g_sel[:, None], axis=-1)
    e_logits = ((xt @ re_w).astype(jnp.float32) + re_b.astype(jnp.float32)).reshape(n_tok, N_GROUPS, EXPERTS_PER_GROUP)
    e_logits = jnp.take_along_axis(e_logits, g_sel[:, None, None], axis=1)[:, 0]
    top_v, top_i = lax.top_k(e_logits, TOP_K)
    gate = p_group * jax.nn.softmax(top_v, axis=-1)
    expert_id = g_sel[:, None] * EXPERTS_PER_GROUP + top_i

    n_assign = n_tok * TOP_K
    flat_e = expert_id.reshape(-1)
    order = jnp.argsort(flat_e)
    sorted_e = flat_e[order]
    tok = order // TOP_K
    counts = jnp.bincount(flat_e, length=N_EXPERTS)
    padded = (counts + MOE_BLOCK - 1) // MOE_BLOCK * MOE_BLOCK
    pad_end = jnp.cumsum(padded)
    pad_start = pad_end - padded
    start = jnp.cumsum(counts) - counts
    dest = pad_start[sorted_e] + jnp.arange(n_assign) - start[sorted_e]
    n_blocks = n_assign // MOE_BLOCK + N_EXPERTS
    buf = jnp.zeros((n_blocks * MOE_BLOCK, d), xt.dtype).at[dest].set(xt[tok])
    block_expert = jnp.minimum(jnp.searchsorted(pad_end, jnp.arange(n_blocks) * MOE_BLOCK, side='right'), N_EXPERTS - 1)

    def expert_block(args):
        xb, e = args
        hb = jax.nn.silu(xb @ w_gate[e]) * (xb @ w_up[e])
        return hb @ w_down[e]

    yb = lax.map(expert_block, (buf.reshape(n_blocks, MOE_BLOCK, d), block_expert))
    y_sorted = yb.reshape(-1, d)[dest] * gate.reshape(-1)[order][:, None].astype(xt.dtype)
    out = jnp.zeros((n_tok, d), xt.dtype).at[tok].add(y_sorted)
    return out.reshape(bsz, seq, d)

def setup_inputs(seed: int = 0) -> dict:
    key = jax.random.key(seed)
    ks = jax.random.split(key, 24)
    L = DEPTH

    def nrm(k, shape, scale):
        return jax.random.normal(k, shape, jnp.float32) * scale

    dt = jnp.exp(jax.random.uniform(ks[5], (L, DN_HEADS), minval=math.log(1e-3), maxval=math.log(1e-1)))
    return {
        'x': nrm(ks[0], (BATCH, SEQ, D_MODEL), 1.0),
        'norm_mix': 1.0 + nrm(ks[1], (L, D_MODEL), 0.02),
        'w_in': nrm(ks[2], (L, D_MODEL, N_IN), D_MODEL ** -0.5),
        'dn_conv': nrm(ks[3], (L, DN_CONV, 3 * DN_WIDTH), DN_CONV ** -0.5),
        'dn_a_log': jnp.log(jax.random.uniform(ks[4], (L, DN_HEADS), minval=1.0, maxval=16.0)),
        'dn_dt_bias': dt + jnp.log(-jnp.expm1(-dt)),
        'dn_out_norm': 1.0 + nrm(ks[6], (L, DN_HEAD_DIM), 0.02),
        'at_q_norm': 1.0 + nrm(ks[7], (L, AT_HEAD_DIM), 0.02),
        'at_k_norm': 1.0 + nrm(ks[8], (L, AT_HEAD_DIM), 0.02),
        'rel_bias': nrm(ks[9], (N_BUCKETS, AT_HEADS), 0.5),
        'cv_dw': nrm(ks[10], (L, CV_KERNEL, CV_WIDTH), CV_KERNEL ** -0.5),
        'cv_dw_bias': nrm(ks[11], (L, CV_WIDTH), 0.02),
        'cv_ln_g': 1.0 + nrm(ks[12], (L, CV_WIDTH), 0.02),
        'cv_ln_b': nrm(ks[13], (L, CV_WIDTH), 0.02),
        'w_out': nrm(ks[14], (L, MIX_WIDTH, D_MODEL), MIX_WIDTH ** -0.5),
        'norm_ffn': 1.0 + nrm(ks[15], (L, D_MODEL), 0.02),
        'router_group_w': nrm(ks[16], (L, D_MODEL, N_GROUPS), D_MODEL ** -0.5),
        'router_group_b': nrm(ks[17], (L, N_GROUPS), 0.01),
        'router_expert_w': nrm(ks[18], (L, D_MODEL, N_EXPERTS), D_MODEL ** -0.5),
        'router_expert_b': nrm(ks[19], (L, N_EXPERTS), 0.01),
        'ex_gate': nrm(ks[20], (L, N_EXPERTS, D_MODEL, D_EXPERT), D_MODEL ** -0.5),
        'ex_up': nrm(ks[21], (L, N_EXPERTS, D_MODEL, D_EXPERT), D_MODEL ** -0.5),
        'ex_down': nrm(ks[22], (L, N_EXPERTS, D_EXPERT, D_MODEL), D_EXPERT ** -0.5),
    }

def reference(x, norm_mix, w_in, dn_conv, dn_a_log, dn_dt_bias, dn_out_norm, at_q_norm, at_k_norm,
              rel_bias, cv_dw, cv_dw_bias, cv_ln_g, cv_ln_b, w_out, norm_ffn, router_group_w,
              router_group_b, router_expert_w, router_expert_b, ex_gate, ex_up, ex_down):
    splits = [DN_WIDTH] * 4 + [DN_HEADS] * 2 + [AT_WIDTH] * 3 + [2 * CV_WIDTH]
    offsets = [int(o) for o in np.cumsum(splits)[:-1]]
    for layer in range(DEPTH):
        h = _rms_norm(x, norm_mix[layer])
        proj = h @ w_in[layer]
        dq, dk, dv, dz, da, db, aq, ak, av, cu = jnp.split(proj, offsets, axis=-1)
        y_dn = _gated_deltanet(dq, dk, dv, dz, da, db, dn_conv[layer], dn_a_log[layer],
                               dn_dt_bias[layer], dn_out_norm[layer])
        y_at = _dilated_attention(aq, ak, av, at_q_norm[layer], at_k_norm[layer], rel_bias)
        y_cv = _conformer_conv(cu, cv_dw[layer], cv_dw_bias[layer], cv_ln_g[layer], cv_ln_b[layer])
        mixed = jnp.concatenate([y_dn, y_at, y_cv], axis=-1).astype(x.dtype)
        x = x + mixed @ w_out[layer]
        h = _rms_norm(x, norm_ffn[layer])
        x = x + _hierarchical_moe(h, router_group_w[layer], router_group_b[layer], router_expert_w[layer],
                                  router_expert_b[layer], ex_gate[layer], ex_up[layer], ex_down[layer])
    return x


_drawn_inputs = setup_inputs


def setup_inputs(seed=0):
    import zlib

    import numpy as np

    out = dict(_drawn_inputs(seed))
    spreads = {}
    factors = {'dn_out_norm': 12.251,
     'at_q_norm': 8.0,
     'at_k_norm': 6.009,
     'cv_ln_g': 11.572,
     'cv_ln_b': 4.465,
     'router_group_b': 17.519,
     'router_expert_b': 12.344,
     'norm_ffn': 3.178}
    for name, (base, spread) in spreads.items():
        noise = np.random.default_rng([zlib.crc32(name.encode()), seed]).standard_normal(out[name].shape)
        drawn = base * np.exp(spread * noise) if base else spread * noise
        out[name] = jnp.asarray(drawn.astype(out[name].dtype))
    for name, factor in factors.items():
        out[name] = (out[name] * factor).astype(out[name].dtype)
    return out
```

```python
import math
from contextlib import ExitStack

import numpy as np
import concourse.bass as bass
from concourse import mybir

F32 = mybir.dt.float32
U32 = mybir.dt.uint32
ALU = mybir.AluOpType
ACT = mybir.ActivationFunctionType
AX = mybir.AxisListType

P = 128
SEQ = 1024
D = 1024
TILES = SEQ // P
KC = D // P
EPS = 1e-6
NEG = -1e30

DN_HEADS, HD = 4, 64
DN_W = DN_HEADS * HD
DN_TAPS = 4
AT_HEADS = 8
AT_W = AT_HEADS * HD
CV_W = 256
CV_TAPS = 31
N_IN = 4 * DN_W + 2 * DN_HEADS + 3 * AT_W + 2 * CV_W
WINDOWS = ((128, 1), (512, 4), (2048, 16))
N_BUCKETS, MAX_DISTANCE = 32, 2048
GROUPS, PER_GROUP = 4, 8
EXPERTS = GROUPS * PER_GROUP
DE = D // 2
FC = DE // P
NREL = SEQ + P
LEVELS = 7

C_ID, C_TRI, C_ONE, C_NEG, C_LVL = 0, P, 2 * P, 3 * P, 4 * P
C_BD = C_LVL + LEVELS * P
C_IOTA = C_BD + P
C_E = C_IOTA + P
C_J = C_E + EXPERTS
C_TOK = C_J + 8
C_HALF = C_TOK + TILES
C_J128 = C_HALF + 8
C_THR = C_J128 + 8
C_EJ = C_THR + 8
NCONST = C_EJ + 256

RANKS = SEQ // P
SLOTS = EXPERTS + 2 * 8
EXTRA = SLOTS - EXPERTS

P_CVW = 0
P_DNW = P_CVW + 2 * CV_TAPS
P_GMIX = P_DNW + 6 * DN_TAPS
P_CVB = P_GMIX + KC
P_LNG = P_CVB + 2
P_LNB = P_LNG + 2
P_QN = P_LNB + 2
P_KN = P_QN + 1
P_ALOG = P_KN + 1
P_DT = P_ALOG + DN_HEADS
P_ON = P_DT + DN_HEADS
P_RB = P_ON + HD
P_RBIAS = P_RB + 36
NPARAM = P_RBIAS + GROUPS + EXPERTS


def shape_constants():
    j, i = np.arange(P)[:, None], np.arange(P)[None, :]
    cols = [(i == j), (j <= i), np.ones((P, P)), np.where(j <= i, 0.0, NEG)]
    for level in range(LEVELS):
        s = 1 << level
        cols.append((i // (2 * s) == j // (2 * s)) & (i // s % 2 == 1) & (j // s % 2 == 0))
    cols.append(i // HD == j // HD)
    cols.append(np.broadcast_to(i, (P, P)))
    cols.append(np.broadcast_to(np.arange(EXPERTS), (P, EXPERTS)))
    cols.append(np.broadcast_to(np.arange(8), (P, 8)))
    cols.append(np.arange(P)[:, None] + P * np.arange(TILES)[None, :])
    cols.append(np.full((P, 8), -0.5))
    cols.append(np.broadcast_to(P * np.arange(8), (P, 8)))
    cols.append(np.broadcast_to(np.where(np.arange(8), P * np.arange(8), 1e9), (P, 8)))
    cols.append(np.broadcast_to(np.repeat(np.arange(EXPERTS), 8), (P, 256)))
    return np.ascontiguousarray(np.concatenate([np.asarray(c, np.float32) for c in cols], 1))


def distance_constants():
    rel = SEQ - 1 - np.arange(NREL)
    exact = N_BUCKETS // 2
    d = np.maximum(rel, 1).astype(np.float32)
    log_bucket = exact + (np.log(d / np.float32(exact)) / np.float32(math.log(MAX_DISTANCE / exact))
                          * np.float32(N_BUCKETS - exact)).astype(np.int32)
    bucket = np.where(rel < exact, np.maximum(rel, 0), np.minimum(log_bucket, N_BUCKETS - 1))
    reach = sum(((rel >= 0) & (rel <= w) & (rel % r == 0)).astype(np.int32) for w, r in WINDOWS)
    rows = np.zeros((N_BUCKETS + 1, NREL), np.float32)
    rows[bucket, np.arange(NREL)] = 1.0
    rows[N_BUCKETS] = np.where(reach > 0, np.log(np.maximum(reach, 1)), NEG)
    return rows


def projection_steps():
    steps = [(0, "gate", c, n) for c in (0, 1) for n in (0, 1)]
    steps += [(0, "glu", c, n) for c in (0, 1) for n in (0, 1)]
    steps += [(1, "dn", c, n) for c in range(4) for n in (0, 1)]
    steps += [(2, "dn", c, n) for c in (4, 5) for n in (0, 1)]
    steps += [(2, "z", 0, t) for t in range(TILES)]
    steps += [(3, "q", 0, t) for t in range(TILES)]
    steps += [(4, "k", 1, t) for t in range(TILES)]
    steps += [(5, "v", 0, t) for t in range(TILES)]
    return steps


STEPS = projection_steps()
FIRST_QK = 28
O_CU = N_IN - 2 * CV_W
WGROUPS = [(O_CU, 512), (0, 512), (512, 520), (1032, 512), (1544, 512), (2056, 512)]
GW = 520


def mixer_schedule():
    out = []
    n_att = TILES * AT_HEADS
    for n in range(n_att + 8):
        if n < n_att:
            i, h = divmod(n, AT_HEADS)
            out.append(("scores", n))
        k = 3 * (n % 8)
        out.append(("dn", n // 8, k) if n < n_att else ("none",))
        if 1 <= n <= n_att:
            out.append(("turn", n - 1))
        out.append(("dn", n // 8, k + 1) if n < n_att else ("none",))
        if 2 <= n <= n_att + 1:
            out.append(("values", n - 2))
        out.append(("dn", n // 8, k + 2) if n < n_att else ("none",))
        if n % 8 == 4 and n >= 12:
            out.append(("att_out", n // 8 - 1))
    return [e for e in out if e[0] != "none"]


DN_PIECES = (["split", "norm", "gram", "inv1"]
             + [f"{s}{lv}" for lv in range(1, LEVELS) for s in ("x", "y")]
             + ["carry", "fresh", "emit", "out"])


def turn_groups(n):
    blocks = n // AT_HEADS + 1
    return [(g, min(4, blocks - g)) for g in range(0, blocks, 4)]


def build(nc, a, out, debug_stop=None):
    ctx = ExitStack()
    with ctx:
        def sem(name):
            return ctx.enter_context(nc.semaphore(name))

        arena = ctx.enter_context(nc.sbuf_tensor("arena", [P, 53200], F32))
        ps = ctx.enter_context(nc.psum_tensor("ps", [P, 8, 512], F32))

        def cut(at, *dims):
            size = int(np.prod(dims))
            flat = arena[:, at:at + size]
            if len(dims) == 1:
                return flat
            names = "abcd"[:len(dims)]
            return flat.rearrange("p (%s) -> p %s" % (" ".join(names), " ".join(names)),
                                  **{n: d for n, d in zip(names[1:], dims[1:])})

        A, B, C, DV, E, F, G, H, I, J = 0, 8192, 16512, 24704, 28800, 34964, 41108, 43220, 45328, 47376
        hT = cut(A, KC, SEQ)
        wb = cut(B, 2, KC, GW)
        x_all = cut(C, TILES, D)
        qkT = cut(C, 2, 4, SEQ)
        v_tok = cut(DV, TILES, AT_W)
        dpad = cut(E, 6, SEQ + 3)
        dconv = cut(F, 6, SEQ)
        zg = cut(G, TILES, DN_W)
        ab = cut(G + 2048, TILES, 8)
        ypad = cut(H, 2, SEQ + 30)
        yc = cut(I, 2, SEQ)
        mixT_cv = yc
        cst = cut(J, NCONST)
        par = cut(J + NCONST, NPARAM)
        K = J + NCONST + NPARAM
        gate32 = cut(K, 9, 32)
        K += 9 * 32
        small = cut(K, 64)
        K += 64
        junk = cut(K, D)
        stage = cut(K + D, 2, AT_W)
        sqb = cut(K + 2 * D, AT_W)
        assert K + 2 * D + AT_W <= 53200
        tabE = cut(B, 1152)
        bvec = cut(B + 1152, 1152)

        slab = cut(A, AT_HEADS, SEQ)
        prob = cut(B, 2, SEQ)
        probT = cut(B + 2048, 2, SEQ)
        mixT_at = cut(B + 4096, 4, SEQ)
        mixT_dn = cut(H, 2, SEQ)
        tok = cut(E, 3 * DN_W)
        tT = cut(E + 768, 2, 3, P)
        dI = cut(E + 1536, 4, P)
        At = cut(E + 2048, 4, P)
        qkD = cut(E + 2560, 4, P)
        AM = cut(E + 3072, 2, 4, P)
        T = cut(E + 4096, 4, P)
        Tt = cut(E + 4608, 4, P)
        Xs = cut(E + 5120, 4, P)
        Tg = cut(K, 4, P)
        dsq = cut(K + 512, 512)
        kb = cut(K + 1024, DN_W)
        kd = cut(K + 1280, DN_W)
        vb = cut(K + 1536, DN_W)
        R = cut(K + 1792, DN_W)
        vn = cut(K + 2048, DN_W)
        o1 = cut(K + 2304, DN_W)
        tmp = cut(K + 2560, DN_W)
        Sst = cut(K + 2816, 2, P)
        att = cut(E + 5632, AT_W)
        assert K + 3072 <= 53200

        w_out = cut(A, KC, D)
        xs = cut(B, 2, D)
        g_ffn = cut(B + 2048, D)
        router = cut(B + 3072, KC, 36)
        logits = cut(B + 3360, TILES, 36)
        h2s = cut(G, 2, D)
        h2T = cut(K, 2, KC, P)
        junk3 = cut(K + 2048, D)
        r0 = B + 4096
        padded = cut(r0, TILES, 8)
        gtop = cut(r0 + 64, TILES, 8)
        gtop_i = cut(r0 + 128, TILES, 8).bitcast(U32)
        em = cut(r0 + 192, TILES, EXPERTS)
        etop = cut(r0 + 448, TILES, 8)
        etop_i = cut(r0 + 512, TILES, 8).bitcast(U32)
        g_hot = cut(r0 + 576, TILES, 4)
        g_idx = cut(r0 + 608, TILES)
        e_idx = cut(r0 + 616, 2, TILES)
        p_grp = cut(r0 + 632, TILES)
        rk_k = cut(r0 + 640, 2, TILES)
        rmod = cut(r0 + 656, 2, TILES)
        jn = cut(r0 + 672, 2, TILES)
        gexp = cut(r0 + 688, TILES, 4)
        e_diff = cut(r0 + 720, TILES)
        jhot = cut(r0 + 768, 2, TILES, 8)
        hot = cut(r0 + 896, 2, TILES, EXPERTS)
        hots = cut(r0 + 1408, TILES, EXPERTS)
        before = cut(r0 + 1664, TILES, EXPERTS)
        rank = cut(r0 + 1920, TILES, EXPERTS)
        rtmp = cut(r0 + 2176, TILES, EXPERTS)
        e_count = cut(r0 + 2432, EXPERTS)
        r_hot = cut(r0 + 2464, 2, P)
        r_val = cut(r0 + 2720, 2, 256)
        code = cut(r0 + 3232, 256)
        active = cut(r0 + 3488, 256)
        slot_of = cut(r0 + 3744, 256)
        zero256 = cut(H, 256)
        otmp = cut(H + 256, 256)
        slots = cut(H + 512, SLOTS)
        code2 = cut(H + 560, SLOTS)
        tok_f = cut(H + 608, SLOTS)
        dst_f = cut(H + 656, SLOTS)
        tok_of = cut(H + 864, SLOTS + 1).bitcast(U32)
        dst_of = cut(H + 928, SLOTS + 1)
        ov_e_f = cut(H + 800, EXTRA)
        ov_e = cut(H + 816, EXTRA).bitcast(U32)
        n_ov = cut(H + 832, 8).bitcast(U32)
        gates = cut(H + 840, 2, TILES)
        tok_b = cut(H + 856, 2).bitcast(U32)
        dst_b = cut(H + 858, 2)
        dst_t = cut(H + 862, 2)
        dst_i = cut(H + 860, 2).bitcast(U32)
        W = [cut(C, 3 * KC * DE), cut(E, 3 * KC * DE)]
        w_gate = [w[:, 0:KC * DE].rearrange("p (k n) -> p k n", k=KC) for w in W]
        w_up = [w[:, KC * DE:2 * KC * DE].rearrange("p (k n) -> p k n", k=KC) for w in W]
        w_down = [w[:, 2 * KC * DE:].rearrange("p (k n) -> p k n", k=FC) for w in W]
        hg = cut(A, 2, D)
        hgT = cut(A + 2048, 2, KC, P)
        silu_g = cut(A + 4096, DE)
        act_g = cut(A + 4608, DE)
        actT = cut(A + 5120, FC, P)
        ys = cut(A + 5632, 2, D)
        fx = cut(C, 2, D)
        fy = cut(C + 2048, 2, 2, D)
        x2_dram = nc.dram_tensor("x2_rows", [SEQ, D], F32).ap()
        h2_dram = nc.dram_tensor("h2_rows", [SEQ, D], F32).ap()
        y_dram = nc.dram_tensor("expert_rows", [2 * SEQ, D], F32).ap()

        ident = cst[:, C_ID:C_ID + P]
        tri = cst[:, C_TRI:C_TRI + P]
        ones = cst[:, C_ONE:C_ONE + P]
        negm = cst[:, C_NEG:C_NEG + P]
        bd = cst[:, C_BD:C_BD + P]

        def lvl(n):
            return cst[:, C_LVL + n * P:C_LVL + (n + 1) * P]

        half_neg = cst[:, C_HALF:C_HALF + 8]
        g_col, beta, t1, t2, t3, Gc, Gtot, eG, ekd = (gate32[:, n, :] for n in range(9))
        ss = small[:, 0:8]
        rs = small[:, 8:16]
        ss2 = small[:, 16:32].rearrange("p (u h) -> p u h", u=2)
        rs2 = small[:, 32:48].rearrange("p (u h) -> p u h", u=2)
        ea = small[:, 48:52]
        mx = small[:, 52:54]
        nmx = small[:, 54:56]
        Z = small[:, 16:32].rearrange("p (u h) -> p u h", u=2)
        rZ = small[:, 32:40]
        egl = small[:, 0:16].rearrange("p (t c) -> p t c", c=2)
        dss = small[:, 40:48]
        drs = small[:, 56:64]
        egl_all = t3
        negG = t2

        def bc_h(col, n=HD):
            return col.unsqueeze(2).to_broadcast([P, col.shape[1], n])

        def bc_f(mat, n):
            return mat.unsqueeze(1).to_broadcast([P, n, mat.shape[1]])

        def flipped(ap):
            dims = [list(d) for d in ap.ap]
            step, n = dims[-1]
            dims[-1] = [-step, n]
            return bass.AP(tensor=ap.tensor, offset=ap.offset + step * (n - 1), ap=dims)

        bias_dram = nc.dram_tensor("bias_by_distance", [AT_HEADS, NREL], F32).ap()

        consts_in = sem("consts_in")
        params_in = sem("params_in")
        onehot_in = sem("onehot_in")
        x_in = [sem(f"x_in{t}") for t in range(TILES)]
        w_in_sem = [sem(f"w_in{n}") for n in range(2)]
        sumsq_done = sem("sumsq_done")
        meansq_done = sem("meansq_done")
        rms_done = sem("rms_done")
        h_scaled = sem("h_scaled")
        hT_turned = sem("hT_turned")
        hT_done = sem("hT_done")
        table_mm = sem("table_mm")
        table_sb = sem("table_sb")
        bias_out = sem("bias_out")
        slab_in = sem("slab_in")
        pads_zero = sem("pads_zero")
        proj_done = sem("proj_done")
        act_took = sem("act_took")
        dve_took = sem("dve_took")
        tap_done = sem("tap_done")
        cv_mean = sem("cv_mean")
        cv_centred = sem("cv_centred")
        cv_squared = sem("cv_squared")
        cv_var = sem("cv_var")
        cv_varsb = sem("cv_varsb")
        cv_rstd = sem("cv_rstd")
        cv_normed = sem("cv_normed")
        cv_out = sem("cv_out")
        dn_tapped = sem("dn_tapped")
        dn_silu = sem("dn_silu")
        qk_sq = sem("qk_sq")
        qk_ss = sem("qk_ss")
        qk_rs = sem("qk_rs")
        qk_normed = sem("qk_normed")
        qk_turned = sem("qk_turned")
        qk_out = sem("qk_out")
        zg_done = sem("zg_done")
        gate_a = sem("gate_a")
        gate_v = sem("gate_v")
        gate_p = sem("gate_p")
        s_scores = sem("s_scores")
        s_max = sem("s_max")
        s_exp = sem("s_exp")
        s_turn = sem("s_turn")
        s_turned_a = sem("s_turned_a")
        s_turned_v = sem("s_turned_v")
        s_values = sem("s_values")
        s_att = sem("s_att")
        s_attT = sem("s_attT")
        s_attT_out = sem("s_attT_out")
        d_pe = sem("d_pe")
        d_act = sem("d_act")
        d_dve = sem("d_dve")
        d_pool = sem("d_pool")

        w_out_in = sem("w_out_in")
        ffn_in = sem("ffn_in")
        xs_in = [sem(f"xs_in{n}") for n in range(2)]
        out_mm = sem("out_mm")
        x2_done = sem("x2_done")
        x2_sq = sem("x2_sq")
        x2_ms = sem("x2_ms")
        x2_rs = sem("x2_rs")
        h2_done = sem("h2_done")
        x2_out = [sem(f"x2_out{n}") for n in range(2)]
        h2_out = [sem(f"h2_out{n}") for n in range(2)]
        h2_turned = sem("h2_turned")
        h2T_done = sem("h2T_done")
        logit_mm = sem("logit_mm")
        logit_sb = sem("logit_sb")
        route_v = sem("route_v")
        route_a = sem("route_a")
        rank_mm = sem("rank_mm")
        list_v = sem("list_v")
        list_mm = sem("list_mm")
        slots_ready = sem("slots_ready")
        gu_in = [sem(f"gu_in{n}") for n in range(2)]
        down_in = [sem(f"down_in{n}") for n in range(2)]
        rows_in = [sem(f"rows_in{n}") for n in range(2)]
        idx_copied = sem("idx_copied")
        rows_turned = sem("rows_turned")
        rowsT_a = sem("rowsT_a")
        rowsT_v = sem("rowsT_v")
        gu_mm = sem("gu_mm")
        silu_done = sem("silu_done")
        act_done = sem("act_done")
        act_turned = sem("act_turned")
        actT_done = sem("actT_done")
        down_mm = sem("down_mm")
        y_a = sem("y_a")
        y_v = sem("y_v")
        y_out = [sem(f"y_out{n}") for n in range(2)]
        final_in = [sem(f"final_in{n}") for n in range(2)]
        y_all_out = sem("y_all_out")
        final_v = sem("final_v")
        final_out = [sem(f"final_out{n}") for n in range(2)]

        def at_least(eng, s, value):
            if not isinstance(value, int) or value > 0:
                eng.wait_ge(s, value)

        def for_blocks(eng, body, count=None):
            for u in range(2):
                body(u, u, 0)
            with eng.Fori(1, EXPERTS // 2) as pair:
                for u in range(2):
                    body(2 * pair + u, u, pair)
            more = eng.value_load(n_ov[0:1, 0:1], min_val=0, max_val=EXTRA)
            with eng.Fori(EXPERTS // 2, SLOTS // 2) as pair:
                for u in range(2):
                    slot = 2 * pair + u
                    with eng.If(more + EXPERTS > slot):
                        body(slot, u, pair)

        def act_taken(step):
            glu = [n for n, s in enumerate(STEPS[:step + 1]) if s[1] == "glu"]
            return (dve_took, len(glu)) if STEPS[step][1] == "glu" else (act_took, step + 1 - len(glu))

        group_end = {g: max(n for n, s in enumerate(STEPS) if s[0] == g) + 1 for g in range(6)}

        PE_MARKS = ["split", "gb", "norm", "gram", "inv1"] + DN_PIECES[4:16] + ["carry", "fresh", "emit", "out"]
        ACT_MARKS = ["split", "decay", "norm"] + [f"x{lv}" for lv in range(1, LEVELS)] + ["fresh", "out"]
        DVE_MARKS = ["ss", "qkn", "gram", "inv1"] + [f"y{lv}" for lv in range(1, LEVELS)] + ["carry", "emit", "oss", "onorm"]
        POOL_MARKS = ["tg", "sq", "rs", "kb", "kdvb"] + [f"am{lv}" for lv in range(LEVELS)] + ["osq", "ors"]

        def pe_at(i, mark):
            return i * len(PE_MARKS) + PE_MARKS.index(mark) + 1

        def act_at(i, mark):
            return i * len(ACT_MARKS) + ACT_MARKS.index(mark) + 1

        def dve_at(i, mark):
            return i * len(DVE_MARKS) + DVE_MARKS.index(mark) + 1

        def pool_at(i, mark):
            return i * len(POOL_MARKS) + POOL_MARKS.index(mark) + 1

        turn_total = [0]
        for n in range(TILES * AT_HEADS):
            turn_total.append(turn_total[-1] + len(turn_groups(n)))
        TURNS = []
        for ev in mixer_schedule():
            if ev[0] == "turn":
                TURNS += [("p", ev[1], g, c) for g, c in turn_groups(ev[1])]
            elif ev[0] == "att_out":
                TURNS.append(("o", ev[1], 0, 4))
        TAKER = ["v" if (n % 2) else "a" for n in range(len(TURNS))]

        def taken(idx):
            who = TAKER[idx]
            return (s_turned_a if who == "a" else s_turned_v), TAKER[:idx + 1].count(who)

        first_turn = {}
        last_turn = {}
        for n, (kind, m, g, c) in enumerate(TURNS):
            first_turn.setdefault((kind, m), n)
            last_turn[(kind, m)] = n

        block = ctx.enter_context(nc.Block())

        def last_rows(eng):
            eng.wait_ge(y_all_out, 1)

        def store(eng, t):
            eng.wait_ge(final_v, t + 1)
            eng.dma_start(out[t * P:(t + 1) * P, :], fx[:, t % 2, :]).then_inc(final_out[t % 2], 16)

        @block.sync
        def _(sp):
            sp.dma_start(cst, a["constants"]).then_inc(consts_in, 16)
            for t in range(TILES):
                sp.dma_start(x_all[:, t, :], a["x"][t * P:(t + 1) * P, :]).then_inc(x_in[t], 16)
            sp.dma_start(tabE[0:N_BUCKETS + 1, :], a["distances"]).then_inc(onehot_in, 16)
            for g, (c0, width) in enumerate(WGROUPS):
                if g == 0:
                    sp.wait_ge(bias_out, 16)
                if g >= 2:
                    sp.wait_ge(proj_done, group_end[g - 2])
                sp.dma_start(wb[:, g % 2, :, 0:width],
                             a["w_in"][:, c0:c0 + width].rearrange("(k p) n -> p k n", p=P)).then_inc(w_in_sem[g % 2], 16)
            sp.wait_ge(proj_done, len(STEPS))
            sp.wait_ge(bias_out, 16)
            src = bass.AP(tensor=bias_dram.tensor, offset=0, ap=[[1, P], [NREL, AT_HEADS], [1, SEQ]])
            sp.dma_start(slab, src).then_inc(slab_in, 16)

            n_att = TILES * AT_HEADS
            sp.wait_ge(s_max, n_att)
            sp.dma_start(w_out, a["w_out"].rearrange("(k p) n -> p k n", p=P)).then_inc(w_out_in, 16)
            sp.wait_ge(s_values, n_att)
            sp.wait_ge(s_turned_a, TAKER.count("a"))
            sp.wait_ge(s_turned_v, TAKER.count("v"))
            sp.dma_start(g_ffn, a["norm_ffn"]).then_inc(ffn_in, 16)
            sp.dma_start(router, a["router"].rearrange("(k p) n -> p k n", p=P)).then_inc(ffn_in, 16)
            for t in range(2):
                sp.dma_start(xs[:, t, :], a["x"][t * P:(t + 1) * P, :]).then_inc(xs_in[t], 16)
            sp.wait_ge(d_dve, TILES * len(DVE_MARKS))
            sp.wait_ge(d_pe, TILES * len(PE_MARKS))

            def load_weights(slot, u, expert):
                at_least(sp, gu_mm, slot - 1)
                for w, name in ((w_gate, "ex_gate"), (w_up, "ex_up")):
                    sp.dma_start(w[u], a[name][bass.ds(expert, 1), :, :].rearrange("e (k p) n -> p (e k) n", p=P))\
                      .then_inc(gu_in[u], 16)
                at_least(sp, down_mm, slot - 1)
                sp.dma_start(w_down[u], a["ex_down"][bass.ds(expert, 1), :, :].rearrange("e (k p) n -> p (e k) n", p=P))\
                  .then_inc(down_in[u], 16)

            for u in range(2):
                load_weights(u, u, u)
            for t in range(TILES):
                sp.wait_ge(x2_done, t + 1)
                sp.dma_start(x2_dram[t * P:(t + 1) * P, :], xs[:, t % 2, :]).then_inc(x2_out[t % 2], 16)
                sp.wait_ge(h2_done, t + 1)
                sp.dma_start(h2_dram[t * P:(t + 1) * P, :], h2s[:, t % 2, :]).then_inc(h2_out[t % 2], 16)
                if t + 2 < TILES:
                    sp.wait_ge(x2_out[t % 2], 16 * (t // 2 + 1))
                    sp.wait_ge(x2_sq, t + 1)
                    sp.dma_start(xs[:, t % 2, :], a["x"][(t + 2) * P:(t + 3) * P, :]).then_inc(xs_in[t % 2], 16)
            with sp.Fori(1, EXPERTS // 2) as pair:
                for u in range(2):
                    load_weights(2 * pair + u, u, 2 * pair + u)
            sp.wait_ge(slots_ready, 1)
            more = sp.value_load(n_ov[0:1, 0:1], min_val=0, max_val=EXTRA)
            with sp.Fori(0, EXTRA // 2) as pair:
                for u in range(2):
                    with sp.If(more > 2 * pair + u):
                        expert = sp.value_load(ov_e[0:1, bass.ds(2 * pair + u, 1)], min_val=0, max_val=EXPERTS - 1)
                        load_weights(2 * pair + EXPERTS + u, u, expert)
            last_rows(sp)
            for t in range(TILES):
                if t >= 2:
                    sp.wait_ge(final_out[t % 2], 16 * (t // 2))
                rows = slice(t * P, (t + 1) * P)
                sp.dma_start(fx[:, t % 2, :], x2_dram[rows, :]).then_inc(final_in[t % 2], 16)
                for c in range(2):
                    sp.dma_start(fy[:, t % 2, c, :], y_dram[c * SEQ + t * P:c * SEQ + (t + 1) * P, :]).then_inc(final_in[t % 2], 16)
                if t >= 1:
                    store(sp, t - 1)
            store(sp, TILES - 1)
            for u in range(2):
                sp.wait_ge(final_out[u], 16 * TILES // 2)

        @block.tensor
        def _(pe):
            mm, tr = nc.tensor.matmul, nc.tensor.transpose
            pe.wait_ge(consts_in, 16)
            pe.wait_ge(params_in, 16)
            pe.wait_ge(onehot_in, 16)
            for c in range(3):
                last = mm(ps[0:AT_HEADS, 5 + c, 0:384], par[0:N_BUCKETS + 1, P_RB:P_RB + AT_HEADS],
                          tabE[0:N_BUCKETS + 1, c * 384:(c + 1) * 384], start=True, stop=True)
            last.then_inc(table_mm, 1)
            for t in range(TILES):
                pe.wait_ge(h_scaled, t + 1)
                if t >= 2:
                    pe.wait_ge(hT_done, 2 * (t - 1))
                for half in range(2):
                    for c in range(4):
                        k = 4 * half + c
                        last = tr(ps[:, 2 * (t % 2) + half, c * P:(c + 1) * P], x_all[:, t, k * P:(k + 1) * P], ident)
                    last.then_inc(hT_turned, 1)
            pe.wait_ge(hT_done, 2 * TILES)

            def turn_qk(j):
                pe.wait_ge(qk_normed, j + 1)
                if j >= 2:
                    pe.wait_ge(qk_out, j - 1)
                for c in range(4):
                    last = tr(ps[:, 4 + j % 2, c * P:(c + 1) * P], stage[:, j % 2, c * P:(c + 1) * P], ident)
                last.then_inc(qk_turned, 1)

            group = -1
            for n, (g, kind, c, m) in enumerate(STEPS):
                if g != group:
                    group = g
                    pe.wait_ge(w_in_sem[g % 2], 16 * (g // 2 + 1))
                if n >= 4:
                    pe.wait_ge(*act_taken(n - 4))
                bank = n % 4
                w = wb[:, g % 2]
                for k in range(KC):
                    f = dict(start=(k == 0), stop=(k == KC - 1))
                    if kind in ("gate", "glu", "dn"):
                        col = {"gate": 2 + c, "glu": c, "dn": c % 4}[kind] * P
                        last = mm(ps[:, bank, :], w[:, k, col:col + P], hT[:, k, m * 512:(m + 1) * 512], **f)
                    elif kind == "z":
                        last = mm(ps[:, bank, 0:264], hT[:, k, m * P:(m + 1) * P], w[:, k, 256:520], **f)
                    else:
                        last = mm(ps[:, bank, :], hT[:, k, m * P:(m + 1) * P], w[:, k, 0:512], **f)
                last.then_inc(proj_done, 1)
                if n == 19:
                    pe.wait_ge(tap_done, 2 * CV_TAPS)
                    for half in range(2):
                        for c2 in range(2):
                            last = mm(ps[:, 6 + half, :], ones, yc[:, c2, half * 512:(half + 1) * 512],
                                      start=(c2 == 0), stop=(c2 == 1))
                    last.then_inc(cv_mean, 1)
                if n == 22:
                    pe.wait_ge(cv_squared, 2)
                    for half in range(2):
                        for c2 in range(2):
                            last = mm(ps[:, 6 + half, :], ones, ypad[:, c2, half * 512:(half + 1) * 512],
                                      start=(c2 == 0), stop=(c2 == 1))
                    last.then_inc(cv_var, 1)
                if n > FIRST_QK and n - FIRST_QK - 1 < 16:
                    turn_qk(n - FIRST_QK - 1)
            pe.wait_ge(gate_v, 4)
            pe.wait_ge(cv_varsb, 1)
            mm(ps[:, 6, 0:32], tri, g_col, start=True, stop=True)
            mm(ps[:, 6, 32:64], ones, g_col, start=True, stop=True).then_inc(cv_mean, 1)

            D0, D1, D2, PV, TB = 0, 1, 2, 3, 4

            def dn(i, k):
                if k >= len(DN_PIECES):
                    return
                piece = DN_PIECES[k]
                if piece == "split":
                    if i == 0:
                        pe.wait_ge(dn_silu, 6)
                        pe.wait_ge(act_took, len(STEPS) - 4)
                        pe.wait_ge(gate_a, 5)
                    else:
                        pe.wait_ge(d_dve, dve_at(i - 1, "onorm"))
                    for c in range(6):
                        last = tr(ps[:, c // 4, (c % 4) * P:(c % 4 + 1) * P], dconv[:, c, i * P:(i + 1) * P], ident)
                    last.then_inc(d_pe, 1)
                    pe.wait_ge(d_pool, pool_at(i, "tg"))
                    if i:
                        pe.wait_ge(d_act, act_at(i - 1, "out"))
                    mm(ps[:, D2, :], ones, Tg.rearrange("p h n -> p (h n)"), start=True, stop=False)
                    for h in range(4):
                        last = mm(ps[:, D2, h * P:(h + 1) * P], ident, negm, start=False, stop=(h == 3))
                    last.then_inc(d_pe, 1)
                elif piece == "norm":
                    pe.wait_ge(d_dve, dve_at(i, "qkn"))
                    pe.wait_ge(d_pool, pool_at(i, "kb"))
                    for pair in range(2):
                        cols = slice(pair * P, (pair + 1) * P)
                        for m, src in enumerate((kb[:, cols], tok[:, cols], tok[:, DN_W + pair * P:DN_W + (pair + 1) * P])):
                            last = tr(ps[:, pair, m * P:(m + 1) * P], src, ident)
                    last.then_inc(d_pe, 1)
                elif piece == "gram":
                    pe.wait_ge(d_act, act_at(i, "norm"))
                    for h in range(4):
                        rows = slice(HD * (h % 2), HD * (h % 2) + HD)
                        last = mm(ps[:, h % 2, (h // 2) * 256:(h // 2) * 256 + 256], tT[rows, h // 2, 2, :],
                                  tT[rows, h // 2, 0:2, :], start=True, stop=True)
                    last.then_inc(d_pe, 1)
                elif piece == "inv1":
                    pe.wait_ge(d_pool, pool_at(i, "am0"))
                    pe.wait_ge(d_act, act_at(i, "decay"))
                    for h in range(4):
                        last = tr(ps[:, D2, h * P:(h + 1) * P], AM[:, 0, h, :], ident)
                    last.then_inc(d_pe, 1)
                elif piece[0] == "x":
                    lv = int(piece[1:])
                    pe.wait_ge(d_pool, pool_at(i, f"am{lv}"))
                    pe.wait_ge(d_dve, dve_at(i, f"y{lv - 1}" if lv > 1 else "inv1"))
                    for h in range(4):
                        last = mm(ps[:, D2, h * P:(h + 1) * P], AM[:, lv % 2, h, :], T[:, h, :], start=True, stop=True)
                    last.then_inc(d_pe, 1)
                elif piece[0] == "y":
                    lv = int(piece[1:])
                    pe.wait_ge(d_act, act_at(i, f"x{lv}"))
                    for h in range(4):
                        if lv < LEVELS - 1:
                            mm(ps[:, D0, h * P:(h + 1) * P], Tt[:, h, :], Xs[:, h, :], start=True, stop=True)
                    for h in range(4):
                        last = mm(ps[:, D1, h * P:(h + 1) * P], Xs[:, h, :], Tt[:, h, :], start=True, stop=True)
                    last.then_inc(d_pe, 1)
                elif piece == "carry":
                    if i:
                        pe.wait_ge(d_dve, dve_at(i - 1, "emit"))
                    else:
                        pe.wait_ge(pads_zero, 2)
                    for m in range(2):
                        for pair in range(2):
                            last = mm(ps[:, D2, m * 256 + pair * P:m * 256 + (pair + 1) * P], tT[:, pair, m, :],
                                      Sst[:, pair, :], start=True, stop=True)
                    last.then_inc(d_pe, 1)
                elif piece == "fresh":
                    pe.wait_ge(d_dve, dve_at(i, "carry"))
                    for h in range(4):
                        last = mm(ps[:, D0, h * HD:(h + 1) * HD], Tt[:, h, :], R[:, h * HD:(h + 1) * HD],
                                  start=True, stop=True)
                    last.then_inc(d_pe, 1)
                elif piece == "emit":
                    pe.wait_ge(d_act, act_at(i, "fresh"))
                    pe.wait_ge(d_pool, pool_at(i, "kdvb"))
                    for h in range(4):
                        mm(ps[:, D1, h * HD:(h + 1) * HD], qkD[:, h, :], vn[:, h * HD:(h + 1) * HD], start=True, stop=True)
                    for pair in range(2):
                        cols = slice(pair * P, (pair + 1) * P)
                        last = mm(ps[:, D0, pair * P:(pair + 1) * P], kd[:, cols], vn[:, cols], start=True, stop=True)
                    last.then_inc(d_pe, 1)
                elif piece == "out":
                    pe.wait_ge(d_dve, dve_at(i, "onorm"))
                    for pair in range(2):
                        last = tr(ps[:, D2, pair * P:(pair + 1) * P], o1[:, pair * P:(pair + 1) * P], ident)
                    last.then_inc(d_pe, 1)

            pe.wait_ge(qk_out, 16)
            pe.wait_ge(act_took, len(STEPS) - 4)
            pe.wait_ge(slab_in, 16)
            pe.wait_ge(gate_a, 5)
            idx = 0
            for ev in mixer_schedule():
                if ev[0] == "scores":
                    n = ev[1]
                    i, h = divmod(n, AT_HEADS)
                    rows = slice(HD * (h % 2), HD * (h % 2) + HD)
                    pe.wait_ge(s_max, n)
                    for c0 in range(0, (i + 1) * P, 512):
                        w = min(512, (i + 1) * P - c0)
                        last = mm(ps[:, 6 + c0 // 512, 0:w], qkT[rows, 0, h // 2, i * P:(i + 1) * P],
                                  qkT[rows, 1, h // 2, c0:c0 + w], start=True, stop=True)
                    last.then_inc(s_scores, 1)
                elif ev[0] == "dn":
                    dn(ev[1], ev[2])
                elif ev[0] == "turn":
                    n = ev[1]
                    pe.wait_ge(s_exp, n + 1)
                    for g, cnt in turn_groups(n):
                        if idx >= 2:
                            pe.wait_ge(*taken(idx - 2))
                        for c in range(cnt):
                            last = tr(ps[:, TB + idx % 2, c * P:(c + 1) * P], prob[:, n % 2, (g + c) * P:(g + c + 1) * P], ident)
                        last.then_inc(s_turn, 1)
                        idx += 1
                elif ev[0] == "values":
                    n = ev[1]
                    i, h = divmod(n, AT_HEADS)
                    if h == 0:
                        pe.wait_ge(s_att, i)
                    for who in range(first_turn[("p", n)], last_turn[("p", n)] + 1):
                        pe.wait_ge(*taken(who))
                    for b in range(i + 1):
                        last = mm(ps[:, PV, h * HD:(h + 1) * HD], probT[:, n % 2, b * P:(b + 1) * P],
                                  v_tok[:, b, h * HD:(h + 1) * HD], start=(b == 0), stop=(b == i))
                    last.then_inc(s_values, 1)
                else:
                    i = ev[1]
                    pe.wait_ge(s_att, i + 1)
                    pe.wait_ge(*taken(idx - 2))
                    for c in range(4):
                        last = tr(ps[:, TB + idx % 2, c * P:(c + 1) * P], att[:, c * P:(c + 1) * P], ident)
                    last.then_inc(s_turn, 1)
                    idx += 1

            pe.wait_ge(w_out_in, 16)
            pe.wait_ge(ffn_in, 32)
            pe.wait_ge(d_act, TILES * len(ACT_MARKS))
            pe.wait_ge(cv_out, 2)

            def logits_of(t):
                pe.wait_ge(h2_done, t + 1)
                if t:
                    pe.wait_ge(h2T_done, t)
                for k in range(KC):
                    last = tr(ps[:, 4 + k // 4, (k % 4) * P:(k % 4 + 1) * P], h2s[:, t % 2, k * P:(k + 1) * P], ident)
                last.then_inc(h2_turned, 1)
                pe.wait_ge(h2T_done, t + 1)
                if t:
                    pe.wait_ge(logit_sb, t)
                for k in range(KC):
                    last = mm(ps[:, 6, 0:36], h2T[:, t % 2, k, :], router[:, k, :], start=(k == 0), stop=(k == KC - 1))
                last.then_inc(logit_mm, 1)

            mixT = [mixT_dn[:, 0], mixT_dn[:, 1]] + [mixT_at[:, c] for c in range(4)] + [mixT_cv[:, 0], mixT_cv[:, 1]]
            for t in range(TILES):
                if t >= 2:
                    pe.wait_ge(x2_done, t - 1)
                for half in range(2):
                    for k in range(KC):
                        last = mm(ps[:, 2 * (t % 2) + half, :], mixT[k][:, t * P:(t + 1) * P],
                                  w_out[:, k, half * 512:(half + 1) * 512], start=(k == 0), stop=(k == KC - 1))
                last.then_inc(out_mm, 1)
                if t:
                    logits_of(t - 1)
            logits_of(TILES - 1)
            pe.wait_ge(route_v, 3)
            flat = lambda x: x.rearrange("p t e -> p (t e)")
            mm(ps[:, 7, 0:256], tri, flat(hots), start=True, stop=False)
            mm(ps[:, 7, 0:256], ones, flat(before), start=False, stop=True)
            mm(ps[:, 7, 256:288], ones, hots[:, TILES - 1, :], start=True, stop=False)
            mm(ps[:, 7, 256:288], ones, before[:, TILES - 1, :], start=False, stop=True).then_inc(rank_mm, 1)
            for m in range(2 * TILES):
                pe.wait_ge(list_v, m + 1)
                mm(ps[:, 6, 0:256], r_hot[:, m % 2, :], r_val[:, m % 2, :], start=(m == 0), stop=(m == 2 * TILES - 1))\
                    .then_inc(list_mm, 1)

            def turn_rows(slot, u, pair):
                pe.wait_ge(rows_in[u], 16 * (pair + 1))
                for k in range(KC):
                    last = tr(ps[:, k // 4, (k % 4) * P:(k % 4 + 1) * P], hg[:, u, k * P:(k + 1) * P], ident)
                last.then_inc(rows_turned, 1)

            def expert(slot, u, pair):
                pe.wait_ge(rowsT_a, slot + 1)
                pe.wait_ge(rowsT_v, slot + 1)
                pe.wait_ge(gu_in[u], 32 * (pair + 1))
                at_least(pe, act_done, slot)
                for k in range(KC):
                    mm(ps[:, 2, :], hgT[:, u, k, :], w_gate[u][:, k, :], start=(k == 0), stop=(k == KC - 1))
                for k in range(KC):
                    last = mm(ps[:, 3, :], hgT[:, u, k, :], w_up[u][:, k, :], start=(k == 0), stop=(k == KC - 1))
                last.then_inc(gu_mm, 1)
                turn_rows(slot + 1, 1 - u, pair + u)
                pe.wait_ge(act_done, slot + 1)
                at_least(pe, actT_done, slot)
                for k in range(FC):
                    last = tr(ps[:, 4, k * P:(k + 1) * P], act_g[:, k * P:(k + 1) * P], ident)
                last.then_inc(act_turned, 1)
                pe.wait_ge(actT_done, slot + 1)
                pe.wait_ge(down_in[u], 16 * (pair + 1))
                at_least(pe, y_a, slot)
                at_least(pe, y_v, slot)
                for half in range(2):
                    for k in range(FC):
                        last = mm(ps[:, 5 + half, :], actT[:, k, :], w_down[u][:, k, half * 512:(half + 1) * 512],
                                  start=(k == 0), stop=(k == FC - 1))
                last.then_inc(down_mm, 1)

            pe.wait_ge(slots_ready, 1)
            turn_rows(0, 0, 0)
            for_blocks(pe, expert)

        @block.vector
        def _(v):
            tt, ts, stt = nc.vector.tensor_tensor, nc.vector.tensor_scalar, nc.vector.scalar_tensor_tensor
            nc.vector.memset(ypad[:, :, 0:30], 0.0)
            nc.vector.memset(dpad[:, :, 0:3], 0.0).then_inc(pads_zero, 1)

            def take_hT(t):
                for half in range(2):
                    v.wait_ge(hT_turned, 2 * t + half + 1)
                    k0 = 4 * half
                    tt(hT[:, k0:k0 + 4, t * P:(t + 1) * P], ps[:, 2 * (t % 2) + half, :].rearrange("p (k n) -> p k n", k=4),
                       bc_h(par[:, P_GMIX + k0:P_GMIX + k0 + 4], P), ALU.mult).then_inc(hT_done, 1)

            v.wait_ge(params_in, 16)
            v.wait_ge(consts_in, 16)
            for t in range(TILES):
                v.wait_ge(rms_done, t + 1)
                ts(x_all[:, t, :], x_all[:, t, :], rs[:, t:t + 1], None, ALU.mult).then_inc(h_scaled, 1)
                if t:
                    take_hT(t - 1)
            take_hT(TILES - 1)

            for n, (g, kind, c, m) in enumerate(STEPS):
                if kind == "glu":
                    v.wait_ge(proj_done, n + 1)
                    v.wait_ge(act_took, 4)
                    tt(ypad[:, c, 30 + m * 512:30 + (m + 1) * 512], ps[:, n % 4, :], yc[:, c, m * 512:(m + 1) * 512],
                       ALU.mult).then_inc(dve_took, 1)
            v.wait_ge(dve_took, 4)
            for c in range(2):
                ts(yc[:, c, :], ypad[:, c, 0:SEQ], par[:, P_CVW + c * CV_TAPS:P_CVW + c * CV_TAPS + 1],
                   par[:, P_CVB + c:P_CVB + c + 1], ALU.mult, ALU.add).then_inc(tap_done, 1)
            for tap in range(1, CV_TAPS):
                for c in range(2):
                    v.wait_ge(tap_done, 2 * tap + c - 1)
                    col = P_CVW + c * CV_TAPS + tap
                    stt(yc[:, c, :], ypad[:, c, tap:tap + SEQ], par[:, col:col + 1], yc[:, c, :],
                        ALU.mult, ALU.add).then_inc(tap_done, 1)
            v.wait_ge(cv_mean, 1)
            for half in range(2):
                for c in range(2):
                    seg = yc[:, c, half * 512:(half + 1) * 512]
                    last = stt(seg, ps[:, 6 + half, :], -1.0 / CV_W, seg, ALU.mult, ALU.add)
            last.then_inc(cv_centred, 1)

            def dn_conv(c):
                v.wait_ge(*act_taken(8 + 2 * c + 1))
                w0 = P_DNW + c * DN_TAPS
                ts(dconv[:, c, :], dpad[:, c, 0:SEQ], par[:, w0:w0 + 1], None, ALU.mult)
                for tap in range(1, DN_TAPS):
                    nc.vector.drain()
                    last = stt(dconv[:, c, :], dpad[:, c, tap:tap + SEQ], par[:, w0 + tap:w0 + tap + 1], dconv[:, c, :],
                               ALU.mult, ALU.add)
                last.then_inc(dn_tapped, 1)

            dn_conv(0)
            dn_conv(1)
            v.wait_ge(cv_var, 1)
            for half in range(2):
                ts(junk[:, half * 512:(half + 1) * 512], ps[:, 6 + half, :], 1.0 / CV_W, EPS, ALU.mult, ALU.add)
            nc.vector.drain()
            nc.vector.reciprocal(junk, junk).then_inc(cv_varsb, 1)
            for c in range(2, 6):
                dn_conv(c)
            v.wait_ge(cv_rstd, 1)
            tt(yc, yc, bc_f(junk, 2), ALU.mult).then_inc(cv_normed, 1)
            v.wait_ge(act_took, 4 + 8 + 4 + 8)
            tt(zg.rearrange("p t (h d) -> p (t h) d", d=HD), zg.rearrange("p t (h d) -> p (t h) d", d=HD),
               bc_f(par[:, P_ON:P_ON + HD], TILES * DN_HEADS), ALU.mult).then_inc(zg_done, 1)
            for j in range(16):
                v.wait_ge(qk_sq, j + 1)
                nc.vector.tensor_reduce(ss2[:, j % 2, :], sqb.rearrange("p (h d) -> p h d", d=HD), AX.X, ALU.add)
                nc.vector.drain()
                if j < 8:
                    ts(ss2[:, j % 2, :], ss2[:, j % 2, :], HD * EPS, None, ALU.add).then_inc(qk_ss, 1)
                else:
                    ts(ss2[:, j % 2, :], ss2[:, j % 2, :], 1.0 / HD, EPS, ALU.mult, ALU.add).then_inc(qk_ss, 1)
                v.wait_ge(qk_rs, j + 1)
                s3 = stage[:, j % 2, :].rearrange("p (h d) -> p h d", d=HD)
                tt(s3, s3, bc_h(rs2[:, j % 2, :]), ALU.mult).then_inc(qk_normed, 1)
            a8 = ab[:, :, 0:4]
            b8 = ab[:, :, 4:8]
            g3, beta3, t13, t23, t33 = (x.rearrange("p (t h) -> p t h", h=4) for x in (g_col, beta, t1, t2, t3))
            tt(t13, a8, bc_f(par[:, P_DT:P_DT + 4], TILES), ALU.add)
            nc.vector.drain()
            stt(t23, t13, -1.0, t13, ALU.mult, ALU.min)
            v.wait_ge(act_took, 4 + 8 + 4 + 8)
            nc.vector.tensor_copy(t33, b8)
            nc.vector.drain().then_inc(gate_v, 1)
            v.wait_ge(gate_a, 2)
            stt(t13, t13, 0.0, t23, ALU.max, ALU.add)
            ts(t3, t3, 1.0, None, ALU.add)
            nc.vector.drain().then_inc(gate_v, 1)
            nc.vector.reciprocal(beta, t3)
            stt(g3, t13, -1.0, bc_f(ea, TILES), ALU.mult, ALU.mult)
            nc.vector.drain().then_inc(gate_v, 2)
            v.wait_ge(cv_mean, 2)
            nc.vector.tensor_copy(Gc, ps[:, 6, 0:32])
            nc.vector.tensor_copy(Gtot, ps[:, 6, 32:64])
            nc.vector.drain()
            tt(ekd, Gtot, Gc, ALU.subtract)
            ts(negG, Gc, -1.0, None, ALU.mult)
            nc.vector.drain().then_inc(gate_v, 1)
            v.wait_ge(gate_a, 5)
            e3 = egl_all.rearrange("p (t c two) -> p t c two", two=2, c=2)
            nc.vector.tensor_copy(egl[0:HD], e3[0:HD, :, :, 0])
            nc.vector.tensor_copy(egl[HD:P], e3[HD:P, :, :, 1])
            nc.vector.memset(Sst, 0.0)
            nc.vector.drain().then_inc(pads_zero, 1)

            def dn(i, k):
                if k >= len(DN_PIECES):
                    return
                piece = DN_PIECES[k]
                ti = slice(4 * i, 4 * i + 4)
                if piece == "split":
                    v.wait_ge(d_pool, pool_at(i, "sq"))
                    nc.vector.tensor_reduce(dss, dsq.rearrange("p (h d) -> p h d", d=HD), AX.X, ALU.add)
                    nc.vector.drain()
                    ts(dss[:, 4:8], dss[:, 4:8], EPS, None, ALU.add)
                    ts(dss[:, 0:4], dss[:, 0:4], EPS, float(HD), ALU.add, ALU.mult)
                    nc.vector.drain().then_inc(d_dve, 1)
                    v.wait_ge(d_pool, pool_at(i, "rs"))
                    t8 = tok[:, 0:512].rearrange("p (h d) -> p h d", d=HD)
                    tt(t8, t8, bc_h(drs), ALU.mult).then_inc(d_dve, 1)
                elif piece == "gram":
                    v.wait_ge(d_pe, pe_at(i, "gram"))
                    v.wait_ge(d_act, act_at(i, "decay"))
                    both = ps[:, 0:2, :].rearrange("p b (c m n) -> p b c m n", m=2, n=P)
                    of_bank = lambda x: x.rearrange("p (c b) n -> p b c n", b=2)
                    tt(of_bank(At), both[:, :, :, 0, :], of_bank(dI), ALU.mult)
                    tt(of_bank(qkD), both[:, :, :, 1, :], of_bank(dI), ALU.mult)
                    nc.vector.drain().then_inc(d_dve, 1)
                elif piece == "inv1":
                    v.wait_ge(d_pe, pe_at(i, "inv1"))
                    tt(T, bc_f(ident, 4), ps[:, 2, :].rearrange("p (h n) -> p h n", h=4), ALU.subtract)
                    tt(Tt, bc_f(ident, 4), AM[:, 0], ALU.subtract)
                    nc.vector.drain().then_inc(d_dve, 1)
                elif piece[0] == "y":
                    lv = int(piece[1:])
                    v.wait_ge(d_pe, pe_at(i, piece))
                    if lv < LEVELS - 1:
                        tt(T, T, ps[:, 0, :].rearrange("p (h n) -> p h n", h=4), ALU.subtract)
                    tt(Tt, Tt, ps[:, 1, :].rearrange("p (h n) -> p h n", h=4), ALU.subtract)
                    nc.vector.drain().then_inc(d_dve, 1)
                elif piece == "carry":
                    v.wait_ge(d_pe, pe_at(i, "carry"))
                    v.wait_ge(d_pool, pool_at(i, "kdvb"))
                    h4 = lambda x: x.rearrange("p (h d) -> p h d", d=HD)
                    tt(h4(tmp), h4(ps[:, 2, 0:256]), bc_h(eG[:, ti]), ALU.mult)
                    tt(h4(o1), h4(ps[:, 2, 256:512]), bc_h(eG[:, ti]), ALU.mult)
                    nc.vector.drain()
                    tt(R, vb, tmp, ALU.subtract).then_inc(d_dve, 1)
                elif piece == "emit":
                    v.wait_ge(d_pe, pe_at(i, "emit"))
                    tt(tmp.rearrange("p (c n) -> p c n", c=2), ps[:, 0, 0:256].rearrange("p (c n) -> p c n", c=2),
                       bc_f(bd, 2), ALU.mult)
                    tt(o1, ps[:, 1, 0:256], o1, ALU.add)
                    nc.vector.drain()
                    for pair in range(2):
                        stt(Sst[:, pair, :], Sst[:, pair, :], egl[:, i, pair:pair + 1], tmp[:, pair * P:(pair + 1) * P],
                            ALU.mult, ALU.add)
                    nc.vector.drain().then_inc(d_dve, 1)
                    v.wait_ge(d_pool, pool_at(i, "osq"))
                    nc.vector.tensor_reduce(dss[:, 0:4], dsq[:, 0:256].rearrange("p (h d) -> p h d", d=HD), AX.X, ALU.add)
                    nc.vector.drain()
                    ts(dss[:, 0:4], dss[:, 0:4], 1.0 / HD, EPS, ALU.mult, ALU.add).then_inc(d_dve, 1)
                    tt(o1, o1, zg[:, i, :], ALU.mult)
                    nc.vector.drain()
                    v.wait_ge(d_pool, pool_at(i, "ors"))
                    o3 = o1.rearrange("p (h d) -> p h d", d=HD)
                    tt(o3, o3, bc_h(drs[:, 0:4]), ALU.mult).then_inc(d_dve, 1)

            v.wait_ge(slab_in, 16)
            v.wait_ge(proj_done, len(STEPS))
            v.wait_ge(qk_turned, 16)
            idx = 0
            for ev in mixer_schedule():
                if ev[0] == "scores":
                    n = ev[1]
                    i, h = divmod(n, AT_HEADS)
                    L = (i + 1) * P
                    v.wait_ge(s_scores, n + 1)
                    if n >= 2:
                        v.wait_ge(s_turn, first_turn[("p", n - 1)])
                        v.wait_ge(s_exp, n - 1)
                    scores = ps[:, 6:8, :].rearrange("p b n -> p (b n)")[:, 0:L]
                    nc.vector.tensor_tensor_reduce(prob[:, n % 2, 0:L], scores, slab[:, h, 896 - i * P:896 - i * P + L],
                                                   1.0, -3e38, ALU.add, ALU.max, mx[:, n % 2:n % 2 + 1])
                    nc.vector.drain()
                    ts(nmx[:, n % 2:n % 2 + 1], mx[:, n % 2:n % 2 + 1], -1.0, None, ALU.mult).then_inc(s_max, 1)
                elif ev[0] == "dn":
                    dn(ev[1], ev[2])
                elif ev[0] == "turn":
                    n = ev[1]
                    for g, cnt in turn_groups(n):
                        if TAKER[idx] == "v":
                            v.wait_ge(s_turn, idx + 1)
                            if n >= 2:
                                v.wait_ge(s_values, n - 1)
                            nc.vector.tensor_copy(probT[:, n % 2, g * P:(g + cnt) * P], ps[:, 4 + idx % 2, 0:cnt * P])\
                                .then_inc(s_turned_v, 1)
                        idx += 1
                elif ev[0] == "values":
                    n = ev[1]
                    i, h = divmod(n, AT_HEADS)
                    if h == AT_HEADS - 1:
                        v.wait_ge(s_values, n + 1)
                        v.wait_ge(s_exp, n + 1)
                        if i:
                            v.wait_ge(s_turn, first_turn[("o", i - 1)] + 1)
                        nc.vector.reciprocal(rZ, Z[:, i % 2, :])
                        nc.vector.drain()
                        tt(att.rearrange("p (h d) -> p h d", d=HD), ps[:, 3, :].rearrange("p (h d) -> p h d", d=HD),
                           bc_h(rZ), ALU.mult).then_inc(s_att, 1)
                else:
                    i = ev[1]
                    if TAKER[idx] == "v":
                        v.wait_ge(s_turn, idx + 1)
                        nc.vector.tensor_copy(mixT_at[:, :, i * P:(i + 1) * P],
                                              flipped(ps[:, 4 + idx % 2, :].rearrange("p (c n) -> p c n", c=4))).then_inc(s_turned_v, 1)
                    idx += 1

            v.wait_ge(ffn_in, 32)
            v.wait_ge(params_in, 16)

            def residual(t):
                v.wait_ge(out_mm, t + 1)
                v.wait_ge(xs_in[t % 2], 16 * (t // 2 + 1))
                tt(xs[:, t % 2, :], ps[:, 2 * (t % 2):2 * (t % 2) + 2, :].rearrange("p b n -> p (b n)"), xs[:, t % 2, :],
                   ALU.add).then_inc(x2_done, 1)

            def gained(t):
                v.wait_ge(x2_rs, t + 1)
                if t >= 2:
                    v.wait_ge(h2_turned, t - 1)
                    v.wait_ge(h2_out[t % 2], 16 * (t // 2))
                stt(h2s[:, t % 2, :], xs[:, t % 2, :], rs[:, t:t + 1], g_ffn, ALU.mult, ALU.mult).then_inc(h2_done, 1)

            def logits_out(t):
                v.wait_ge(logit_mm, t + 1)
                tt(logits[:, t, :], ps[:, 6, 0:36], par[:, P_RBIAS:P_RBIAS + 36], ALU.add).then_inc(logit_sb, 1)

            for t in range(TILES):
                residual(t)
                gained(t)
                if t:
                    logits_out(t - 1)
            logits_out(TILES - 1)
            v.wait_ge(out_mm, TILES)
            glog = logits[:, :, 0:4]
            nc.vector.memset(padded, -3e38)
            nc.vector.memset(zero256, 0.0)
            nc.vector.drain()
            nc.vector.tensor_copy(padded[:, :, 0:4], glog)
            nc.vector.drain()
            for t in range(TILES):
                nc.vector.max(gtop[:, t, :], padded[:, t, :])
            nc.vector.drain()
            for t in range(TILES):
                nc.vector.max_index(gtop_i[:, t, :], gtop[:, t, :], padded[:, t, :])
            tt(gexp, glog, gtop[:, :, 0:1].to_broadcast([P, TILES, 4]), ALU.subtract)
            nc.vector.drain().then_inc(route_v, 1)
            nc.vector.tensor_copy(g_idx, gtop_i[:, :, 0])
            nc.vector.drain()
            tt(g_hot, bc_f(cst[:, C_J:C_J + 4], TILES), bc_h(g_idx, 4), ALU.is_equal)
            nc.vector.drain()
            ts(g_hot, g_hot, -1.0, -NEG, ALU.add, ALU.mult)
            nc.vector.drain()
            tt(em.rearrange("p t (g e) -> p t g e", g=4), logits[:, :, 4:36].rearrange("p t (g e) -> p t g e", g=4),
               g_hot.unsqueeze(3).to_broadcast([P, TILES, 4, 8]), ALU.add)
            nc.vector.drain()
            for t in range(TILES):
                nc.vector.max(etop[:, t, :], em[:, t, :])
            nc.vector.drain()
            for t in range(TILES):
                nc.vector.max_index(etop_i[:, t, :], etop[:, t, :], em[:, t, :])
            tt(e_diff, etop[:, :, 1], etop[:, :, 0], ALU.subtract)
            nc.vector.drain().then_inc(route_v, 1)
            nc.vector.tensor_copy(e_idx.rearrange("p c t -> p t c"), etop_i[:, :, 0:2])
            nc.vector.drain()
            for c in range(2):
                tt(hot[:, c], bc_f(cst[:, C_E:C_E + EXPERTS], TILES), bc_h(e_idx[:, c, :], EXPERTS), ALU.is_equal)
            nc.vector.drain()
            tt(hots, hot[:, 0], hot[:, 1], ALU.add)
            nc.vector.memset(before[:, 0, :], 0.0)
            for t in range(1, TILES):
                nc.vector.drain()
                tt(before[:, t, :], before[:, t - 1, :], hots[:, t - 1, :], ALU.add)
            nc.vector.drain().then_inc(route_v, 1)
            v.wait_ge(route_a, 2)
            nc.vector.tensor_reduce(p_grp, gexp, AX.X, ALU.add)
            ts(gates[:, 0, :], e_diff, 1.0, None, ALU.add)
            nc.vector.drain()
            tt(gates[:, 0, :], gates[:, 0, :], p_grp, ALU.mult)
            nc.vector.drain()
            nc.vector.reciprocal(gates[:, 0, :], gates[:, 0, :])
            nc.vector.drain()
            tt(gates[:, 1, :], gates[:, 0, :], e_diff, ALU.mult)
            v.wait_ge(rank_mm, 1)
            nc.vector.tensor_copy(rank.rearrange("p t e -> p (t e)"), ps[:, 7, 0:256])
            nc.vector.tensor_copy(e_count, ps[:, 7, 256:288])
            nc.vector.drain()
            for c in range(2):
                tt(rtmp, rank, hot[:, c], ALU.mult)
                nc.vector.drain()
                nc.vector.tensor_reduce(rk_k[:, c, :], rtmp, AX.X, ALU.add)
                nc.vector.drain()
            ts(rk_k, rk_k, -1.0, None, ALU.add)
            nc.vector.drain()
            for c in range(2):
                tt(jhot[:, c], bc_h(rk_k[:, c, :], 8), bc_f(cst[:, C_J128:C_J128 + 8], TILES), ALU.is_ge)
            nc.vector.drain()
            nc.vector.tensor_reduce(jn, jhot, AX.X, ALU.add)
            nc.vector.drain()
            ts(jn, jn, -1.0, None, ALU.add)
            nc.vector.drain()
            stt(rmod, jn, -float(P), rk_k, ALU.mult, ALU.add)
            for c in range(2):
                tt(jhot[:, c], bc_h(jn[:, c, :], 8), bc_f(cst[:, C_J:C_J + 8], TILES), ALU.is_equal)
            nc.vector.drain()
            for c in range(2):
                stt(jhot[:, c], bc_h(cst[:, C_TOK:C_TOK + TILES], 8), float(c * SEQ + 1), jhot[:, c], ALU.add, ALU.mult)
            nc.vector.drain()
            for m in range(2 * TILES):
                t, c = divmod(m, 2)
                if m >= 2:
                    v.wait_ge(list_mm, m - 1)
                ts(r_hot[:, m % 2, :], cst[:, C_IOTA:C_IOTA + P], rmod[:, c, t:t + 1], None, ALU.is_equal)
                tt(r_val[:, m % 2, :].rearrange("p (e j) -> p e j", j=8), bc_h(hot[:, c, t, :], 8),
                   bc_f(jhot[:, c, t, :], EXPERTS), ALU.mult)
                nc.vector.drain().then_inc(list_v, 1)
            tt(active.rearrange("p (e j) -> p e j", j=8), bc_h(e_count, 8), bc_f(cst[:, C_THR:C_THR + 8], EXPERTS), ALU.is_gt)
            nc.vector.drain()
            nc.vector.tensor_tensor_scan(slot_of, active, zero256, 0.0, ALU.add, ALU.add)
            nc.vector.drain()
            nc.vector.tensor_copy(n_ov[:, 0:1], slot_of[:, 255:256])
            nc.vector.drain()
            tt(slot_of, slot_of, active, ALU.mult)
            v.wait_ge(list_mm, 2 * TILES)
            nc.vector.tensor_copy(code, ps[:, 6, 0:256])
            nc.vector.drain()
            nc.vector.tensor_copy(slots[:, 0:EXPERTS], code.rearrange("p (e j) -> p e j", j=8)[:, :, 0])
            for m in range(EXTRA):
                stt(otmp, slot_of, float(m + 1), code, ALU.is_equal, ALU.mult, accum_out=slots[:, EXPERTS + m:EXPERTS + m + 1])
                nc.vector.drain()
                stt(otmp, slot_of, float(m + 1), cst[:, C_EJ:C_EJ + 256], ALU.is_equal, ALU.mult, accum_out=ov_e_f[:, m:m + 1])
                nc.vector.drain()
            nc.vector.tensor_copy(ov_e, ov_e_f)
            ts(slots, slots, -1.0, None, ALU.add)
            nc.vector.drain()
            ts(tok_f, slots, float(SEQ), -float(SEQ), ALU.is_ge, ALU.mult)
            ts(dst_f, slots, 0.0, 4.0 * SEQ, ALU.is_lt, ALU.mult)
            nc.vector.drain()
            tt(tok_f, tok_f, slots, ALU.add)
            tt(dst_f, dst_f, slots, ALU.add)
            nc.vector.drain()
            ts(tok_f, tok_f, 0.0, None, ALU.max)
            nc.vector.drain()
            nc.vector.tensor_copy(tok_of[:, 0:SLOTS], tok_f)
            nc.vector.tensor_copy(dst_of[:, 0:SLOTS], dst_f)
            nc.vector.drain().then_inc(slots_ready, 1)

            def rowsT(slot, u):
                v.wait_ge(rows_turned, slot + 1)
                at_least(v, gu_mm, slot - 1)
                nc.vector.tensor_copy(hgT[:, u, 4:8, :], ps[:, 1, :].rearrange("p (k n) -> p k n", k=4)).then_inc(rowsT_v, 1)

            def expert(slot, u, pair):
                v.wait_ge(silu_done, slot + 1)
                at_least(v, act_turned, slot)
                tt(act_g, silu_g, ps[:, 3, :], ALU.mult).then_inc(act_done, 1)
                rowsT(slot + 1, 1 - u)
                v.wait_ge(down_mm, slot + 1)
                at_least(v, y_out[u], pair * 16)
                nc.vector.tensor_copy(ys[:, u, 512:1024], ps[:, 6, :]).then_inc(y_v, 1)

            rowsT(0, 0)
            for_blocks(v, expert)
            for t in range(TILES):
                v.wait_ge(final_in[t % 2], 48 * (t // 2 + 1))
                x_t = fx[:, t % 2, :]
                stt(x_t, fy[:, t % 2, 0, :], gates[:, 0, t:t + 1], x_t, ALU.mult, ALU.add)
                nc.vector.drain()
                stt(x_t, fy[:, t % 2, 1, :], gates[:, 1, t:t + 1], x_t, ALU.mult, ALU.add).then_inc(final_v, 1)

        @block.scalar
        def _(act):
            f = nc.scalar.activation
            act.dma_start(par, a["params"]).then_inc(params_in, 16)
            for t in range(TILES):
                act.wait_ge(x_in[t], 16)
                act.wait_ge(sumsq_done, t)
                f(junk, x_all[:, t, :], ACT.Square, accum_out=ss[:, t:t + 1]).then_inc(sumsq_done, 1)
            act.wait_ge(table_mm, 1)
            f(bvec[0:AT_HEADS, :].rearrange("p (c n) -> p c n", c=3), ps[0:AT_HEADS, 5:8, 0:384], ACT.Copy).then_inc(table_sb, 1)
            act.wait_ge(table_sb, 1)
            act.dma_start(bias_dram, bvec[0:AT_HEADS, :]).then_inc(bias_out, 16)

            def put_qk(j):
                act.wait_ge(qk_turned, j + 1)
                col = P_QN + j // 8
                turned = ps[:, 4 + j % 2, :].rearrange("p (c n) -> p c n", c=4)
                f(qkT[:, j // 8, :, (j % 8) * P:(j % 8 + 1) * P], flipped(turned) if j < TILES else turned,
                  ACT.Copy, scale=par[:, col:col + 1]).then_inc(qk_out, 1)

            act.wait_ge(pads_zero, 1)
            for n, (g, kind, c, m) in enumerate(STEPS):
                if kind == "glu":
                    continue
                act.wait_ge(proj_done, n + 1)
                bank = ps[:, n % 4, :]
                if kind == "gate":
                    last = f(yc[:, c, m * 512:(m + 1) * 512], bank, ACT.Sigmoid)
                elif kind == "dn":
                    last = f(dpad[:, c, 3 + m * 512:3 + (m + 1) * 512], bank, ACT.Copy)
                elif kind == "z":
                    f(ab[:, m, :], bank[:, 256:264], ACT.Copy)
                    last = f(zg[:, m, :], bank[:, 0:256], ACT.Silu)
                elif kind in "qk":
                    j = n - FIRST_QK
                    if j >= 2:
                        act.wait_ge(qk_turned, j - 1)
                    last = f(stage[:, j % 2, :], bank, ACT.Copy)
                else:
                    last = f(v_tok[:, m, :], bank, ACT.Copy)
                last.then_inc(act_took, 1)
                if n > FIRST_QK and n - FIRST_QK - 1 < 16:
                    put_qk(n - FIRST_QK - 1)
                if n == 20:
                    act.wait_ge(cv_centred, 1)
                    for c2 in range(2):
                        f(ypad[:, c2, 0:SEQ], yc[:, c2, :], ACT.Square).then_inc(cv_squared, 1)
                if n == 23:
                    act.wait_ge(cv_varsb, 1)
                    f(junk, junk, ACT.Sqrt).then_inc(cv_rstd, 1)
                if n == FIRST_QK - 1:
                    for c2 in range(6):
                        act.wait_ge(dn_tapped, c2 + 1)
                        f(dconv[:, c2, :], dconv[:, c2, :], ACT.Silu).then_inc(dn_silu, 1)
                    act.wait_ge(cv_normed, 1)
                    for c2 in range(2):
                        f(yc[:, c2, :], yc[:, c2, :], ACT.Silu, scale=par[:, P_LNG + c2:P_LNG + c2 + 1],
                          bias=par[:, P_LNB + c2:P_LNB + c2 + 1]).then_inc(cv_out, 1)
            act.wait_ge(gate_v, 1)
            f(t2, t2, ACT.Exp)
            f(t3, t3, ACT.Exp, scale=-1.0)
            f(ea, par[:, P_ALOG:P_ALOG + 4], ACT.Exp).then_inc(gate_a, 1)
            act.wait_ge(gate_a, 1)
            f(t2, t2, ACT.Ln, bias=1.0).then_inc(gate_a, 1)
            act.wait_ge(gate_v, 5)
            f(eG, Gc, ACT.Exp).then_inc(gate_a, 1)
            f(ekd, ekd, ACT.Exp).then_inc(gate_a, 1)
            f(egl_all, Gtot, ACT.Exp).then_inc(gate_a, 1)

            def dn(i, k):
                if k >= len(DN_PIECES):
                    return
                piece = DN_PIECES[k]
                if piece == "split":
                    act.wait_ge(d_pe, pe_at(i, "split"))
                    if i:
                        act.wait_ge(d_pe, pe_at(i - 1, "norm"))
                        act.wait_ge(d_pool, pool_at(i - 1, "kdvb"))
                    f(tok[:, 0:512], ps[:, 0, :], ACT.Copy)
                    f(tok[:, 512:768], ps[:, 1, 0:256], ACT.Copy).then_inc(d_act, 1)
                    act.wait_ge(d_pe, pe_at(i, "gb"))
                    if i:
                        act.wait_ge(d_dve, dve_at(i - 1, "gram"))
                    for h in range(4):
                        last = f(dI[:, h, :], ps[:, 2, h * P:(h + 1) * P], ACT.Exp, bias=negG[:, 4 * i + h:4 * i + h + 1])
                    last.then_inc(d_act, 1)
                elif piece == "norm":
                    act.wait_ge(d_pe, pe_at(i, "norm"))
                    if i:
                        act.wait_ge(d_pe, pe_at(i - 1, "carry"))
                    f(tT.rearrange("p c m n -> p c (m n)"), ps[:, 0:2, 0:384], ACT.Copy).then_inc(d_act, 1)
                elif piece[0] == "x":
                    act.wait_ge(d_pe, pe_at(i, piece))
                    f(Xs.rearrange("p h n -> p (h n)"), ps[:, 2, :], ACT.Copy).then_inc(d_act, 1)
                elif piece == "fresh":
                    act.wait_ge(d_pe, pe_at(i, "fresh"))
                    f(vn, ps[:, 0, 0:256], ACT.Copy).then_inc(d_act, 1)
                elif piece == "out":
                    act.wait_ge(d_pe, pe_at(i, "out"))
                    f(mixT_dn[:, :, i * P:(i + 1) * P], ps[:, 2, 0:256].rearrange("p (c n) -> p c n", c=2),
                      ACT.Copy).then_inc(d_act, 1)

            idx = 0
            for ev in mixer_schedule():
                if ev[0] == "scores":
                    n = ev[1]
                    i, h = divmod(n, AT_HEADS)
                    L = (i + 1) * P
                    act.wait_ge(s_max, n + 1)
                    if h == 0 and i >= 2:
                        act.wait_ge(s_att, i - 1)
                    f(prob[:, n % 2, 0:L], prob[:, n % 2, 0:L], ACT.Exp, bias=nmx[:, n % 2:n % 2 + 1],
                      accum_out=Z[:, i % 2, h:h + 1]).then_inc(s_exp, 1)
                elif ev[0] == "dn":
                    dn(ev[1], ev[2])
                elif ev[0] == "turn":
                    n = ev[1]
                    for g, cnt in turn_groups(n):
                        if TAKER[idx] == "a":
                            act.wait_ge(s_turn, idx + 1)
                            if n >= 2:
                                act.wait_ge(s_values, n - 1)
                            f(probT[:, n % 2, g * P:(g + cnt) * P], ps[:, 4 + idx % 2, 0:cnt * P], ACT.Copy)\
                                .then_inc(s_turned_a, 1)
                        idx += 1
                elif ev[0] == "att_out":
                    i = ev[1]
                    if TAKER[idx] == "a":
                        act.wait_ge(s_turn, idx + 1)
                        f(mixT_at[:, :, i * P:(i + 1) * P], flipped(ps[:, 4 + idx % 2, :].rearrange("p (c n) -> p c n", c=4)),
                          ACT.Copy).then_inc(s_turned_a, 1)
                    idx += 1

            act.wait_ge(d_pe, TILES * len(PE_MARKS))
            act.wait_ge(d_dve, TILES * len(DVE_MARKS))

            def rows2(t):
                act.wait_ge(h2_turned, t + 1)
                if t >= 2:
                    act.wait_ge(logit_mm, t - 1)
                f(h2T[:, t % 2].rearrange("p k n -> p (k n)"), ps[:, 4:6, :].rearrange("p b n -> p (b n)"), ACT.Copy)\
                    .then_inc(h2T_done, 1)

            for t in range(TILES):
                act.wait_ge(x2_done, t + 1)
                act.wait_ge(x2_sq, t)
                f(junk3, xs[:, t % 2, :], ACT.Square, accum_out=ss[:, t:t + 1]).then_inc(x2_sq, 1)
                if t:
                    rows2(t - 1)
            rows2(TILES - 1)
            act.wait_ge(route_v, 1)
            f(gexp, gexp, ACT.Exp).then_inc(route_a, 1)
            act.wait_ge(route_v, 2)
            f(e_diff, e_diff, ACT.Exp).then_inc(route_a, 1)

            def rowsT(slot, u):
                act.wait_ge(rows_turned, slot + 1)
                at_least(act, gu_mm, slot - 1)
                f(hgT[:, u, 0:4, :], ps[:, 0, :].rearrange("p (k n) -> p k n", k=4), ACT.Copy).then_inc(rowsT_a, 1)

            def expert(slot, u, pair):
                act.wait_ge(gu_mm, slot + 1)
                at_least(act, act_done, slot)
                f(silu_g, ps[:, 2, :], ACT.Silu).then_inc(silu_done, 1)
                rowsT(slot + 1, 1 - u)
                act.wait_ge(act_turned, slot + 1)
                at_least(act, down_mm, slot)
                f(actT.rearrange("p k n -> p (k n)"), ps[:, 4, :], ACT.Copy).then_inc(actT_done, 1)
                act.wait_ge(down_mm, slot + 1)
                at_least(act, y_out[u], pair * 16)
                f(ys[:, u, 0:512], ps[:, 5, :], ACT.Copy).then_inc(y_a, 1)

            act.wait_ge(slots_ready, 1)
            rowsT(0, 0)
            for_blocks(act, expert)

        @block.gpsimd
        def _(pool):
            tt, ts = nc.gpsimd.tensor_tensor, nc.gpsimd.tensor_scalar
            pool.wait_ge(consts_in, 16)
            for t in range(TILES):
                pool.wait_ge(sumsq_done, t + 1)
                ts(ss[:, t:t + 1], ss[:, t:t + 1], 1.0 / D, EPS, ALU.mult, ALU.add).then_inc(meansq_done, 1)
                pool.wait_ge(meansq_done, t + 1)
                tt(rs[:, t:t + 1], ss[:, t:t + 1], half_neg[:, 0:1], ALU.pow).then_inc(rms_done, 1)
            for j in range(16):
                pool.wait_ge(*act_taken(FIRST_QK + j))
                if j:
                    pool.wait_ge(qk_ss, j)
                tt(sqb, stage[:, j % 2, :], stage[:, j % 2, :], ALU.mult).then_inc(qk_sq, 1)
                pool.wait_ge(qk_ss, j + 1)
                if j >= 2:
                    pool.wait_ge(qk_normed, j - 1)
                tt(rs2[:, j % 2, :], ss2[:, j % 2, :], half_neg, ALU.pow).then_inc(qk_rs, 1)

            pool.wait_ge(qk_turned, 16)
            pool.wait_ge(gate_a, 5)

            def dn(i, k):
                if k >= len(DN_PIECES):
                    return
                piece = DN_PIECES[k]
                ti = slice(4 * i, 4 * i + 4)
                h4 = lambda x: x.rearrange("p (h d) -> p h d", d=HD)
                if piece == "split":
                    if i:
                        pool.wait_ge(d_pe, pe_at(i - 1, "gb"))
                    for h in range(4):
                        last = ts(Tg[:, h, :], tri, g_col[:, 4 * i + h:4 * i + h + 1], None, ALU.mult)
                    last.then_inc(d_pool, 1)
                    pool.wait_ge(d_act, act_at(i, "split"))
                    if i:
                        pool.wait_ge(d_dve, dve_at(i - 1, "oss"))
                    tt(dsq, tok[:, 0:512], tok[:, 0:512], ALU.mult).then_inc(d_pool, 1)
                    pool.wait_ge(d_dve, dve_at(i, "ss"))
                    tt(drs, dss, half_neg, ALU.pow).then_inc(d_pool, 1)
                    pool.wait_ge(d_dve, dve_at(i, "qkn"))
                    if i:
                        pool.wait_ge(d_pe, pe_at(i - 1, "emit"))
                    tt(h4(kb), h4(tok[:, 256:512]), bc_h(beta[:, ti]), ALU.mult).then_inc(d_pool, 1)
                    tt(h4(kd), h4(tok[:, 256:512]), bc_h(ekd[:, ti]), ALU.mult)
                    tt(h4(vb), h4(tok[:, 512:768]), bc_h(beta[:, ti]), ALU.mult)
                    nc.gpsimd.drain().then_inc(d_pool, 1)
                elif piece == "gram":
                    pool.wait_ge(d_dve, dve_at(i, "gram"))
                    for lv in range(2):
                        if i:
                            pool.wait_ge(d_pe, pe_at(i - 1, f"x{LEVELS - 2 + lv}"))
                            pool.wait_ge(d_dve, dve_at(i - 1, "inv1"))
                        tt(AM[:, lv], At, bc_f(lvl(lv), 4), ALU.mult).then_inc(d_pool, 1)
                elif piece[0] == "x" and int(piece[1:]) < LEVELS - 1:
                    lv = int(piece[1:]) + 1
                    if lv == 2:
                        pool.wait_ge(d_dve, dve_at(i, "inv1"))
                    else:
                        pool.wait_ge(d_pe, pe_at(i, f"x{lv - 2}"))
                    tt(AM[:, lv % 2], At, bc_f(lvl(lv), 4), ALU.mult).then_inc(d_pool, 1)
                elif piece == "emit":
                    pool.wait_ge(d_dve, dve_at(i, "emit"))
                    tt(dsq[:, 0:256], o1, o1, ALU.mult).then_inc(d_pool, 1)
                    pool.wait_ge(d_dve, dve_at(i, "oss"))
                    tt(drs[:, 0:4], dss[:, 0:4], half_neg[:, 0:4], ALU.pow).then_inc(d_pool, 1)

            for ev in mixer_schedule():
                if ev[0] == "dn":
                    dn(ev[1], ev[2])

            pool.wait_ge(d_dve, TILES * len(DVE_MARKS))
            for t in range(TILES):
                pool.wait_ge(x2_sq, t + 1)
                ts(ss[:, t:t + 1], ss[:, t:t + 1], 1.0 / D, EPS, ALU.mult, ALU.add).then_inc(x2_ms, 1)
                pool.wait_ge(x2_ms, t + 1)
                tt(rs[:, t:t + 1], ss[:, t:t + 1], half_neg[:, 0:1], ALU.pow).then_inc(x2_rs, 1)

            def gather(slot, u, pair):
                at_least(pool, rows_turned, slot - 1)
                at_least(pool, y_out[u], 16 * pair)
                nc.gpsimd.tensor_copy(tok_b[:, u:u + 1], tok_of[:, bass.ds(slot, 1)])
                nc.gpsimd.tensor_copy(dst_b[:, u:u + 1], dst_of[:, bass.ds(slot, 1)])
                nc.gpsimd.drain()
                nc.gpsimd.indirect_dma_start(hg[:, u, :], None, h2_dram, bass.IndirectOffsetOnAxis(ap=tok_b[:, u:u + 1], axis=0))\
                    .then_inc(rows_in[u], 16)

            def expert(slot, u, pair):
                gather(slot + 1, 1 - u, pair + u)
                pool.wait_ge(y_a, slot + 1)
                pool.wait_ge(y_v, slot + 1)
                tt(dst_t[:, u:u + 1], dst_b[:, u:u + 1], zero256[:, 0:1], ALU.add)
                nc.gpsimd.drain()
                nc.gpsimd.tensor_copy(dst_i[:, u:u + 1], dst_t[:, u:u + 1])
                nc.gpsimd.drain()
                nc.gpsimd.indirect_dma_start(y_dram, bass.IndirectOffsetOnAxis(ap=dst_i[:, u:u + 1], axis=0), ys[:, u, :], None,
                                             bounds_check=2 * SEQ - 1, oob_is_err=False).then_inc(y_out[u], 16)
                pool.wait_ge(y_out[u], 16 * (pair + 1))

            pool.wait_ge(slots_ready, 1)
            for u in range(2):
                pool.wait_ge(h2_out[u], 16 * TILES // 2)
            gather(0, 0, 0)
            for_blocks(pool, expert)
            nc.gpsimd.drain().then_inc(y_all_out, 1)


def lay_out(inputs):
    f = {k: np.asarray(v) for k, v in inputs.items()}
    cols = [f["cv_dw"][0].T.reshape(2, P, CV_TAPS).transpose(1, 0, 2).reshape(P, -1),
            f["dn_conv"][0].T.reshape(6, P, DN_TAPS).transpose(1, 0, 2).reshape(P, -1),
            f["norm_mix"][0].reshape(KC, P).T,
            f["cv_dw_bias"][0].reshape(2, P).T, f["cv_ln_g"][0].reshape(2, P).T, f["cv_ln_b"][0].reshape(2, P).T,
            np.tile(f["at_q_norm"][0], 2)[:, None], np.tile(f["at_k_norm"][0], 2)[:, None],
            np.broadcast_to(f["dn_a_log"][0], (P, DN_HEADS)), np.broadcast_to(f["dn_dt_bias"][0], (P, DN_HEADS)),
            np.broadcast_to(f["dn_out_norm"][0], (P, HD))]
    table = np.ones((P, 36), np.float32)
    table[:N_BUCKETS, :AT_HEADS] = f["rel_bias"]
    cols.append(table)
    cols.append(np.broadcast_to(np.concatenate([f["router_group_b"][0], f["router_expert_b"][0]]), (P, GROUPS + EXPERTS)))
    return {
        "x": f["x"].reshape(SEQ, D), "constants": shape_constants(), "distances": distance_constants(),
        "params": np.ascontiguousarray(np.concatenate(cols, 1)),
        "w_in": f["w_in"].reshape(D, N_IN), "w_out": f["w_out"].reshape(D, D),
        "norm_ffn": np.ascontiguousarray(np.broadcast_to(f["norm_ffn"][0], (P, D))),
        "router": np.ascontiguousarray(np.concatenate([f["router_group_w"][0], f["router_expert_w"][0]], 1)),
        "ex_gate": f["ex_gate"][0], "ex_up": f["ex_up"][0], "ex_down": f["ex_down"][0],
    }


def kernel(**inputs):
    import concourse.bacc as _bacc
    from concourse.bass_utils import run_bass_kernel_spmd as _run

    arrays = lay_out(inputs)
    nc = _bacc.Bacc("TRN2", target_bir_lowering=False, num_devices=1)
    args = {k: nc.dram_tensor(f"in_{k}", v.shape, mybir.dt.from_np(v.dtype), kind="ExternalInput").ap()
            for k, v in arrays.items()}
    out = nc.dram_tensor("out", [SEQ, D], F32, kind="ExternalOutput").ap()
    build(nc, args, out)
    r = _run(nc, [{f"in_{k}": v for k, v in arrays.items()}], core_ids=[0])
    return r.results[0]["out"].reshape(1, SEQ, D)
```

```python
import math
from contextlib import ExitStack

import numpy as np
import concourse.bass as bass
from concourse import mybir

F32 = mybir.dt.float32
U32 = mybir.dt.uint32
ALU = mybir.AluOpType
ACT = mybir.ActivationFunctionType
AX = mybir.AxisListType

P = 128
SEQ = 1024
D = 1024
TILES = SEQ // P
KC = D // P
EPS = 1e-6
NEG = -1e30

DN_HEADS, HD = 4, 64
DN_W = DN_HEADS * HD
DN_TAPS = 4
AT_HEADS = 8
AT_W = AT_HEADS * HD
CV_W = 256
CV_TAPS = 31
N_IN = 4 * DN_W + 2 * DN_HEADS + 3 * AT_W + 2 * CV_W
WINDOWS = ((128, 1), (512, 4), (2048, 16))
N_BUCKETS, MAX_DISTANCE = 32, 2048
GROUPS, PER_GROUP = 4, 8
EXPERTS = GROUPS * PER_GROUP
DE = D // 2
FC = DE // P
NREL = SEQ + P
LEVELS = 7

C_ID, C_TRI, C_ONE, C_NEG, C_LVL = 0, P, 2 * P, 3 * P, 4 * P
C_BD = C_LVL + LEVELS * P
C_IOTA = C_BD + P
C_E = C_IOTA + P
C_J = C_E + EXPERTS
C_TOK = C_J + 8
C_HALF = C_TOK + TILES
C_J128 = C_HALF + 8
C_THR = C_J128 + 8
C_EJ = C_THR + 8
NCONST = C_EJ + 256

RANKS = SEQ // P
SLOTS = EXPERTS + 2 * 8
EXTRA = SLOTS - EXPERTS

P_CVW = 0
P_DNW = P_CVW + 2 * CV_TAPS
P_GMIX = P_DNW + 6 * DN_TAPS
P_CVB = P_GMIX + KC
P_LNG = P_CVB + 2
P_LNB = P_LNG + 2
P_QN = P_LNB + 2
P_KN = P_QN + 1
P_ALOG = P_KN + 1
P_DT = P_ALOG + DN_HEADS
P_ON = P_DT + DN_HEADS
P_RB = P_ON + HD
P_RBIAS = P_RB + 36
NPARAM = P_RBIAS + GROUPS + EXPERTS


def shape_constants():
    j, i = np.arange(P)[:, None], np.arange(P)[None, :]
    cols = [(i == j), (j <= i), np.ones((P, P)), np.where(j <= i, 0.0, NEG)]
    for level in range(LEVELS):
        s = 1 << level
        cols.append((i // (2 * s) == j // (2 * s)) & (i // s % 2 == 1) & (j // s % 2 == 0))
    cols.append(i // HD == j // HD)
    cols.append(np.broadcast_to(i, (P, P)))
    cols.append(np.broadcast_to(np.arange(EXPERTS), (P, EXPERTS)))
    cols.append(np.broadcast_to(np.arange(8), (P, 8)))
    cols.append(np.arange(P)[:, None] + P * np.arange(TILES)[None, :])
    cols.append(np.full((P, 8), -0.5))
    cols.append(np.broadcast_to(P * np.arange(8), (P, 8)))
    cols.append(np.broadcast_to(np.where(np.arange(8), P * np.arange(8), 1e9), (P, 8)))
    cols.append(np.broadcast_to(np.repeat(np.arange(EXPERTS), 8), (P, 256)))
    return np.ascontiguousarray(np.concatenate([np.asarray(c, np.float32) for c in cols], 1))


def distance_constants():
    rel = SEQ - 1 - np.arange(NREL)
    exact = N_BUCKETS // 2
    d = np.maximum(rel, 1).astype(np.float32)
    log_bucket = exact + (np.log(d / np.float32(exact)) / np.float32(math.log(MAX_DISTANCE / exact))
                          * np.float32(N_BUCKETS - exact)).astype(np.int32)
    bucket = np.where(rel < exact, np.maximum(rel, 0), np.minimum(log_bucket, N_BUCKETS - 1))
    reach = sum(((rel >= 0) & (rel <= w) & (rel % r == 0)).astype(np.int32) for w, r in WINDOWS)
    rows = np.zeros((N_BUCKETS + 1, NREL), np.float32)
    rows[bucket, np.arange(NREL)] = 1.0
    rows[N_BUCKETS] = np.where(reach > 0, np.log(np.maximum(reach, 1)), NEG)
    return rows


def projection_steps():
    steps = [(0, "gate", c, n) for c in (0, 1) for n in (0, 1)]
    steps += [(0, "glu", c, n) for c in (0, 1) for n in (0, 1)]
    steps += [(1, "dn", c, n) for c in range(4) for n in (0, 1)]
    steps += [(2, "dn", c, n) for c in (4, 5) for n in (0, 1)]
    steps += [(2, "z", 0, t) for t in range(TILES)]
    steps += [(3, "q", 0, t) for t in range(TILES)]
    steps += [(4, "k", 1, t) for t in range(TILES)]
    steps += [(5, "v", 0, t) for t in range(TILES)]
    return steps


STEPS = projection_steps()
FIRST_QK = 28
O_CU = N_IN - 2 * CV_W
WGROUPS = [(O_CU, 512), (0, 512), (512, 520), (1032, 512), (1544, 512), (2056, 512)]
GW = 520


DN_PIECES = (["split", "ss", "qkn", "norm", "gram", "inv1"]
             + [f"{s}{lv}" for lv in range(1, LEVELS) for s in ("x", "y")]
             + ["carry", "fresh", "emit", "osum", "onorm", "out"])
DN_LAG = len(DN_PIECES) // 2


def attention_step(n):
    pair, rest = divmod(n, 2 * TILES)
    return pair, rest // 2, rest % 2


def mixer_schedule():
    n_att = TILES * AT_HEADS
    attention = []
    for n in range(n_att + 8):
        if n < n_att:
            attention.append((("scores", n), 2 * attention_step(n)[1] + 2))
        if 1 <= n <= n_att:
            attention.append((("turn", n - 1), attention_step(n - 1)[1] + 1))
        if 2 <= n <= n_att + 1:
            attention.append((("values", n - 2), attention_step(n - 2)[1] + 1))
        if n % 8 == 4 and n >= 12:
            attention.append((("att_out", n // 8 - 1), 1))
    pieces = []
    phases = (TILES + 1) * DN_LAG
    for phase in range(phases):
        i, k = divmod(phase, DN_LAG)
        if i:
            pieces.append((("dn", i - 1, k + DN_LAG), phase / phases))
        if i < TILES:
            pieces.append((("dn", i, k), (phase + 0.5) / phases))
    total, done, out = sum(c for _, c in attention), 0, []
    for event, cost in attention:
        while pieces and pieces[0][1] * total <= done:
            out.append(pieces.pop(0)[0])
        out.append(event)
        done += cost
    return out + [p for p, _ in pieces]


def turn_groups(n):
    blocks = attention_step(n)[1] + 1
    return [(g, min(4, blocks - g)) for g in range(0, blocks, 4)]


def build(nc, a, out, debug_stop=None):
    ctx = ExitStack()
    with ctx:
        def sem(name):
            return ctx.enter_context(nc.semaphore(name))

        arena = ctx.enter_context(nc.sbuf_tensor("arena", [P, 53200], F32))
        ps = ctx.enter_context(nc.psum_tensor("ps", [P, 8, 512], F32))

        def cut(at, *dims):
            size = int(np.prod(dims))
            flat = arena[:, at:at + size]
            if len(dims) == 1:
                return flat
            names = "abcd"[:len(dims)]
            return flat.rearrange("p (%s) -> p %s" % (" ".join(names), " ".join(names)),
                                  **{n: d for n, d in zip(names[1:], dims[1:])})

        A, B, C, DV, E, F, G, H, I, J = 0, 8192, 16512, 24704, 28800, 34964, 41108, 43220, 45328, 47376
        hT = cut(A, KC, SEQ)
        wb = cut(B, 2, KC, GW)
        x_all = cut(C, TILES, D)
        qkT = cut(C, 2, 4, SEQ)
        v_tok = cut(DV, TILES, AT_W)
        dpad = cut(E, 6, SEQ + 3)
        dconv = cut(F, 6, SEQ)
        zg = cut(G, TILES, DN_W)
        ab = cut(G + 2048, TILES, 8)
        ypad = cut(H, 2, SEQ + 30)
        yc = cut(I, 2, SEQ)
        mixT_cv = yc
        cst = cut(J, NCONST)
        par = cut(J + NCONST, NPARAM)
        K = J + NCONST + NPARAM
        gate32 = cut(K, 9, 32)
        K += 9 * 32
        small = cut(K, 64)
        K += 64
        junk = cut(K, D)
        stage = cut(K + D, 2, AT_W)
        sqb = cut(K + 2 * D, AT_W)
        assert K + 2 * D + AT_W <= 53200
        tabE = cut(B, 1152)
        bvec = cut(B + 1152, 1152)

        slab = cut(A, 2, 2, SEQ)
        prob = cut(B, 2, SEQ)
        probT = cut(B + 2048, 2, SEQ)
        mixT_at = cut(B + 4096, 4, SEQ)
        mixT_dn = cut(H, 2, SEQ)
        tok = cut(E, 3 * DN_W)
        tT = [cut(at, 2, 3, P) for at in (E + 768, A + 4096)]
        dI = cut(E + 1536, 4, P)
        At = cut(E + 2048, 4, P)
        qkD = [cut(at, 4, P) for at in (E + 2560, A + 4864)]
        AM = cut(E + 3072, 2, 4, P)
        T = cut(E + 4096, 4, P)
        Tt = [cut(at, 4, P) for at in (E + 4608, A + 5376)]
        Xs = cut(E + 5120, 4, P)
        Tg = cut(K, 4, P)
        dsq = cut(K + 512, 512)
        kb = cut(K + 1024, DN_W)
        kd = [cut(at, DN_W) for at in (K + 1280, A + 5888)]
        vb = [cut(at, DN_W) for at in (K + 1536, A + 6144)]
        R = cut(K + 1792, DN_W)
        vn = cut(K + 2048, DN_W)
        o1 = cut(K + 2304, DN_W)
        tmp = cut(K + 2560, DN_W)
        Sst = cut(K + 2816, 2, P)
        att = cut(E + 5632, AT_W)
        assert K + 3072 <= 53200

        w_out = [cut(at, D) for at in (C, C + SEQ, C + 2 * SEQ, C + 4 * SEQ, C + 5 * SEQ, C + 6 * SEQ, A, A + D)]
        xs = cut(B, 2, D)
        g_ffn = cut(B + 2048, D)
        router = cut(B + 3072, KC, 36)
        logits = cut(B + 3360, TILES, 36)
        h2s = cut(G, 2, D)
        h2T = cut(K, 2, KC, P)
        junk3 = cut(K + 2048, D)
        r0 = B + 4096
        padded = cut(r0, TILES, 8)
        gtop = cut(r0 + 64, TILES, 8)
        gtop_i = cut(r0 + 128, TILES, 8).bitcast(U32)
        em = cut(r0 + 192, TILES, EXPERTS)
        etop = cut(r0 + 448, TILES, 8)
        etop_i = cut(r0 + 512, TILES, 8).bitcast(U32)
        g_hot = cut(r0 + 576, TILES, 4)
        g_idx = cut(r0 + 608, TILES)
        e_idx = cut(r0 + 616, 2, TILES)
        p_grp = cut(r0 + 632, TILES)
        rk_k = cut(r0 + 640, 2, TILES)
        rmod = cut(r0 + 656, 2, TILES)
        jn = cut(r0 + 672, 2, TILES)
        gexp = cut(r0 + 688, TILES, 4)
        e_diff = cut(r0 + 720, TILES)
        jhot = cut(r0 + 768, 2, TILES, 8)
        hot = cut(r0 + 896, 2, TILES, EXPERTS)
        hots = cut(r0 + 1408, TILES, EXPERTS)
        before = cut(r0 + 1664, TILES, EXPERTS)
        rank = cut(r0 + 1920, TILES, EXPERTS)
        rtmp = cut(r0 + 2176, TILES, EXPERTS)
        e_count = cut(r0 + 2432, EXPERTS)
        r_hot = cut(r0 + 2464, 2, P)
        r_val = cut(r0 + 2720, 2, 256)
        code = cut(r0 + 3232, 256)
        active = cut(r0 + 3488, 256)
        slot_of = cut(r0 + 3744, 256)
        zero256 = cut(H, 256)
        otmp = cut(H + 256, 256)
        slots = cut(H + 512, SLOTS)
        code2 = cut(H + 560, SLOTS)
        tok_f = cut(H + 608, SLOTS)
        dst_f = cut(H + 656, SLOTS)
        tok_of = cut(H + 864, SLOTS + 2).bitcast(U32)
        dst_of = cut(H + 928, SLOTS + 2)
        ov_e_f = cut(H + 800, EXTRA)
        ov_e = cut(H + 816, EXTRA).bitcast(U32)
        n_ov = cut(H + 832, 8).bitcast(U32)
        gates = cut(H + 840, 2, TILES)
        tok_b = cut(H + 856, 2).bitcast(U32)
        dst_b = cut(H + 858, 2)
        dst_t = cut(H + 862, 2)
        tok_t = cut(H + 1000, 2)
        dst_i = cut(H + 860, 2).bitcast(U32)
        W = [cut(E, 3 * KC * DE), cut(C, 3 * KC * DE)]
        w_gate = [w[:, 0:KC * DE].rearrange("p (k n) -> p k n", k=KC) for w in W]
        w_up = [w[:, KC * DE:2 * KC * DE].rearrange("p (k n) -> p k n", k=KC) for w in W]
        w_down = [w[:, 2 * KC * DE:].rearrange("p (k n) -> p k n", k=FC) for w in W]
        hg = cut(A, 2, D)
        hgT = cut(A + 2048, 2, KC, P)
        silu_g = cut(A + 4096, DE)
        act_g = cut(A + 4608, DE)
        actT = cut(A + 5120, FC, P)
        ys = cut(A + 5632, 2, D)
        fx = cut(B, TILES, D)
        fy = [cut(at, TILES, D) for at in (C, C + 8192)]
        x2_dram = nc.dram_tensor("x2_rows", [SEQ, D], F32).ap()
        h2_dram = nc.dram_tensor("h2_rows", [SEQ, D], F32).ap()
        y_dram = nc.dram_tensor("expert_rows", [2 * SEQ, D], F32).ap()

        ident = cst[:, C_ID:C_ID + P]
        tri = cst[:, C_TRI:C_TRI + P]
        ones = cst[:, C_ONE:C_ONE + P]
        negm = cst[:, C_NEG:C_NEG + P]
        bd = cst[:, C_BD:C_BD + P]

        def lvl(n):
            return cst[:, C_LVL + n * P:C_LVL + (n + 1) * P]

        half_neg = cst[:, C_HALF:C_HALF + 8]
        g_col, beta, t1, t2, t3, Gc, Gtot, eG, ekd = (gate32[:, n, :] for n in range(9))
        ss = small[:, 0:8]
        rs = small[:, 8:16]
        ss2 = small[:, 16:32].rearrange("p (u h) -> p u h", u=2)
        rs2 = small[:, 32:48].rearrange("p (u h) -> p u h", u=2)
        ea = small[:, 48:52]
        mx = small[:, 52:54]
        nmx = small[:, 54:56]
        Z = small[:, 16:32].rearrange("p (u h) -> p u h", u=2)
        rZ = small[:, 32:40]
        egl = small[:, 0:16].rearrange("p (t c) -> p t c", c=2)
        dss = small[:, 40:48]
        drs = small[:, 56:64]
        egl_all = t3
        negG = t2

        def bc_h(col, n=HD):
            return col.unsqueeze(2).to_broadcast([P, col.shape[1], n])

        def bc_f(mat, n):
            return mat.unsqueeze(1).to_broadcast([P, n, mat.shape[1]])

        def flipped(ap):
            dims = [list(d) for d in ap.ap]
            step, n = dims[-1]
            dims[-1] = [-step, n]
            return bass.AP(tensor=ap.tensor, offset=ap.offset + step * (n - 1), ap=dims)

        bias_dram = nc.dram_tensor("bias_by_distance", [AT_HEADS, NREL], F32).ap()

        consts_in = sem("consts_in")
        params_in = sem("params_in")
        onehot_in = sem("onehot_in")
        x_in = [sem(f"x_in{t}") for t in range(TILES)]
        w_in_sem = [sem(f"w_in{n}") for n in range(2)]
        sumsq_done = sem("sumsq_done")
        meansq_done = sem("meansq_done")
        rms_done = sem("rms_done")
        h_scaled = sem("h_scaled")
        hT_turned = sem("hT_turned")
        hT_done = sem("hT_done")
        table_mm = sem("table_mm")
        table_sb = sem("table_sb")
        bias_out = sem("bias_out")
        slab_in = [sem(f"slab_in{n}") for n in range(2)]
        pads_zero = sem("pads_zero")
        proj_done = sem("proj_done")
        act_took = sem("act_took")
        dve_took = sem("dve_took")
        tap_done = sem("tap_done")
        cv_mean = sem("cv_mean")
        cv_centred = sem("cv_centred")
        cv_squared = sem("cv_squared")
        cv_var = sem("cv_var")
        cv_varsb = sem("cv_varsb")
        cv_rstd = sem("cv_rstd")
        cv_normed = sem("cv_normed")
        cv_out = sem("cv_out")
        dn_tapped = sem("dn_tapped")
        dn_silu = sem("dn_silu")
        qk_sq = sem("qk_sq")
        qk_ss = sem("qk_ss")
        qk_rs = sem("qk_rs")
        qk_normed = sem("qk_normed")
        qk_turned = sem("qk_turned")
        qk_out = sem("qk_out")
        zg_done = sem("zg_done")
        gate_a = sem("gate_a")
        gate_v = sem("gate_v")
        gate_p = sem("gate_p")
        s_scores = sem("s_scores")
        s_max = sem("s_max")
        s_exp = sem("s_exp")
        s_turn = sem("s_turn")
        s_turned_a = sem("s_turned_a")
        s_turned_v = sem("s_turned_v")
        s_values = sem("s_values")
        s_att = sem("s_att")
        s_attT = sem("s_attT")
        s_attT_out = sem("s_attT_out")
        d_pe = sem("d_pe")
        d_act = sem("d_act")
        d_dve = sem("d_dve")
        d_pool = sem("d_pool")

        w_out_in = sem("w_out_in")
        ffn_in = sem("ffn_in")
        xs_in = [sem(f"xs_in{n}") for n in range(2)]
        out_mm = sem("out_mm")
        x2_done = sem("x2_done")
        x2_sq = sem("x2_sq")
        x2_ms = sem("x2_ms")
        x2_rs = sem("x2_rs")
        h2_done = sem("h2_done")
        x2_out = [sem(f"x2_out{n}") for n in range(2)]
        h2_out = [sem(f"h2_out{n}") for n in range(2)]
        h2_turned = sem("h2_turned")
        h2T_done = sem("h2T_done")
        logit_mm = sem("logit_mm")
        logit_sb = sem("logit_sb")
        route_v = sem("route_v")
        route_a = sem("route_a")
        rank_mm = sem("rank_mm")
        list_v = sem("list_v")
        list_mm = sem("list_mm")
        slots_ready = sem("slots_ready")
        hg_zero = sem("hg_zero")
        gu_in = [sem(f"gu_in{n}") for n in range(2)]
        down_in = [sem(f"down_in{n}") for n in range(2)]
        rows_in = [sem(f"rows_in{n}") for n in range(2)]
        idx_copied = sem("idx_copied")
        rows_turned = sem("rows_turned")
        rowsT_a = sem("rowsT_a")
        rowsT_v = sem("rowsT_v")
        gu_mm = sem("gu_mm")
        silu_done = sem("silu_done")
        act_done = sem("act_done")
        act_turned = sem("act_turned")
        actT_done = sem("actT_done")
        down_mm = sem("down_mm")
        y_a = sem("y_a")
        y_v = sem("y_v")
        y_out = [sem(f"y_out{n}") for n in range(2)]
        final_in = [sem(f"final_in{n}") for n in range(TILES)]
        y_all_out = sem("y_all_out")
        final_v = sem("final_v")
        final_out = sem("final_out")
        x2_back = sem("x2_back")

        def at_least(eng, s, value):
            if not isinstance(value, int) or value > 0:
                eng.wait_ge(s, value)

        def experts_loop(eng, body):
            for u in range(2):
                body(u, u, 0)
            with eng.Fori(1, EXPERTS // 2) as pair:
                for u in range(2):
                    body(2 * pair + u, u, pair)

        def extras_loop(eng, body, finish=None):
            more = eng.value_load(n_ov[0:1, 0:1], min_val=0, max_val=EXTRA)
            if finish:
                with eng.If(more < 1):
                    finish(EXPERTS - 1, 1, EXPERTS // 2 - 1)
            with eng.Fori(EXPERTS // 2, SLOTS // 2) as pair:
                for u in range(2):
                    slot = 2 * pair + u
                    with eng.If(more + EXPERTS > slot):
                        body(slot, u, pair)
                        if finish:
                            with eng.If(more + EXPERTS < slot + 2):
                                finish(slot, u, pair)

        def act_taken(step):
            glu = [n for n, s in enumerate(STEPS[:step + 1]) if s[1] == "glu"]
            return (dve_took, len(glu)) if STEPS[step][1] == "glu" else (act_took, step + 1 - len(glu))

        group_end = {g: max(n for n, s in enumerate(STEPS) if s[0] == g) + 1 for g in range(6)}

        pe_marks = {p: [p] for p in DN_PIECES if p not in ("ss", "qkn", "osum", "onorm")}
        pe_marks["split"] = ["split", "gb"]
        act_marks = {"split": ["split", "decay"], "norm": ["norm"], "fresh": ["fresh"], "out": ["out"],
                     **{f"x{lv}": [f"x{lv}"] for lv in range(1, LEVELS)}}
        dve_marks = {**{p: [p] for p in ("ss", "qkn", "gram", "inv1", "carry", "emit", "osum", "onorm")},
                     **{f"y{lv}": [f"y{lv}"] for lv in range(1, LEVELS)}}
        pool_marks = {"split": ["tg", "sq"], "ss": ["rs"], "qkn": ["kb", "kdvb"], "gram": ["am0", "am1"],
                      **{f"x{lv}": [f"am{lv + 1}"] for lv in range(1, LEVELS - 1)}, "emit": ["osq"], "osum": ["ors"]}
        SCHEDULE = mixer_schedule()

        def in_order(marks):
            return [(ev[1], m) for ev in SCHEDULE if ev[0] == "dn" for m in marks.get(DN_PIECES[ev[2]], [])]

        PE_ORDER, ACT_ORDER, DVE_ORDER, POOL_ORDER = (in_order(m) for m in (pe_marks, act_marks, dve_marks, pool_marks))

        def pe_at(i, mark):
            return PE_ORDER.index((i, mark)) + 1

        def act_at(i, mark):
            return ACT_ORDER.index((i, mark)) + 1

        def dve_at(i, mark):
            return DVE_ORDER.index((i, mark)) + 1

        def pool_at(i, mark):
            return POOL_ORDER.index((i, mark)) + 1

        TURNS = []
        for ev in SCHEDULE:
            if ev[0] == "turn":
                TURNS += [("p", ev[1], g, c) for g, c in turn_groups(ev[1])]
            elif ev[0] == "att_out":
                TURNS.append(("o", ev[1], 0, 4))
        TAKER = ["v" if (n % 2) else "a" for n in range(len(TURNS))]

        def taken(idx):
            who = TAKER[idx]
            return (s_turned_a if who == "a" else s_turned_v), TAKER[:idx + 1].count(who)

        first_turn = {}
        last_turn = {}
        for n, (kind, m, g, c) in enumerate(TURNS):
            first_turn.setdefault((kind, m), n)
            last_turn[(kind, m)] = n

        def att_place(group):
            return mixT_at[:, group // 2, group % 2 * 512:(group % 2 + 1) * 512].rearrange("p (c n) -> p c n", c=4)

        block = ctx.enter_context(nc.Block())

        @block.sync
        def _(sp):
            sp.dma_start(cst, a["constants"]).then_inc(consts_in, 16)
            for t in range(TILES):
                sp.dma_start(x_all[:, t, :], a["x"][t * P:(t + 1) * P, :]).then_inc(x_in[t], 16)
            sp.dma_start(tabE[0:N_BUCKETS + 1, :], a["distances"]).then_inc(onehot_in, 16)
            for g, (c0, width) in enumerate(WGROUPS):
                if g == 0:
                    sp.wait_ge(bias_out, 16)
                if g >= 2:
                    sp.wait_ge(proj_done, group_end[g - 2])
                sp.dma_start(wb[:, g % 2, :, 0:width],
                             a["w_in"][:, c0:c0 + width].rearrange("(k p) n -> p k n", p=P)).then_inc(w_in_sem[g % 2], 16)
            sp.wait_ge(proj_done, len(STEPS))
            sp.wait_ge(bias_out, 16)
            for pair in range(AT_HEADS // 2):
                if pair >= 2:
                    sp.wait_ge(s_max, 2 * TILES * (pair - 1))
                src = bass.AP(tensor=bias_dram.tensor, offset=2 * pair * NREL, ap=[[1, P], [NREL, 2], [1, SEQ]])
                sp.dma_start(slab[:, pair % 2], src).then_inc(slab_in[pair % 2], 16)

            n_att = TILES * AT_HEADS
            sp.wait_ge(s_max, 3 * 2 * TILES)
            for k in range(KC):
                sp.dma_start(w_out[k], a["w_out"][k * P:(k + 1) * P, :]).then_inc(w_out_in, 16)
            sp.wait_ge(s_values, n_att)
            sp.wait_ge(s_turned_a, TAKER.count("a"))
            sp.wait_ge(s_turned_v, TAKER.count("v"))
            sp.dma_start(g_ffn, a["norm_ffn"]).then_inc(ffn_in, 16)
            sp.dma_start(router, a["router"].rearrange("(k p) n -> p k n", p=P)).then_inc(ffn_in, 16)
            for t in range(2):
                sp.dma_start(xs[:, t, :], a["x"][t * P:(t + 1) * P, :]).then_inc(xs_in[t], 16)
            sp.wait_ge(d_dve, len(DVE_ORDER))
            sp.wait_ge(d_pe, len(PE_ORDER))

            def load_weights(slot, u, expert):
                at_least(sp, gu_mm, slot - 1)
                for w, name in ((w_gate, "ex_gate"), (w_up, "ex_up")):
                    sp.dma_start(w[u], a[name][bass.ds(expert, 1), :, :].rearrange("e (k p) n -> p (e k) n", p=P))\
                      .then_inc(gu_in[u], 16)
                at_least(sp, down_mm, slot - 1)
                sp.dma_start(w_down[u], a["ex_down"][bass.ds(expert, 1), :, :].rearrange("e (k p) n -> p (e k) n", p=P))\
                  .then_inc(down_in[u], 16)

            load_weights(0, 0, 0)
            for t in range(TILES):
                sp.wait_ge(x2_done, t + 1)
                sp.dma_start(x2_dram[t * P:(t + 1) * P, :], xs[:, t % 2, :]).then_inc(x2_out[t % 2], 16)
                sp.wait_ge(h2_done, t + 1)
                sp.dma_start(h2_dram[t * P:(t + 1) * P, :], h2s[:, t % 2, :]).then_inc(h2_out[t % 2], 16)
                if t + 2 < TILES:
                    sp.wait_ge(x2_out[t % 2], 16 * (t // 2 + 1))
                    sp.wait_ge(x2_sq, t + 1)
                    sp.dma_start(xs[:, t % 2, :], a["x"][(t + 2) * P:(t + 3) * P, :]).then_inc(xs_in[t % 2], 16)
            sp.wait_ge(out_mm, TILES)
            load_weights(1, 1, 1)
            sp.wait_ge(slots_ready, 1)
            for u in range(2):
                sp.wait_ge(x2_out[u], 16 * TILES // 2)
            sp.dma_start(fx, x2_dram.rearrange("(t p) d -> p t d", p=P)).then_inc(x2_back, 16)
            with sp.Fori(1, EXPERTS // 2) as pair:
                for u in range(2):
                    load_weights(2 * pair + u, u, 2 * pair + u)
            sp.wait_ge(slots_ready, 1)
            more = sp.value_load(n_ov[0:1, 0:1], min_val=0, max_val=EXTRA)
            with sp.Fori(0, EXTRA // 2) as pair:
                for u in range(2):
                    with sp.If(more > 2 * pair + u):
                        expert = sp.value_load(ov_e[0:1, bass.ds(2 * pair + u, 1)], min_val=0, max_val=EXPERTS - 1)
                        load_weights(2 * pair + EXPERTS + u, u, expert)
            sp.wait_ge(y_all_out, 1)
            for t in range(TILES):
                for c in range(2):
                    sp.dma_start(fy[c][:, t, :], y_dram[c * SEQ + t * P:c * SEQ + (t + 1) * P, :]).then_inc(final_in[t], 16)
            for t in range(TILES):
                sp.wait_ge(final_v, t + 1)
                sp.dma_start(out[t * P:(t + 1) * P, :], fx[:, t, :]).then_inc(final_out, 16)
            sp.wait_ge(final_out, 16 * TILES)

        @block.tensor
        def _(pe):
            mm, tr = nc.tensor.matmul, nc.tensor.transpose
            pe.wait_ge(consts_in, 16)
            pe.wait_ge(params_in, 16)
            pe.wait_ge(onehot_in, 16)
            for c in range(3):
                last = mm(ps[0:AT_HEADS, 5 + c, 0:384], par[0:N_BUCKETS + 1, P_RB:P_RB + AT_HEADS],
                          tabE[0:N_BUCKETS + 1, c * 384:(c + 1) * 384], start=True, stop=True)
            last.then_inc(table_mm, 1)
            for t in range(TILES):
                pe.wait_ge(h_scaled, t + 1)
                if t >= 2:
                    pe.wait_ge(hT_done, 2 * (t - 1))
                for half in range(2):
                    for c in range(4):
                        k = 4 * half + c
                        last = tr(ps[:, 2 * (t % 2) + half, c * P:(c + 1) * P], x_all[:, t, k * P:(k + 1) * P], ident)
                    last.then_inc(hT_turned, 1)
            pe.wait_ge(hT_done, 2 * TILES)

            def turn_qk(j):
                pe.wait_ge(qk_normed, j + 1)
                if j >= 2:
                    pe.wait_ge(qk_out, j - 1)
                for c in range(4):
                    last = tr(ps[:, 4 + j % 2, c * P:(c + 1) * P], stage[:, j % 2, c * P:(c + 1) * P], ident)
                last.then_inc(qk_turned, 1)

            group = -1
            for n, (g, kind, c, m) in enumerate(STEPS):
                if g != group:
                    group = g
                    pe.wait_ge(w_in_sem[g % 2], 16 * (g // 2 + 1))
                if n >= 4:
                    pe.wait_ge(*act_taken(n - 4))
                bank = n % 4
                w = wb[:, g % 2]
                for k in range(KC):
                    f = dict(start=(k == 0), stop=(k == KC - 1))
                    if kind in ("gate", "glu", "dn"):
                        col = {"gate": 2 + c, "glu": c, "dn": c % 4}[kind] * P
                        last = mm(ps[:, bank, :], w[:, k, col:col + P], hT[:, k, m * 512:(m + 1) * 512], **f)
                    elif kind == "z":
                        last = mm(ps[:, bank, 0:264], hT[:, k, m * P:(m + 1) * P], w[:, k, 256:520], **f)
                    else:
                        last = mm(ps[:, bank, :], hT[:, k, m * P:(m + 1) * P], w[:, k, 0:512], **f)
                last.then_inc(proj_done, 1)
                if n == 19:
                    pe.wait_ge(tap_done, 2 * CV_TAPS)
                    for half in range(2):
                        for c2 in range(2):
                            last = mm(ps[:, 6 + half, :], ones, yc[:, c2, half * 512:(half + 1) * 512],
                                      start=(c2 == 0), stop=(c2 == 1))
                    last.then_inc(cv_mean, 1)
                if n == 22:
                    pe.wait_ge(cv_squared, 2)
                    for half in range(2):
                        for c2 in range(2):
                            last = mm(ps[:, 6 + half, :], ones, ypad[:, c2, half * 512:(half + 1) * 512],
                                      start=(c2 == 0), stop=(c2 == 1))
                    last.then_inc(cv_var, 1)
                if n > FIRST_QK and n - FIRST_QK - 1 < 16:
                    turn_qk(n - FIRST_QK - 1)
            pe.wait_ge(gate_v, 4)
            pe.wait_ge(cv_varsb, 1)
            mm(ps[:, 6, 0:32], tri, g_col, start=True, stop=True)
            mm(ps[:, 6, 32:64], ones, g_col, start=True, stop=True).then_inc(cv_mean, 1)

            D0, D1, D2, PV, TB = 0, 1, 2, 3, 4

            def dn(i, k):
                if k >= len(DN_PIECES):
                    return
                piece = DN_PIECES[k]
                if piece == "split":
                    if i == 0:
                        pe.wait_ge(dn_silu, 6)
                        pe.wait_ge(act_took, len(STEPS) - 4)
                        pe.wait_ge(gate_a, 5)
                    else:
                        pe.wait_ge(d_dve, dve_at(i - 1, "y3"))
                    for c in range(6):
                        last = tr(ps[:, c // 4, (c % 4) * P:(c % 4 + 1) * P], dconv[:, c, i * P:(i + 1) * P], ident)
                    last.then_inc(d_pe, 1)
                    pe.wait_ge(d_pool, pool_at(i, "tg"))
                    if i:
                        pe.wait_ge(d_act, act_at(i - 1, "x4"))
                    mm(ps[:, D2, :], ones, Tg.rearrange("p h n -> p (h n)"), start=True, stop=False)
                    for h in range(4):
                        last = mm(ps[:, D2, h * P:(h + 1) * P], ident, negm, start=False, stop=(h == 3))
                    last.then_inc(d_pe, 1)
                elif piece == "norm":
                    pe.wait_ge(d_dve, dve_at(i, "qkn"))
                    pe.wait_ge(d_pool, pool_at(i, "kb"))
                    if i:
                        pe.wait_ge(d_dve, dve_at(i - 1, "y5"))
                    for pair in range(2):
                        cols = slice(pair * P, (pair + 1) * P)
                        for m, src in enumerate((kb[:, cols], tok[:, cols], tok[:, DN_W + pair * P:DN_W + (pair + 1) * P])):
                            last = tr(ps[:, pair, m * P:(m + 1) * P], src, ident)
                    last.then_inc(d_pe, 1)
                elif piece == "gram":
                    pe.wait_ge(d_act, act_at(i, "norm"))
                    for h in range(4):
                        rows = slice(HD * (h % 2), HD * (h % 2) + HD)
                        last = mm(ps[:, h % 2, (h // 2) * 256:(h // 2) * 256 + 256], tT[i % 2][rows, h // 2, 2, :],
                                  tT[i % 2][rows, h // 2, 0:2, :], start=True, stop=True)
                    last.then_inc(d_pe, 1)
                elif piece == "inv1":
                    pe.wait_ge(d_pool, pool_at(i, "am0"))
                    pe.wait_ge(d_act, act_at(i, "decay"))
                    if i:
                        pe.wait_ge(d_act, act_at(i - 1, "x6"))
                    for h in range(4):
                        last = tr(ps[:, D2, h * P:(h + 1) * P], AM[:, 0, h, :], ident)
                    last.then_inc(d_pe, 1)
                elif piece[0] == "x":
                    lv = int(piece[1:])
                    pe.wait_ge(d_pool, pool_at(i, f"am{lv}"))
                    pe.wait_ge(d_dve, dve_at(i, f"y{lv - 1}" if lv > 1 else "inv1"))
                    if lv == 1 and i:
                        pe.wait_ge(d_dve, dve_at(i - 1, "carry"))
                    if lv == 4 and i:
                        pe.wait_ge(d_act, act_at(i - 1, "out"))
                    if lv == 5 and i + 1 < TILES:
                        pe.wait_ge(d_act, act_at(i + 1, "decay"))
                    for h in range(4):
                        last = mm(ps[:, D2, h * P:(h + 1) * P], AM[:, lv % 2, h, :], T[:, h, :], start=True, stop=True)
                    last.then_inc(d_pe, 1)
                elif piece[0] == "y":
                    lv = int(piece[1:])
                    pe.wait_ge(d_act, act_at(i, f"x{lv}"))
                    if lv == 1 and i:
                        pe.wait_ge(d_act, act_at(i - 1, "fresh"))
                        pe.wait_ge(d_dve, dve_at(i - 1, "y6"))
                    if lv == 2 and i:
                        pe.wait_ge(d_dve, dve_at(i - 1, "emit"))
                    if lv == 4 and i + 1 < TILES:
                        pe.wait_ge(d_act, act_at(i + 1, "split"))
                    if lv == 6 and i + 1 < TILES:
                        pe.wait_ge(d_dve, dve_at(i + 1, "gram"))
                    for h in range(4):
                        if lv < LEVELS - 1:
                            mm(ps[:, D0, h * P:(h + 1) * P], Tt[i % 2][:, h, :], Xs[:, h, :], start=True, stop=True)
                    for h in range(4):
                        last = mm(ps[:, D1, h * P:(h + 1) * P], Xs[:, h, :], Tt[i % 2][:, h, :], start=True, stop=True)
                    last.then_inc(d_pe, 1)
                elif piece == "carry":
                    if i:
                        pe.wait_ge(d_dve, dve_at(i - 1, "emit"))
                    else:
                        pe.wait_ge(pads_zero, 2)
                    if i + 1 < TILES:
                        pe.wait_ge(d_dve, dve_at(i + 1, "inv1"))
                    for m in range(2):
                        for pair in range(2):
                            last = mm(ps[:, D2, m * 256 + pair * P:m * 256 + (pair + 1) * P], tT[i % 2][:, pair, m, :],
                                      Sst[:, pair, :], start=True, stop=True)
                    last.then_inc(d_pe, 1)
                elif piece == "fresh":
                    pe.wait_ge(d_dve, dve_at(i, "carry"))
                    if i + 1 < TILES:
                        pe.wait_ge(d_dve, dve_at(i + 1, "gram"))
                    for h in range(4):
                        last = mm(ps[:, D0, h * HD:(h + 1) * HD], Tt[i % 2][:, h, :], R[:, h * HD:(h + 1) * HD],
                                  start=True, stop=True)
                    last.then_inc(d_pe, 1)
                elif piece == "emit":
                    pe.wait_ge(d_act, act_at(i, "fresh"))
                    pe.wait_ge(d_pool, pool_at(i, "kdvb"))
                    if i + 1 < TILES:
                        pe.wait_ge(d_dve, dve_at(i + 1, "y1"))
                    for h in range(4):
                        mm(ps[:, D1, h * HD:(h + 1) * HD], qkD[i % 2][:, h, :], vn[:, h * HD:(h + 1) * HD], start=True, stop=True)
                    for pair in range(2):
                        cols = slice(pair * P, (pair + 1) * P)
                        last = mm(ps[:, D0, pair * P:(pair + 1) * P], kd[i % 2][:, cols], vn[:, cols], start=True, stop=True)
                    last.then_inc(d_pe, 1)
                elif piece == "out":
                    pe.wait_ge(d_dve, dve_at(i, "onorm"))
                    if i + 1 < TILES:
                        pe.wait_ge(d_act, act_at(i + 1, "x3"))
                    for pair in range(2):
                        last = tr(ps[:, D2, pair * P:(pair + 1) * P], o1[:, pair * P:(pair + 1) * P], ident)
                    last.then_inc(d_pe, 1)

            pe.wait_ge(qk_out, 16)
            pe.wait_ge(act_took, len(STEPS) - 4)
            pe.wait_ge(gate_a, 5)
            idx = 0
            for ev in SCHEDULE:
                if ev[0] == "scores":
                    n = ev[1]
                    pair, i, hh = attention_step(n)
                    rows = slice(HD * hh, HD * hh + HD)
                    pe.wait_ge(s_max, n)
                    for c0 in range(0, (i + 1) * P, 512):
                        w = min(512, (i + 1) * P - c0)
                        last = mm(ps[:, 6 + c0 // 512, 0:w], qkT[rows, 0, pair, i * P:(i + 1) * P],
                                  qkT[rows, 1, pair, c0:c0 + w], start=True, stop=True)
                    last.then_inc(s_scores, 1)
                elif ev[0] == "dn":
                    dn(ev[1], ev[2])
                elif ev[0] == "turn":
                    n = ev[1]
                    pe.wait_ge(s_exp, n + 1)
                    for g, cnt in turn_groups(n):
                        if idx >= 2:
                            pe.wait_ge(*taken(idx - 2))
                        for c in range(cnt):
                            last = tr(ps[:, TB + idx % 2, c * P:(c + 1) * P], prob[:, n % 2, (g + c) * P:(g + c + 1) * P], ident)
                        last.then_inc(s_turn, 1)
                        idx += 1
                elif ev[0] == "values":
                    n = ev[1]
                    pair, i, hh = attention_step(n)
                    if n % 8 == 0 and n:
                        pe.wait_ge(s_att, n // 8)
                    for who in range(first_turn[("p", n)], last_turn[("p", n)] + 1):
                        pe.wait_ge(*taken(who))
                    for b in range(i + 1):
                        last = mm(ps[:, PV, n % 8 * HD:(n % 8 + 1) * HD], probT[:, n % 2, b * P:(b + 1) * P],
                                  v_tok[:, b, pair * P + hh * HD:pair * P + (hh + 1) * HD], start=(b == 0), stop=(b == i))
                    last.then_inc(s_values, 1)
                else:
                    i = ev[1]
                    pe.wait_ge(s_att, i + 1)
                    pe.wait_ge(*taken(idx - 2))
                    for c in range(4):
                        last = tr(ps[:, TB + idx % 2, c * P:(c + 1) * P], att[:, c * P:(c + 1) * P], ident)
                    last.then_inc(s_turn, 1)
                    idx += 1

            pe.wait_ge(w_out_in, 16 * KC)
            pe.wait_ge(ffn_in, 32)
            pe.wait_ge(d_act, len(ACT_ORDER))
            pe.wait_ge(cv_out, 2)

            def logits_of(t):
                pe.wait_ge(h2_done, t + 1)
                if t:
                    pe.wait_ge(h2T_done, t)
                for k in range(KC):
                    last = tr(ps[:, 4 + k // 4, (k % 4) * P:(k % 4 + 1) * P], h2s[:, t % 2, k * P:(k + 1) * P], ident)
                last.then_inc(h2_turned, 1)
                pe.wait_ge(h2T_done, t + 1)
                if t:
                    pe.wait_ge(logit_sb, t)
                for k in range(KC):
                    last = mm(ps[:, 6, 0:36], h2T[:, t % 2, k, :], router[:, k, :], start=(k == 0), stop=(k == KC - 1))
                last.then_inc(logit_mm, 1)

            mixT = [mixT_dn[:, 0], mixT_dn[:, 1]] + [mixT_at[:, c] for c in range(4)] + [mixT_cv[:, 0], mixT_cv[:, 1]]
            for t in range(TILES):
                if t >= 2:
                    pe.wait_ge(x2_done, t - 1)
                for half in range(2):
                    for k in range(KC):
                        last = mm(ps[:, 2 * (t % 2) + half, :], mixT[k][:, t * P:(t + 1) * P],
                                  w_out[k][:, half * 512:(half + 1) * 512], start=(k == 0), stop=(k == KC - 1))
                last.then_inc(out_mm, 1)
                if t:
                    logits_of(t - 1)
            logits_of(TILES - 1)
            pe.wait_ge(route_v, 3)
            flat = lambda x: x.rearrange("p t e -> p (t e)")
            mm(ps[:, 7, 0:256], tri, flat(hots), start=True, stop=False)
            mm(ps[:, 7, 0:256], ones, flat(before), start=False, stop=True)
            mm(ps[:, 7, 256:288], ones, hots[:, TILES - 1, :], start=True, stop=False)
            mm(ps[:, 7, 256:288], ones, before[:, TILES - 1, :], start=False, stop=True).then_inc(rank_mm, 1)
            for m in range(2 * TILES):
                pe.wait_ge(list_v, m + 1)
                mm(ps[:, 6, 0:256], r_hot[:, m % 2, :], r_val[:, m % 2, :], start=(m == 0), stop=(m == 2 * TILES - 1))\
                    .then_inc(list_mm, 1)

            def turn_rows(slot, u, pair):
                pe.wait_ge(rows_in[u], 16 * (pair + 1))
                at_least(pe, rowsT_a, slot)
                at_least(pe, rowsT_v, slot)
                for k in range(KC):
                    last = tr(ps[:, k // 4, (k % 4) * P:(k % 4 + 1) * P], hg[:, u, k * P:(k + 1) * P], ident)
                last.then_inc(rows_turned, 1)

            def gate_up(slot, u, pair):
                pe.wait_ge(rowsT_a, slot + 1)
                pe.wait_ge(rowsT_v, slot + 1)
                pe.wait_ge(gu_in[u], 32 * (pair + 1))
                at_least(pe, act_done, slot)
                for k in range(KC):
                    mm(ps[:, 2, :], hgT[:, u, k, :], w_gate[u][:, k, :], start=(k == 0), stop=(k == KC - 1))
                for k in range(KC):
                    last = mm(ps[:, 3, :], hgT[:, u, k, :], w_up[u][:, k, :], start=(k == 0), stop=(k == KC - 1))
                last.then_inc(gu_mm, 1)

            def turn_act(slot):
                pe.wait_ge(act_done, slot + 1)
                at_least(pe, actT_done, slot)
                for k in range(FC):
                    last = tr(ps[:, 4, k * P:(k + 1) * P], act_g[:, k * P:(k + 1) * P], ident)
                last.then_inc(act_turned, 1)

            def down(slot, u, pair):
                pe.wait_ge(actT_done, slot + 1)
                pe.wait_ge(down_in[u], 16 * (pair + 1))
                at_least(pe, y_a, slot)
                at_least(pe, y_v, slot)
                for half in range(2):
                    for k in range(FC):
                        last = mm(ps[:, 5 + half, :], actT[:, k, :], w_down[u][:, k, half * 512:(half + 1) * 512],
                                  start=(k == 0), stop=(k == FC - 1))
                last.then_inc(down_mm, 1)

            def expert(slot, u, pair):
                gate_up(slot, u, pair)
                turn_rows(slot + 1, 1 - u, pair + u)
                if not (isinstance(slot, int) and slot == 0):
                    down(slot - 1, 1 - u, pair + u - 1)
                turn_act(slot)

            pe.wait_ge(slots_ready, 1)
            turn_rows(0, 0, 0)
            experts_loop(pe, expert)
            extras_loop(pe, expert, down)

        @block.vector
        def _(v):
            tt, ts, stt = nc.vector.tensor_tensor, nc.vector.tensor_scalar, nc.vector.scalar_tensor_tensor
            nc.vector.memset(ypad[:, :, 0:30], 0.0)
            nc.vector.memset(dpad[:, :, 0:3], 0.0).then_inc(pads_zero, 1)

            def take_hT(t):
                for half in range(2):
                    v.wait_ge(hT_turned, 2 * t + half + 1)
                    k0 = 4 * half
                    tt(hT[:, k0:k0 + 4, t * P:(t + 1) * P], ps[:, 2 * (t % 2) + half, :].rearrange("p (k n) -> p k n", k=4),
                       bc_h(par[:, P_GMIX + k0:P_GMIX + k0 + 4], P), ALU.mult).then_inc(hT_done, 1)

            v.wait_ge(params_in, 16)
            v.wait_ge(consts_in, 16)
            for t in range(TILES):
                v.wait_ge(rms_done, t + 1)
                ts(x_all[:, t, :], x_all[:, t, :], rs[:, t:t + 1], None, ALU.mult).then_inc(h_scaled, 1)
                if t:
                    take_hT(t - 1)
            take_hT(TILES - 1)

            for n, (g, kind, c, m) in enumerate(STEPS):
                if kind == "glu":
                    v.wait_ge(proj_done, n + 1)
                    v.wait_ge(act_took, 4)
                    tt(ypad[:, c, 30 + m * 512:30 + (m + 1) * 512], ps[:, n % 4, :], yc[:, c, m * 512:(m + 1) * 512],
                       ALU.mult).then_inc(dve_took, 1)
            v.wait_ge(dve_took, 4)
            for c in range(2):
                ts(yc[:, c, :], ypad[:, c, 0:SEQ], par[:, P_CVW + c * CV_TAPS:P_CVW + c * CV_TAPS + 1],
                   par[:, P_CVB + c:P_CVB + c + 1], ALU.mult, ALU.add).then_inc(tap_done, 1)
            for tap in range(1, CV_TAPS):
                for c in range(2):
                    v.wait_ge(tap_done, 2 * tap + c - 1)
                    col = P_CVW + c * CV_TAPS + tap
                    stt(yc[:, c, :], ypad[:, c, tap:tap + SEQ], par[:, col:col + 1], yc[:, c, :],
                        ALU.mult, ALU.add).then_inc(tap_done, 1)
            v.wait_ge(cv_mean, 1)
            for half in range(2):
                for c in range(2):
                    seg = yc[:, c, half * 512:(half + 1) * 512]
                    last = stt(seg, ps[:, 6 + half, :], -1.0 / CV_W, seg, ALU.mult, ALU.add)
            last.then_inc(cv_centred, 1)

            def dn_conv(c):
                v.wait_ge(*act_taken(8 + 2 * c + 1))
                w0 = P_DNW + c * DN_TAPS
                ts(dconv[:, c, :], dpad[:, c, 0:SEQ], par[:, w0:w0 + 1], None, ALU.mult)
                for tap in range(1, DN_TAPS):
                    nc.vector.drain()
                    last = stt(dconv[:, c, :], dpad[:, c, tap:tap + SEQ], par[:, w0 + tap:w0 + tap + 1], dconv[:, c, :],
                               ALU.mult, ALU.add)
                last.then_inc(dn_tapped, 1)

            dn_conv(0)
            dn_conv(1)
            v.wait_ge(cv_var, 1)
            for half in range(2):
                ts(junk[:, half * 512:(half + 1) * 512], ps[:, 6 + half, :], 1.0 / CV_W, EPS, ALU.mult, ALU.add)
            nc.vector.drain()
            nc.vector.reciprocal(junk, junk).then_inc(cv_varsb, 1)
            for c in range(2, 6):
                dn_conv(c)
            v.wait_ge(cv_rstd, 1)
            tt(yc, yc, bc_f(junk, 2), ALU.mult).then_inc(cv_normed, 1)
            v.wait_ge(act_took, 4 + 8 + 4 + 8)
            tt(zg.rearrange("p t (h d) -> p (t h) d", d=HD), zg.rearrange("p t (h d) -> p (t h) d", d=HD),
               bc_f(par[:, P_ON:P_ON + HD], TILES * DN_HEADS), ALU.mult).then_inc(zg_done, 1)
            for j in range(16):
                v.wait_ge(qk_sq, j + 1)
                nc.vector.tensor_reduce(ss2[:, j % 2, :], sqb.rearrange("p (h d) -> p h d", d=HD), AX.X, ALU.add)
                nc.vector.drain()
                if j < 8:
                    ts(ss2[:, j % 2, :], ss2[:, j % 2, :], HD * EPS, None, ALU.add).then_inc(qk_ss, 1)
                else:
                    ts(ss2[:, j % 2, :], ss2[:, j % 2, :], 1.0 / HD, EPS, ALU.mult, ALU.add).then_inc(qk_ss, 1)
                v.wait_ge(qk_rs, j + 1)
                s3 = stage[:, j % 2, :].rearrange("p (h d) -> p h d", d=HD)
                tt(s3, s3, bc_h(rs2[:, j % 2, :]), ALU.mult).then_inc(qk_normed, 1)
            a8 = ab[:, :, 0:4]
            b8 = ab[:, :, 4:8]
            g3, beta3, t13, t23, t33 = (x.rearrange("p (t h) -> p t h", h=4) for x in (g_col, beta, t1, t2, t3))
            tt(t13, a8, bc_f(par[:, P_DT:P_DT + 4], TILES), ALU.add)
            nc.vector.drain()
            stt(t23, t13, -1.0, t13, ALU.mult, ALU.min)
            v.wait_ge(act_took, 4 + 8 + 4 + 8)
            nc.vector.tensor_copy(t33, b8)
            nc.vector.drain().then_inc(gate_v, 1)
            v.wait_ge(gate_a, 2)
            stt(t13, t13, 0.0, t23, ALU.max, ALU.add)
            ts(t3, t3, 1.0, None, ALU.add)
            nc.vector.drain().then_inc(gate_v, 1)
            nc.vector.reciprocal(beta, t3)
            stt(g3, t13, -1.0, bc_f(ea, TILES), ALU.mult, ALU.mult)
            nc.vector.drain().then_inc(gate_v, 2)
            v.wait_ge(cv_mean, 2)
            nc.vector.tensor_copy(Gc, ps[:, 6, 0:32])
            nc.vector.tensor_copy(Gtot, ps[:, 6, 32:64])
            nc.vector.drain()
            tt(ekd, Gtot, Gc, ALU.subtract)
            ts(negG, Gc, -1.0, None, ALU.mult)
            nc.vector.drain().then_inc(gate_v, 1)
            v.wait_ge(gate_a, 5)
            e3 = egl_all.rearrange("p (t c two) -> p t c two", two=2, c=2)
            nc.vector.tensor_copy(egl[0:HD], e3[0:HD, :, :, 0])
            nc.vector.tensor_copy(egl[HD:P], e3[HD:P, :, :, 1])
            nc.vector.memset(Sst, 0.0)
            nc.vector.drain().then_inc(pads_zero, 1)

            def dn(i, k):
                if k >= len(DN_PIECES):
                    return
                piece = DN_PIECES[k]
                ti = slice(4 * i, 4 * i + 4)
                if piece == "ss":
                    v.wait_ge(d_pool, pool_at(i, "sq"))
                    nc.vector.tensor_reduce(dss, dsq.rearrange("p (h d) -> p h d", d=HD), AX.X, ALU.add)
                    nc.vector.drain()
                    ts(dss[:, 4:8], dss[:, 4:8], EPS, None, ALU.add)
                    ts(dss[:, 0:4], dss[:, 0:4], EPS, float(HD), ALU.add, ALU.mult)
                    nc.vector.drain().then_inc(d_dve, 1)
                elif piece == "qkn":
                    v.wait_ge(d_pool, pool_at(i, "rs"))
                    t8 = tok[:, 0:512].rearrange("p (h d) -> p h d", d=HD)
                    tt(t8, t8, bc_h(drs), ALU.mult).then_inc(d_dve, 1)
                elif piece == "gram":
                    v.wait_ge(d_pe, pe_at(i, "gram"))
                    v.wait_ge(d_act, act_at(i, "decay"))
                    if i:
                        v.wait_ge(d_pool, pool_at(i - 1, f"am{LEVELS - 1}"))
                    both = ps[:, 0:2, :].rearrange("p b (c m n) -> p b c m n", m=2, n=P)
                    of_bank = lambda x: x.rearrange("p (c b) n -> p b c n", b=2)
                    tt(of_bank(At), both[:, :, :, 0, :], of_bank(dI), ALU.mult)
                    tt(of_bank(qkD[i % 2]), both[:, :, :, 1, :], of_bank(dI), ALU.mult)
                    nc.vector.drain().then_inc(d_dve, 1)
                elif piece == "inv1":
                    v.wait_ge(d_pe, pe_at(i, "inv1"))
                    tt(T, bc_f(ident, 4), ps[:, 2, :].rearrange("p (h n) -> p h n", h=4), ALU.subtract)
                    tt(Tt[i % 2], bc_f(ident, 4), AM[:, 0], ALU.subtract)
                    nc.vector.drain().then_inc(d_dve, 1)
                elif piece[0] == "y":
                    lv = int(piece[1:])
                    v.wait_ge(d_pe, pe_at(i, piece))
                    if lv < LEVELS - 1:
                        tt(T, T, ps[:, 0, :].rearrange("p (h n) -> p h n", h=4), ALU.subtract)
                    tt(Tt[i % 2], Tt[i % 2], ps[:, 1, :].rearrange("p (h n) -> p h n", h=4), ALU.subtract)
                    nc.vector.drain().then_inc(d_dve, 1)
                elif piece == "carry":
                    v.wait_ge(d_pe, pe_at(i, "carry"))
                    v.wait_ge(d_pool, pool_at(i, "kdvb"))
                    h4 = lambda x: x.rearrange("p (h d) -> p h d", d=HD)
                    tt(h4(tmp), h4(ps[:, 2, 0:256]), bc_h(eG[:, ti]), ALU.mult)
                    tt(h4(o1), h4(ps[:, 2, 256:512]), bc_h(eG[:, ti]), ALU.mult)
                    nc.vector.drain()
                    tt(R, vb[i % 2], tmp, ALU.subtract).then_inc(d_dve, 1)
                elif piece == "emit":
                    v.wait_ge(d_pe, pe_at(i, "emit"))
                    tt(tmp.rearrange("p (c n) -> p c n", c=2), ps[:, 0, 0:256].rearrange("p (c n) -> p c n", c=2),
                       bc_f(bd, 2), ALU.mult)
                    tt(o1, ps[:, 1, 0:256], o1, ALU.add)
                    nc.vector.drain()
                    for pair in range(2):
                        stt(Sst[:, pair, :], Sst[:, pair, :], egl[:, i, pair:pair + 1], tmp[:, pair * P:(pair + 1) * P],
                            ALU.mult, ALU.add)
                    nc.vector.drain().then_inc(d_dve, 1)
                elif piece == "osum":
                    v.wait_ge(d_pool, pool_at(i, "osq"))
                    nc.vector.tensor_reduce(dss[:, 0:4], dsq[:, 0:256].rearrange("p (h d) -> p h d", d=HD), AX.X, ALU.add)
                    nc.vector.drain()
                    ts(dss[:, 0:4], dss[:, 0:4], 1.0 / HD, EPS, ALU.mult, ALU.add).then_inc(d_dve, 1)
                    tt(o1, o1, zg[:, i, :], ALU.mult)
                elif piece == "onorm":
                    nc.vector.drain()
                    v.wait_ge(d_pool, pool_at(i, "ors"))
                    o3 = o1.rearrange("p (h d) -> p h d", d=HD)
                    tt(o3, o3, bc_h(drs[:, 0:4]), ALU.mult).then_inc(d_dve, 1)

            v.wait_ge(proj_done, len(STEPS))
            v.wait_ge(qk_turned, 16)
            idx = 0
            for ev in SCHEDULE:
                if ev[0] == "scores":
                    n = ev[1]
                    pair, i, hh = attention_step(n)
                    L = (i + 1) * P
                    v.wait_ge(slab_in[pair % 2], 16 * (pair // 2 + 1))
                    v.wait_ge(s_scores, n + 1)
                    if n >= 2:
                        v.wait_ge(s_turn, first_turn[("p", n - 1)])
                        v.wait_ge(s_exp, n - 1)
                    scores = ps[:, 6:8, :].rearrange("p b n -> p (b n)")[:, 0:L]
                    nc.vector.tensor_tensor_reduce(prob[:, n % 2, 0:L], scores, slab[:, pair % 2, hh, 896 - i * P:896 - i * P + L],
                                                   1.0, -3e38, ALU.add, ALU.max, mx[:, n % 2:n % 2 + 1])
                    nc.vector.drain()
                    ts(nmx[:, n % 2:n % 2 + 1], mx[:, n % 2:n % 2 + 1], -1.0, None, ALU.mult).then_inc(s_max, 1)
                elif ev[0] == "dn":
                    dn(ev[1], ev[2])
                elif ev[0] == "turn":
                    n = ev[1]
                    for g, cnt in turn_groups(n):
                        if TAKER[idx] == "v":
                            v.wait_ge(s_turn, idx + 1)
                            if n >= 2:
                                v.wait_ge(s_values, n - 1)
                            nc.vector.tensor_copy(probT[:, n % 2, g * P:(g + cnt) * P], ps[:, 4 + idx % 2, 0:cnt * P])\
                                .then_inc(s_turned_v, 1)
                        idx += 1
                elif ev[0] == "values":
                    n = ev[1]
                    if n % 8 == 7:
                        v.wait_ge(s_values, n + 1)
                        v.wait_ge(s_exp, n + 1)
                        if n > 8:
                            v.wait_ge(s_turn, first_turn[("o", n // 8 - 1)] + 1)
                        nc.vector.reciprocal(rZ, Z[:, n // 8 % 2, :])
                        nc.vector.drain()
                        tt(att.rearrange("p (h d) -> p h d", d=HD), ps[:, 3, :].rearrange("p (h d) -> p h d", d=HD),
                           bc_h(rZ), ALU.mult).then_inc(s_att, 1)
                else:
                    i = ev[1]
                    if TAKER[idx] == "v":
                        v.wait_ge(s_turn, idx + 1)
                        nc.vector.tensor_copy(att_place(i), flipped(ps[:, 4 + idx % 2, :].rearrange("p (c n) -> p c n", c=4)))\
                            .then_inc(s_turned_v, 1)
                    idx += 1

            v.wait_ge(ffn_in, 32)
            v.wait_ge(params_in, 16)

            def residual(t):
                v.wait_ge(out_mm, t + 1)
                v.wait_ge(xs_in[t % 2], 16 * (t // 2 + 1))
                tt(xs[:, t % 2, :], ps[:, 2 * (t % 2):2 * (t % 2) + 2, :].rearrange("p b n -> p (b n)"), xs[:, t % 2, :],
                   ALU.add).then_inc(x2_done, 1)

            def gained(t):
                v.wait_ge(x2_rs, t + 1)
                if t >= 2:
                    v.wait_ge(h2_turned, t - 1)
                    v.wait_ge(h2_out[t % 2], 16 * (t // 2))
                stt(h2s[:, t % 2, :], xs[:, t % 2, :], rs[:, t:t + 1], g_ffn, ALU.mult, ALU.mult).then_inc(h2_done, 1)

            def logits_out(t):
                v.wait_ge(logit_mm, t + 1)
                tt(logits[:, t, :], ps[:, 6, 0:36], par[:, P_RBIAS:P_RBIAS + 36], ALU.add).then_inc(logit_sb, 1)

            for t in range(TILES):
                residual(t)
                gained(t)
                if t:
                    logits_out(t - 1)
            logits_out(TILES - 1)
            v.wait_ge(out_mm, TILES)
            glog = logits[:, :, 0:4]
            nc.vector.memset(padded, -3e38)
            nc.vector.memset(zero256, 0.0)
            nc.vector.drain()
            nc.vector.tensor_copy(padded[:, :, 0:4], glog)
            nc.vector.drain()
            for t in range(TILES):
                nc.vector.max(gtop[:, t, :], padded[:, t, :])
            nc.vector.drain()
            for t in range(TILES):
                nc.vector.max_index(gtop_i[:, t, :], gtop[:, t, :], padded[:, t, :])
            tt(gexp, glog, gtop[:, :, 0:1].to_broadcast([P, TILES, 4]), ALU.subtract)
            nc.vector.drain().then_inc(route_v, 1)
            nc.vector.tensor_copy(g_idx, gtop_i[:, :, 0])
            nc.vector.drain()
            tt(g_hot, bc_f(cst[:, C_J:C_J + 4], TILES), bc_h(g_idx, 4), ALU.is_equal)
            nc.vector.drain()
            ts(g_hot, g_hot, -1.0, -NEG, ALU.add, ALU.mult)
            nc.vector.drain()
            tt(em.rearrange("p t (g e) -> p t g e", g=4), logits[:, :, 4:36].rearrange("p t (g e) -> p t g e", g=4),
               g_hot.unsqueeze(3).to_broadcast([P, TILES, 4, 8]), ALU.add)
            nc.vector.drain()
            for t in range(TILES):
                nc.vector.max(etop[:, t, :], em[:, t, :])
            nc.vector.drain()
            for t in range(TILES):
                nc.vector.max_index(etop_i[:, t, :], etop[:, t, :], em[:, t, :])
            tt(e_diff, etop[:, :, 1], etop[:, :, 0], ALU.subtract)
            nc.vector.drain().then_inc(route_v, 1)
            nc.vector.tensor_copy(e_idx.rearrange("p c t -> p t c"), etop_i[:, :, 0:2])
            nc.vector.drain()
            for c in range(2):
                tt(hot[:, c], bc_f(cst[:, C_E:C_E + EXPERTS], TILES), bc_h(e_idx[:, c, :], EXPERTS), ALU.is_equal)
            nc.vector.drain()
            tt(hots, hot[:, 0], hot[:, 1], ALU.add)
            nc.vector.memset(before[:, 0, :], 0.0)
            for t in range(1, TILES):
                nc.vector.drain()
                tt(before[:, t, :], before[:, t - 1, :], hots[:, t - 1, :], ALU.add)
            nc.vector.drain().then_inc(route_v, 1)
            v.wait_ge(route_a, 2)
            nc.vector.tensor_reduce(p_grp, gexp, AX.X, ALU.add)
            ts(gates[:, 0, :], e_diff, 1.0, None, ALU.add)
            nc.vector.drain()
            tt(gates[:, 0, :], gates[:, 0, :], p_grp, ALU.mult)
            nc.vector.drain()
            nc.vector.reciprocal(gates[:, 0, :], gates[:, 0, :])
            nc.vector.drain()
            tt(gates[:, 1, :], gates[:, 0, :], e_diff, ALU.mult)
            v.wait_ge(rank_mm, 1)
            nc.vector.tensor_copy(rank.rearrange("p t e -> p (t e)"), ps[:, 7, 0:256])
            nc.vector.tensor_copy(e_count, ps[:, 7, 256:288])
            nc.vector.drain()
            for c in range(2):
                tt(rtmp, rank, hot[:, c], ALU.mult)
                nc.vector.drain()
                nc.vector.tensor_reduce(rk_k[:, c, :], rtmp, AX.X, ALU.add)
                nc.vector.drain()
            ts(rk_k, rk_k, -1.0, None, ALU.add)
            nc.vector.drain()
            for c in range(2):
                tt(jhot[:, c], bc_h(rk_k[:, c, :], 8), bc_f(cst[:, C_J128:C_J128 + 8], TILES), ALU.is_ge)
            nc.vector.drain()
            nc.vector.tensor_reduce(jn, jhot, AX.X, ALU.add)
            nc.vector.drain()
            ts(jn, jn, -1.0, None, ALU.add)
            nc.vector.drain()
            stt(rmod, jn, -float(P), rk_k, ALU.mult, ALU.add)
            for c in range(2):
                tt(jhot[:, c], bc_h(jn[:, c, :], 8), bc_f(cst[:, C_J:C_J + 8], TILES), ALU.is_equal)
            nc.vector.drain()
            for c in range(2):
                stt(jhot[:, c], bc_h(cst[:, C_TOK:C_TOK + TILES], 8), float(c * SEQ + 1), jhot[:, c], ALU.add, ALU.mult)
            nc.vector.drain()
            for m in range(2 * TILES):
                t, c = divmod(m, 2)
                if m >= 2:
                    v.wait_ge(list_mm, m - 1)
                ts(r_hot[:, m % 2, :], cst[:, C_IOTA:C_IOTA + P], rmod[:, c, t:t + 1], None, ALU.is_equal)
                tt(r_val[:, m % 2, :].rearrange("p (e j) -> p e j", j=8), bc_h(hot[:, c, t, :], 8),
                   bc_f(jhot[:, c, t, :], EXPERTS), ALU.mult)
                nc.vector.drain().then_inc(list_v, 1)
            tt(active.rearrange("p (e j) -> p e j", j=8), bc_h(e_count, 8), bc_f(cst[:, C_THR:C_THR + 8], EXPERTS), ALU.is_gt)
            nc.vector.drain()
            nc.vector.tensor_tensor_scan(slot_of, active, zero256, 0.0, ALU.add, ALU.add)
            nc.vector.drain()
            nc.vector.tensor_copy(n_ov[:, 0:1], slot_of[:, 255:256])
            nc.vector.drain()
            tt(slot_of, slot_of, active, ALU.mult)
            v.wait_ge(list_mm, 2 * TILES)
            nc.vector.tensor_copy(code, ps[:, 6, 0:256])
            nc.vector.drain()
            nc.vector.tensor_copy(slots[:, 0:EXPERTS], code.rearrange("p (e j) -> p e j", j=8)[:, :, 0])
            for m in range(EXTRA):
                stt(otmp, slot_of, float(m + 1), code, ALU.is_equal, ALU.mult, accum_out=slots[:, EXPERTS + m:EXPERTS + m + 1])
                nc.vector.drain()
                stt(otmp, slot_of, float(m + 1), cst[:, C_EJ:C_EJ + 256], ALU.is_equal, ALU.mult, accum_out=ov_e_f[:, m:m + 1])
                nc.vector.drain()
            nc.vector.tensor_copy(ov_e, ov_e_f)
            ts(slots, slots, -1.0, None, ALU.add)
            nc.vector.drain()
            ts(tok_f, slots, float(SEQ), -float(SEQ), ALU.is_ge, ALU.mult)
            ts(dst_f, slots, 0.0, 4.0 * SEQ, ALU.is_lt, ALU.mult)
            nc.vector.drain()
            tt(dst_f, dst_f, slots, ALU.add)
            nc.vector.drain()
            tt(tok_f, tok_f, dst_f, ALU.add)
            nc.vector.drain()
            nc.vector.tensor_copy(tok_of[:, 0:SLOTS], tok_f)
            nc.vector.tensor_copy(dst_of[:, 0:SLOTS], dst_f)
            nc.vector.drain().then_inc(slots_ready, 1)

            def rowsT(slot, u):
                v.wait_ge(rows_turned, slot + 1)
                at_least(v, gu_mm, slot - 1)
                nc.vector.tensor_copy(hgT[:, u, 4:8, :], ps[:, 1, :].rearrange("p (k n) -> p k n", k=4)).then_inc(rowsT_v, 1)

            def product(slot):
                v.wait_ge(silu_done, slot + 1)
                at_least(v, act_turned, slot)
                tt(act_g, silu_g, ps[:, 3, :], ALU.mult).then_inc(act_done, 1)

            def result(slot, u, pair):
                v.wait_ge(down_mm, slot + 1)
                at_least(v, y_out[u], pair * 16)
                nc.vector.tensor_copy(ys[:, u, 512:1024], ps[:, 6, :]).then_inc(y_v, 1)

            def expert(slot, u, pair):
                product(slot)
                rowsT(slot + 1, 1 - u)
                if not (isinstance(slot, int) and slot == 0):
                    result(slot - 1, 1 - u, pair + u - 1)

            nc.vector.memset(hg, 0.0).then_inc(hg_zero, 1)
            rowsT(0, 0)
            experts_loop(v, expert)
            extras_loop(v, expert, result)
            v.wait_ge(x2_back, 16)
            for t in range(TILES):
                v.wait_ge(final_in[t], 32)
                x_t = fx[:, t, :]
                stt(x_t, fy[0][:, t, :], gates[:, 0, t:t + 1], x_t, ALU.mult, ALU.add)
                nc.vector.drain()
                stt(x_t, fy[1][:, t, :], gates[:, 1, t:t + 1], x_t, ALU.mult, ALU.add).then_inc(final_v, 1)

        @block.scalar
        def _(act):
            f = nc.scalar.activation
            act.dma_start(par, a["params"]).then_inc(params_in, 16)
            for t in range(TILES):
                act.wait_ge(x_in[t], 16)
                act.wait_ge(sumsq_done, t)
                f(junk, x_all[:, t, :], ACT.Square, accum_out=ss[:, t:t + 1]).then_inc(sumsq_done, 1)
            act.wait_ge(table_mm, 1)
            f(bvec[0:AT_HEADS, :].rearrange("p (c n) -> p c n", c=3), ps[0:AT_HEADS, 5:8, 0:384], ACT.Copy).then_inc(table_sb, 1)
            act.wait_ge(table_sb, 1)
            act.dma_start(bias_dram, bvec[0:AT_HEADS, :]).then_inc(bias_out, 16)

            def put_qk(j):
                act.wait_ge(qk_turned, j + 1)
                col = P_QN + j // 8
                turned = ps[:, 4 + j % 2, :].rearrange("p (c n) -> p c n", c=4)
                f(qkT[:, j // 8, :, (j % 8) * P:(j % 8 + 1) * P], flipped(turned) if j < TILES else turned,
                  ACT.Copy, scale=par[:, col:col + 1]).then_inc(qk_out, 1)

            act.wait_ge(pads_zero, 1)
            for n, (g, kind, c, m) in enumerate(STEPS):
                if kind == "glu":
                    continue
                act.wait_ge(proj_done, n + 1)
                bank = ps[:, n % 4, :]
                if kind == "gate":
                    last = f(yc[:, c, m * 512:(m + 1) * 512], bank, ACT.Sigmoid)
                elif kind == "dn":
                    last = f(dpad[:, c, 3 + m * 512:3 + (m + 1) * 512], bank, ACT.Copy)
                elif kind == "z":
                    f(ab[:, m, :], bank[:, 256:264], ACT.Copy)
                    last = f(zg[:, m, :], bank[:, 0:256], ACT.Silu)
                elif kind in "qk":
                    j = n - FIRST_QK
                    if j >= 2:
                        act.wait_ge(qk_turned, j - 1)
                    last = f(stage[:, j % 2, :], bank, ACT.Copy)
                else:
                    last = f(v_tok[:, m, :], bank, ACT.Copy)
                last.then_inc(act_took, 1)
                if n > FIRST_QK and n - FIRST_QK - 1 < 16:
                    put_qk(n - FIRST_QK - 1)
                if n == 20:
                    act.wait_ge(cv_centred, 1)
                    for c2 in range(2):
                        f(ypad[:, c2, 0:SEQ], yc[:, c2, :], ACT.Square).then_inc(cv_squared, 1)
                if n == 23:
                    act.wait_ge(cv_varsb, 1)
                    f(junk, junk, ACT.Sqrt).then_inc(cv_rstd, 1)
                if n == FIRST_QK - 1:
                    for c2 in range(6):
                        act.wait_ge(dn_tapped, c2 + 1)
                        f(dconv[:, c2, :], dconv[:, c2, :], ACT.Silu).then_inc(dn_silu, 1)
                    act.wait_ge(cv_normed, 1)
                    for c2 in range(2):
                        f(yc[:, c2, :], yc[:, c2, :], ACT.Silu, scale=par[:, P_LNG + c2:P_LNG + c2 + 1],
                          bias=par[:, P_LNB + c2:P_LNB + c2 + 1]).then_inc(cv_out, 1)
            act.wait_ge(gate_v, 1)
            f(t2, t2, ACT.Exp)
            f(t3, t3, ACT.Exp, scale=-1.0)
            f(ea, par[:, P_ALOG:P_ALOG + 4], ACT.Exp).then_inc(gate_a, 1)
            act.wait_ge(gate_a, 1)
            f(t2, t2, ACT.Ln, bias=1.0).then_inc(gate_a, 1)
            act.wait_ge(gate_v, 5)
            f(eG, Gc, ACT.Exp).then_inc(gate_a, 1)
            f(ekd, ekd, ACT.Exp).then_inc(gate_a, 1)
            f(egl_all, Gtot, ACT.Exp).then_inc(gate_a, 1)

            def dn(i, k):
                if k >= len(DN_PIECES):
                    return
                piece = DN_PIECES[k]
                if piece == "split":
                    act.wait_ge(d_pe, pe_at(i, "split"))
                    if i:
                        act.wait_ge(d_pe, pe_at(i - 1, "norm"))
                        act.wait_ge(d_pool, pool_at(i - 1, "kdvb"))
                    f(tok[:, 0:512], ps[:, 0, :], ACT.Copy)
                    f(tok[:, 512:768], ps[:, 1, 0:256], ACT.Copy).then_inc(d_act, 1)
                    act.wait_ge(d_pe, pe_at(i, "gb"))
                    if i:
                        act.wait_ge(d_dve, dve_at(i - 1, "gram"))
                    for h in range(4):
                        last = f(dI[:, h, :], ps[:, 2, h * P:(h + 1) * P], ACT.Exp, bias=negG[:, 4 * i + h:4 * i + h + 1])
                    last.then_inc(d_act, 1)
                elif piece == "norm":
                    act.wait_ge(d_pe, pe_at(i, "norm"))
                    if i:
                        act.wait_ge(d_pe, pe_at(i - 1, "norm"))
                    if i >= 2:
                        act.wait_ge(d_pe, pe_at(i - 2, "carry"))
                    f(tT[i % 2].rearrange("p c m n -> p c (m n)"), ps[:, 0:2, 0:384], ACT.Copy).then_inc(d_act, 1)
                elif piece[0] == "x":
                    act.wait_ge(d_pe, pe_at(i, piece))
                    f(Xs.rearrange("p h n -> p (h n)"), ps[:, 2, :], ACT.Copy).then_inc(d_act, 1)
                elif piece == "fresh":
                    act.wait_ge(d_pe, pe_at(i, "fresh"))
                    f(vn, ps[:, 0, 0:256], ACT.Copy).then_inc(d_act, 1)
                elif piece == "out":
                    act.wait_ge(d_pe, pe_at(i, "out"))
                    f(mixT_dn[:, :, i * P:(i + 1) * P], ps[:, 2, 0:256].rearrange("p (c n) -> p c n", c=2),
                      ACT.Copy).then_inc(d_act, 1)

            idx = 0
            for ev in SCHEDULE:
                if ev[0] == "scores":
                    n = ev[1]
                    L = (attention_step(n)[1] + 1) * P
                    act.wait_ge(s_max, n + 1)
                    if n % 8 == 0 and n >= 16:
                        act.wait_ge(s_att, n // 8 - 1)
                    f(prob[:, n % 2, 0:L], prob[:, n % 2, 0:L], ACT.Exp, bias=nmx[:, n % 2:n % 2 + 1],
                      accum_out=Z[:, n // 8 % 2, n % 8:n % 8 + 1]).then_inc(s_exp, 1)
                elif ev[0] == "dn":
                    dn(ev[1], ev[2])
                elif ev[0] == "turn":
                    n = ev[1]
                    for g, cnt in turn_groups(n):
                        if TAKER[idx] == "a":
                            act.wait_ge(s_turn, idx + 1)
                            if n >= 2:
                                act.wait_ge(s_values, n - 1)
                            f(probT[:, n % 2, g * P:(g + cnt) * P], ps[:, 4 + idx % 2, 0:cnt * P], ACT.Copy)\
                                .then_inc(s_turned_a, 1)
                        idx += 1
                elif ev[0] == "att_out":
                    i = ev[1]
                    if TAKER[idx] == "a":
                        act.wait_ge(s_turn, idx + 1)
                        f(att_place(i), flipped(ps[:, 4 + idx % 2, :].rearrange("p (c n) -> p c n", c=4)),
                          ACT.Copy).then_inc(s_turned_a, 1)
                    idx += 1

            act.wait_ge(d_pe, len(PE_ORDER))
            act.wait_ge(d_dve, len(DVE_ORDER))

            def rows2(t):
                act.wait_ge(h2_turned, t + 1)
                if t >= 2:
                    act.wait_ge(logit_mm, t - 1)
                f(h2T[:, t % 2].rearrange("p k n -> p (k n)"), ps[:, 4:6, :].rearrange("p b n -> p (b n)"), ACT.Copy)\
                    .then_inc(h2T_done, 1)

            for t in range(TILES):
                act.wait_ge(x2_done, t + 1)
                act.wait_ge(x2_sq, t)
                f(junk3, xs[:, t % 2, :], ACT.Square, accum_out=ss[:, t:t + 1]).then_inc(x2_sq, 1)
                if t:
                    rows2(t - 1)
            rows2(TILES - 1)
            act.wait_ge(route_v, 1)
            f(gexp, gexp, ACT.Exp).then_inc(route_a, 1)
            act.wait_ge(route_v, 2)
            f(e_diff, e_diff, ACT.Exp).then_inc(route_a, 1)

            def rowsT(slot, u):
                act.wait_ge(rows_turned, slot + 1)
                at_least(act, gu_mm, slot - 1)
                f(hgT[:, u, 0:4, :], ps[:, 0, :].rearrange("p (k n) -> p k n", k=4), ACT.Copy).then_inc(rowsT_a, 1)

            def gate(slot):
                act.wait_ge(gu_mm, slot + 1)
                at_least(act, act_done, slot)
                f(silu_g, ps[:, 2, :], ACT.Silu).then_inc(silu_done, 1)

            def put_act(slot):
                act.wait_ge(act_turned, slot + 1)
                at_least(act, down_mm, slot)
                f(actT.rearrange("p k n -> p (k n)"), ps[:, 4, :], ACT.Copy).then_inc(actT_done, 1)

            def result(slot, u, pair):
                act.wait_ge(down_mm, slot + 1)
                at_least(act, y_out[u], pair * 16)
                f(ys[:, u, 0:512], ps[:, 5, :], ACT.Copy).then_inc(y_a, 1)

            def expert(slot, u, pair):
                gate(slot)
                rowsT(slot + 1, 1 - u)
                if not (isinstance(slot, int) and slot == 0):
                    result(slot - 1, 1 - u, pair + u - 1)
                put_act(slot)

            act.wait_ge(slots_ready, 1)
            rowsT(0, 0)
            experts_loop(act, expert)
            extras_loop(act, expert, result)

        @block.gpsimd
        def _(pool):
            tt, ts = nc.gpsimd.tensor_tensor, nc.gpsimd.tensor_scalar
            pool.wait_ge(consts_in, 16)
            for t in range(TILES):
                pool.wait_ge(sumsq_done, t + 1)
                ts(ss[:, t:t + 1], ss[:, t:t + 1], 1.0 / D, EPS, ALU.mult, ALU.add).then_inc(meansq_done, 1)
                pool.wait_ge(meansq_done, t + 1)
                tt(rs[:, t:t + 1], ss[:, t:t + 1], half_neg[:, 0:1], ALU.pow).then_inc(rms_done, 1)
            for j in range(16):
                pool.wait_ge(*act_taken(FIRST_QK + j))
                if j:
                    pool.wait_ge(qk_ss, j)
                tt(sqb, stage[:, j % 2, :], stage[:, j % 2, :], ALU.mult).then_inc(qk_sq, 1)
                pool.wait_ge(qk_ss, j + 1)
                if j >= 2:
                    pool.wait_ge(qk_normed, j - 1)
                tt(rs2[:, j % 2, :], ss2[:, j % 2, :], half_neg, ALU.pow).then_inc(qk_rs, 1)

            pool.wait_ge(qk_turned, 16)
            pool.wait_ge(gate_a, 5)

            def dn(i, k):
                if k >= len(DN_PIECES):
                    return
                piece = DN_PIECES[k]
                ti = slice(4 * i, 4 * i + 4)
                h4 = lambda x: x.rearrange("p (h d) -> p h d", d=HD)
                if piece == "split":
                    if i:
                        pool.wait_ge(d_pe, pe_at(i - 1, "gb"))
                    for h in range(4):
                        last = ts(Tg[:, h, :], tri, g_col[:, 4 * i + h:4 * i + h + 1], None, ALU.mult)
                    last.then_inc(d_pool, 1)
                    pool.wait_ge(d_act, act_at(i, "split"))
                    if i:
                        pool.wait_ge(d_dve, dve_at(i - 1, "ss"))
                    if i >= 2:
                        pool.wait_ge(d_dve, dve_at(i - 2, "osum"))
                    tt(dsq, tok[:, 0:512], tok[:, 0:512], ALU.mult).then_inc(d_pool, 1)
                elif piece == "ss":
                    pool.wait_ge(d_dve, dve_at(i, "ss"))
                    tt(drs, dss, half_neg, ALU.pow).then_inc(d_pool, 1)
                elif piece == "qkn":
                    pool.wait_ge(d_dve, dve_at(i, "qkn"))
                    if i:
                        pool.wait_ge(d_pe, pe_at(i - 1, "norm"))
                    if i >= 2:
                        pool.wait_ge(d_pe, pe_at(i - 2, "emit"))
                    tt(h4(kb), h4(tok[:, 256:512]), bc_h(beta[:, ti]), ALU.mult).then_inc(d_pool, 1)
                    tt(h4(kd[i % 2]), h4(tok[:, 256:512]), bc_h(ekd[:, ti]), ALU.mult)
                    tt(h4(vb[i % 2]), h4(tok[:, 512:768]), bc_h(beta[:, ti]), ALU.mult)
                    nc.gpsimd.drain().then_inc(d_pool, 1)
                elif piece == "gram":
                    pool.wait_ge(d_dve, dve_at(i, "gram"))
                    if i:
                        pool.wait_ge(d_pe, pe_at(i - 1, f"x{LEVELS - 1}"))
                    for lv in range(2):
                        tt(AM[:, lv], At, bc_f(lvl(lv), 4), ALU.mult).then_inc(d_pool, 1)
                elif piece[0] == "x" and int(piece[1:]) < LEVELS - 1:
                    lv = int(piece[1:]) + 1
                    if lv == 2:
                        pool.wait_ge(d_dve, dve_at(i, "inv1"))
                    else:
                        pool.wait_ge(d_pe, pe_at(i, f"x{lv - 2}"))
                    tt(AM[:, lv % 2], At, bc_f(lvl(lv), 4), ALU.mult).then_inc(d_pool, 1)
                elif piece == "emit":
                    pool.wait_ge(d_dve, dve_at(i, "emit"))
                    tt(dsq[:, 0:256], o1, o1, ALU.mult).then_inc(d_pool, 1)
                elif piece == "osum":
                    pool.wait_ge(d_dve, dve_at(i, "osum"))
                    tt(drs[:, 0:4], dss[:, 0:4], half_neg[:, 0:4], ALU.pow).then_inc(d_pool, 1)

            for ev in SCHEDULE:
                if ev[0] == "dn":
                    dn(ev[1], ev[2])

            pool.wait_ge(d_dve, len(DVE_ORDER))
            for t in range(TILES):
                pool.wait_ge(x2_sq, t + 1)
                ts(ss[:, t:t + 1], ss[:, t:t + 1], 1.0 / D, EPS, ALU.mult, ALU.add).then_inc(x2_ms, 1)
                pool.wait_ge(x2_ms, t + 1)
                tt(rs[:, t:t + 1], ss[:, t:t + 1], half_neg[:, 0:1], ALU.pow).then_inc(x2_rs, 1)

            def gather(slot, u, pair):
                nc.gpsimd.tensor_copy(tok_b[:, u:u + 1], tok_of[:, bass.ds(slot, 1)])
                at_least(pool, rows_turned, slot - 1)
                tt(tok_t[:, u:u + 1], zero256[:, 0:1], zero256[:, 0:1], ALU.add)
                nc.gpsimd.drain()
                nc.gpsimd.indirect_dma_start(hg[:, u, :], None, h2_dram, bass.IndirectOffsetOnAxis(ap=tok_b[:, u:u + 1], axis=0),
                                             bounds_check=SEQ - 1, oob_is_err=False).then_inc(rows_in[u], 16)

            def scatter(slot, u, pair):
                nc.gpsimd.tensor_copy(dst_b[:, u:u + 1], dst_of[:, bass.ds(slot, 1)])
                pool.wait_ge(y_v, slot + 1)
                pool.wait_ge(y_a, slot + 1)
                tt(dst_t[:, u:u + 1], zero256[:, 0:1], zero256[:, 0:1], ALU.add)
                nc.gpsimd.drain()
                nc.gpsimd.tensor_copy(dst_i[:, u:u + 1], dst_b[:, u:u + 1])
                nc.gpsimd.drain()
                nc.gpsimd.indirect_dma_start(y_dram, bass.IndirectOffsetOnAxis(ap=dst_i[:, u:u + 1], axis=0), ys[:, u, :], None,
                                             bounds_check=2 * SEQ - 1, oob_is_err=False).then_inc(y_out[u], 16)

            def expert(slot, u, pair):
                gather(slot + 2, u, pair + 1)
                if not (isinstance(slot, int) and slot == 0):
                    scatter(slot - 1, 1 - u, pair + u - 1)

            pool.wait_ge(hg_zero, 1)
            pool.wait_ge(slots_ready, 1)
            for u in range(2):
                pool.wait_ge(h2_out[u], 16 * TILES // 2)
            gather(0, 0, 0)
            gather(1, 1, 0)
            experts_loop(pool, expert)

            def finish(slot, u, pair):
                scatter(slot, u, pair)
                pool.wait_ge(y_out[u], 16 * (pair + 1))
                pool.wait_ge(y_out[1 - u], 16 * (pair + u))

            extras_loop(pool, expert, finish)
            nc.gpsimd.drain().then_inc(y_all_out, 1)


def lay_out(inputs):
    f = {k: np.asarray(v) for k, v in inputs.items()}
    cols = [f["cv_dw"][0].T.reshape(2, P, CV_TAPS).transpose(1, 0, 2).reshape(P, -1),
            f["dn_conv"][0].T.reshape(6, P, DN_TAPS).transpose(1, 0, 2).reshape(P, -1),
            f["norm_mix"][0].reshape(KC, P).T,
            f["cv_dw_bias"][0].reshape(2, P).T, f["cv_ln_g"][0].reshape(2, P).T, f["cv_ln_b"][0].reshape(2, P).T,
            np.tile(f["at_q_norm"][0], 2)[:, None], np.tile(f["at_k_norm"][0], 2)[:, None],
            np.broadcast_to(f["dn_a_log"][0], (P, DN_HEADS)), np.broadcast_to(f["dn_dt_bias"][0], (P, DN_HEADS)),
            np.broadcast_to(f["dn_out_norm"][0], (P, HD))]
    table = np.ones((P, 36), np.float32)
    table[:N_BUCKETS, :AT_HEADS] = f["rel_bias"]
    cols.append(table)
    cols.append(np.broadcast_to(np.concatenate([f["router_group_b"][0], f["router_expert_b"][0]]), (P, GROUPS + EXPERTS)))
    return {
        "x": f["x"].reshape(SEQ, D), "constants": shape_constants(), "distances": distance_constants(),
        "params": np.ascontiguousarray(np.concatenate(cols, 1)),
        "w_in": f["w_in"].reshape(D, N_IN), "w_out": f["w_out"].reshape(D, D),
        "norm_ffn": np.ascontiguousarray(np.broadcast_to(f["norm_ffn"][0], (P, D))),
        "router": np.ascontiguousarray(np.concatenate([f["router_group_w"][0], f["router_expert_w"][0]], 1)),
        "ex_gate": f["ex_gate"][0], "ex_up": f["ex_up"][0], "ex_down": f["ex_down"][0],
    }


def kernel(**inputs):
    import concourse.bacc as _bacc
    from concourse.bass_utils import run_bass_kernel_spmd as _run

    arrays = lay_out(inputs)
    nc = _bacc.Bacc("TRN2", target_bir_lowering=False, num_devices=1)
    args = {k: nc.dram_tensor(f"in_{k}", v.shape, mybir.dt.from_np(v.dtype), kind="ExternalInput").ap()
            for k, v in arrays.items()}
    out = nc.dram_tensor("out", [SEQ, D], F32, kind="ExternalOutput").ap()
    build(nc, args, out)
    r = _run(nc, [{f"in_{k}": v for k, v in arrays.items()}], core_ids=[0])
    return r.results[0]["out"].reshape(1, SEQ, D)
```

```python
import math
from contextlib import ExitStack

import numpy as np
import concourse.bass as bass
from concourse import mybir

F32 = mybir.dt.float32
U32 = mybir.dt.uint32
ALU = mybir.AluOpType
ACT = mybir.ActivationFunctionType
AX = mybir.AxisListType

P = 128
SEQ = 1024
D = 1024
TILES = SEQ // P
KC = D // P
EPS = 1e-6
NEG = -1e30

DN_HEADS, HD = 4, 64
DN_W = DN_HEADS * HD
DN_TAPS = 4
AT_HEADS = 8
AT_W = AT_HEADS * HD
CV_W = 256
CV_TAPS = 31
N_IN = 4 * DN_W + 2 * DN_HEADS + 3 * AT_W + 2 * CV_W
WINDOWS = ((128, 1), (512, 4), (2048, 16))
N_BUCKETS, MAX_DISTANCE = 32, 2048
GROUPS, PER_GROUP = 4, 8
EXPERTS = GROUPS * PER_GROUP
DE = D // 2
FC = DE // P
NREL = SEQ + P
LEVELS = 7

C_ID, C_TRI, C_ONE, C_NEG, C_LVL = 0, P, 2 * P, 3 * P, 4 * P
C_BD = C_LVL + LEVELS * P
C_IOTA = C_BD + P
C_E = C_IOTA + P
C_J = C_E + EXPERTS
C_TOK = C_J + 8
C_HALF = C_TOK + TILES
C_J128 = C_HALF + 8
C_THR = C_J128 + 8
C_EJ = C_THR + 8
NCONST = C_EJ + 256

RANKS = SEQ // P
SLOTS = EXPERTS + 2 * 8
EXTRA = SLOTS - EXPERTS

P_CVW = 0
P_DNW = P_CVW + 2 * CV_TAPS
P_GMIX = P_DNW + 6 * DN_TAPS
P_CVB = P_GMIX + KC
P_LNG = P_CVB + 2
P_LNB = P_LNG + 2
P_QN = P_LNB + 2
P_KN = P_QN + 1
P_ALOG = P_KN + 1
P_DT = P_ALOG + DN_HEADS
P_ON = P_DT + DN_HEADS
P_RB = P_ON + HD
P_RBIAS = P_RB + 36
NPARAM = P_RBIAS + GROUPS + EXPERTS


def shape_constants():
    j, i = np.arange(P)[:, None], np.arange(P)[None, :]
    cols = [(i == j), (j <= i), np.ones((P, P)), np.where(j <= i, 0.0, NEG)]
    for level in range(LEVELS):
        s = 1 << level
        cols.append((i // (2 * s) == j // (2 * s)) & (i // s % 2 == 1) & (j // s % 2 == 0))
    cols.append(i // HD == j // HD)
    cols.append(np.broadcast_to(i, (P, P)))
    cols.append(np.broadcast_to(np.arange(EXPERTS), (P, EXPERTS)))
    cols.append(np.broadcast_to(np.arange(8), (P, 8)))
    cols.append(np.arange(P)[:, None] + P * np.arange(TILES)[None, :])
    cols.append(np.full((P, 8), -0.5))
    cols.append(np.broadcast_to(P * np.arange(8), (P, 8)))
    cols.append(np.broadcast_to(np.where(np.arange(8), P * np.arange(8), 1e9), (P, 8)))
    cols.append(np.broadcast_to(np.repeat(np.arange(EXPERTS), 8), (P, 256)))
    return np.ascontiguousarray(np.concatenate([np.asarray(c, np.float32) for c in cols], 1))


def distance_constants():
    rel = SEQ - 1 - np.arange(NREL)
    exact = N_BUCKETS // 2
    d = np.maximum(rel, 1).astype(np.float32)
    log_bucket = exact + (np.log(d / np.float32(exact)) / np.float32(math.log(MAX_DISTANCE / exact))
                          * np.float32(N_BUCKETS - exact)).astype(np.int32)
    bucket = np.where(rel < exact, np.maximum(rel, 0), np.minimum(log_bucket, N_BUCKETS - 1))
    reach = sum(((rel >= 0) & (rel <= w) & (rel % r == 0)).astype(np.int32) for w, r in WINDOWS)
    rows = np.zeros((N_BUCKETS + 1, NREL), np.float32)
    rows[bucket, np.arange(NREL)] = 1.0
    rows[N_BUCKETS] = np.where(reach > 0, np.log(np.maximum(reach, 1)), NEG)
    return rows


def projection_steps():
    steps = [(0, "gate", c, n) for c in (0, 1) for n in (0, 1)]
    steps += [(0, "glu", c, n) for c in (0, 1) for n in (0, 1)]
    steps += [(1, "dn", c, n) for c in range(4) for n in (0, 1)]
    steps += [(2, "dn", c, n) for c in (4, 5) for n in (0, 1)]
    steps += [(2, "z", 0, t) for t in range(TILES)]
    steps += [(3, "q", 0, t) for t in range(TILES)]
    steps += [(4, "k", 1, t) for t in range(TILES)]
    steps += [(5, "v", 0, t) for t in range(TILES)]
    return steps


STEPS = projection_steps()
FIRST_QK = 28
FIRST_V = FIRST_QK + 2 * TILES
O_CU = N_IN - 2 * CV_W
WGROUPS = [(O_CU, 512), (0, 512), (512, 520), (1032, 512), (1544, 512), (2056, 512)]
GW = 520


DN_PIECES = (["split", "ss", "qkn", "norm", "gram", "inv1"]
             + [f"{s}{lv}" for lv in range(1, LEVELS) for s in ("x", "y")]
             + ["carry", "fresh", "emit", "osum", "onorm", "out"])
DN_LAG = len(DN_PIECES) // 2


def attention_step(n):
    pair, rest = divmod(n, 2 * TILES)
    return pair, rest // 2, rest % 2


def mixer_schedule():
    n_att = TILES * AT_HEADS
    attention = []
    for n in range(n_att + 8):
        if n < n_att:
            attention.append((("scores", n), 1.5 * attention_step(n)[1] + 2))
        if 1 <= n <= n_att:
            attention.append((("turn", n - 1), 1.5 * attention_step(n - 1)[1] + 2))
        if 2 <= n <= n_att + 1:
            attention.append((("values", n - 2), 0.5 * attention_step(n - 2)[1] + 1))
        if n % 8 == 4 and n >= 12:
            attention.append((("att_out", n // 8 - 1), 1))
    pieces = []
    phases = (TILES + 1) * DN_LAG
    beside_v = DN_LAG
    for phase in range(beside_v, phases):
        i, k = divmod(phase, DN_LAG)
        at = (phase - beside_v) / (phases - beside_v)
        if i:
            pieces.append((("dn", i - 1, k + DN_LAG), at))
        if i < TILES:
            pieces.append((("dn", i, k), at + 0.5 / (phases - beside_v)))
    out = []
    for t in range(TILES):
        out.append(("v", t))
        out += [("dn", 0, k) for k in range(t * beside_v // TILES, (t + 1) * beside_v // TILES)]
    total, done = sum(c for _, c in attention), 0
    for event, cost in attention:
        while pieces and pieces[0][1] * total <= done:
            out.append(pieces.pop(0)[0])
        out.append(event)
        done += cost
    return out + [p for p, _ in pieces]


def turn_groups(n):
    blocks = attention_step(n)[1] + 1
    return [(g, min(4, blocks - g)) for g in range(0, blocks, 4)]


def build(nc, a, out, debug_stop=None):
    ctx = ExitStack()
    with ctx:
        def sem(name):
            return ctx.enter_context(nc.semaphore(name))

        arena = ctx.enter_context(nc.sbuf_tensor("arena", [P, 53200], F32))
        ps = ctx.enter_context(nc.psum_tensor("ps", [P, 8, 512], F32))

        def cut(at, *dims):
            size = int(np.prod(dims))
            flat = arena[:, at:at + size]
            if len(dims) == 1:
                return flat
            names = "abcd"[:len(dims)]
            return flat.rearrange("p (%s) -> p %s" % (" ".join(names), " ".join(names)),
                                  **{n: d for n, d in zip(names[1:], dims[1:])})

        A, B, C, DV, E, F, G, H, I, J = 0, 8192, 16512, 24704, 28800, 34964, 41108, 43220, 45328, 47376
        hT = cut(A, KC, SEQ)
        wb = cut(B, 2, KC, GW)
        x_all = cut(C, TILES, D)
        qkT = cut(C, 2, 4, SEQ)
        v_tok = cut(DV, TILES, AT_W)
        dpad = cut(E, 6, SEQ + 3)
        dconv = cut(F, 6, SEQ)
        zg = cut(G, TILES, DN_W)
        ab = cut(G + 2048, TILES, 8)
        ypad = cut(H, 2, SEQ + 30)
        yc = cut(I, 2, SEQ)
        mixT_cv = yc
        cst = cut(J, NCONST)
        par = cut(J + NCONST, NPARAM)
        K = J + NCONST + NPARAM
        gate32 = cut(K, 9, 32)
        K += 9 * 32
        small = cut(K, 64)
        K += 64
        junk = cut(K, D)
        stage = cut(K + D, 2, AT_W)
        sqb = cut(K + 2 * D, AT_W)
        assert K + 2 * D + AT_W <= 53200
        tabE = cut(F, 1152)
        bvec = cut(F + 1152, 1152)

        slab = cut(A, 2, 2, SEQ)
        prob = cut(B, 2, SEQ)
        probT = cut(B + 2048, 2, SEQ)
        mixT_at = cut(B + 4096, 4, SEQ)
        mixT_dn = cut(H, 2, SEQ)
        tok = cut(E, 3 * DN_W)
        tT = [cut(at, 2, 3, P) for at in (E + 768, A + 4096)]
        dI = cut(E + 1536, 4, P)
        At = cut(E + 2048, 4, P)
        qkD = [cut(at, 4, P) for at in (E + 2560, A + 4864)]
        AM = cut(E + 3072, 2, 4, P)
        T = cut(E + 4096, 4, P)
        Tt = [cut(at, 4, P) for at in (E + 4608, A + 5376)]
        Xs = cut(E + 5120, 4, P)
        Tg = cut(K, 4, P)
        dsq = cut(K + 512, 512)
        kb = cut(K + 1024, DN_W)
        kd = [cut(at, DN_W) for at in (K + 1280, A + 5888)]
        vb = [cut(at, DN_W) for at in (K + 1536, A + 6144)]
        R = cut(K + 1792, DN_W)
        vn = cut(K + 2048, DN_W)
        o1 = cut(K + 2304, DN_W)
        tmp = cut(K + 2560, DN_W)
        Sst = cut(K + 2816, 2, P)
        att = cut(E + 5632, AT_W)
        assert K + 3072 <= 53200

        w_out = [cut(at, D) for at in (C, C + SEQ, C + 2 * SEQ, C + 4 * SEQ, C + 5 * SEQ, C + 6 * SEQ, A, A + D)]
        xs = cut(B, 2, D)
        g_ffn = cut(B + 2048, D)
        router = cut(B + 3072, KC, 36)
        logits = cut(B + 3360, TILES, 36)
        h2s = cut(G, 2, D)
        h2T = cut(K, 2, KC, P)
        junk3 = cut(K + 2048, D)
        r0 = A + 2048
        padded = cut(r0, TILES, 8)
        gtop = cut(r0 + 64, TILES, 8)
        gtop_i = cut(r0 + 128, TILES, 8).bitcast(U32)
        em = cut(r0 + 192, TILES, EXPERTS)
        etop = cut(r0 + 448, TILES, 8)
        etop_i = cut(r0 + 512, TILES, 8).bitcast(U32)
        g_hot = cut(r0 + 576, TILES, 4)
        g_idx = cut(r0 + 608, TILES)
        e_idx = cut(r0 + 616, 2, TILES)
        p_grp = cut(r0 + 632, TILES)
        rk_k = cut(r0 + 640, 2, TILES)
        rmod = cut(r0 + 656, 2, TILES)
        jn = cut(r0 + 672, 2, TILES)
        gexp = cut(r0 + 688, TILES, 4)
        e_diff = cut(r0 + 720, TILES)
        jhot = cut(r0 + 768, 2, TILES, 8)
        hot = cut(r0 + 896, 2, TILES, EXPERTS)
        hots = cut(r0 + 1408, TILES, EXPERTS)
        before = cut(r0 + 1664, TILES, EXPERTS)
        rtmp = cut(r0 + 2176, 2, EXPERTS)
        e_count = cut(r0 + 2432, EXPERTS)
        r_hot = cut(r0 + 2464, 2, P)
        r_val = cut(r0 + 2720, 2, 256)
        code = cut(r0 + 3232, 256)
        active = cut(r0 + 3488, 256)
        slot_of = cut(r0 + 3744, 256)
        r1 = A + 6144
        zero256 = cut(r1, 256)
        otmp = cut(r1 + 256, 256)
        slots = cut(r1 + 512, SLOTS)
        code2 = cut(r1 + 560, SLOTS)
        tok_f = cut(r1 + 608, SLOTS)
        dst_f = cut(r1 + 656, SLOTS)
        tok_of = cut(r1 + 864, SLOTS + 2).bitcast(U32)
        dst_of = cut(r1 + 928, SLOTS + 2)
        ov_e_f = cut(r1 + 784, EXTRA + 1)
        ov_e = cut(r1 + 804, EXTRA + 1).bitcast(U32)
        n_ov = cut(r1 + 824, 8).bitcast(U32)
        gates = cut(r1 + 840, 2, TILES)
        tok_b = cut(r1 + 856, 2).bitcast(U32)
        dst_b = cut(r1 + 858, 2)
        dst_t = cut(r1 + 862, 2)
        tok_t = cut(r1 + 1000, 2)
        dst_i = cut(r1 + 860, 2).bitcast(U32)
        W = [cut(E, 3 * KC * DE), cut(C, 3 * KC * DE)]
        w_gate = [w[:, 0:KC * DE].rearrange("p (k n) -> p k n", k=KC) for w in W]
        w_up = [w[:, KC * DE:2 * KC * DE].rearrange("p (k n) -> p k n", k=KC) for w in W]
        w_down = [w[:, 2 * KC * DE:].rearrange("p (k n) -> p k n", k=FC) for w in W]
        hg = cut(H, 2, D)
        hgT = cut(I, 2, KC, P)
        silu_g = cut(A, DE)
        act_g = cut(A + 512, DE)
        actT = cut(A + 1024, FC, P)
        ys = cut(K, 2, D)
        fx = cut(B, TILES, D)
        fy = [cut(at, TILES, D) for at in (C, C + 8192)]
        x2_dram = nc.dram_tensor("x2_rows", [SEQ, D], F32).ap()
        h2_dram = nc.dram_tensor("h2_rows", [SEQ, D], F32).ap()
        y_dram = nc.dram_tensor("expert_rows", [2 * SEQ, D], F32).ap()

        ident = cst[:, C_ID:C_ID + P]
        tri = cst[:, C_TRI:C_TRI + P]
        ones = cst[:, C_ONE:C_ONE + P]
        negm = cst[:, C_NEG:C_NEG + P]
        bd = cst[:, C_BD:C_BD + P]

        def lvl(n):
            return cst[:, C_LVL + n * P:C_LVL + (n + 1) * P]

        half_neg = cst[:, C_HALF:C_HALF + 8]
        g_col, beta, t1, t2, t3, Gc, Gtot, eG, ekd = (gate32[:, n, :] for n in range(9))
        ss = small[:, 0:8]
        rs = small[:, 8:16]
        ss2 = small[:, 16:32].rearrange("p (u h) -> p u h", u=2)
        rs2 = small[:, 32:48].rearrange("p (u h) -> p u h", u=2)
        ea = small[:, 48:52]
        mx = small[:, 52:54]
        nmx = small[:, 54:56]
        Z = small[:, 16:32].rearrange("p (u h) -> p u h", u=2)
        rZ = small[:, 32:40]
        egl = small[:, 0:16].rearrange("p (t c) -> p t c", c=2)
        dss = small[:, 40:48]
        drs = small[:, 56:64]
        egl_all = t3
        negG = t2

        def bc_h(col, n=HD):
            return col.unsqueeze(2).to_broadcast([P, col.shape[1], n])

        def bc_f(mat, n):
            return mat.unsqueeze(1).to_broadcast([P, n, mat.shape[1]])

        def flipped(ap):
            dims = [list(d) for d in ap.ap]
            step, n = dims[-1]
            dims[-1] = [-step, n]
            return bass.AP(tensor=ap.tensor, offset=ap.offset + step * (n - 1), ap=dims)

        bias_dram = nc.dram_tensor("bias_by_distance", [AT_HEADS, NREL], F32).ap()

        consts_in = sem("consts_in")
        params_in = sem("params_in")
        onehot_in = sem("onehot_in")
        x_in = [sem(f"x_in{t}") for t in range(TILES)]
        w_in_sem = [sem(f"w_in{n}") for n in range(2)]
        sumsq_done = sem("sumsq_done")
        meansq_done = sem("meansq_done")
        rms_done = sem("rms_done")
        h_scaled = sem("h_scaled")
        hT_turned = sem("hT_turned")
        hT_done = sem("hT_done")
        table_mm = sem("table_mm")
        table_sb = sem("table_sb")
        bias_out = sem("bias_out")
        slab_in = [sem(f"slab_in{n}") for n in range(2)]
        pads_zero = sem("pads_zero")
        proj_done = sem("proj_done")
        act_took = sem("act_took")
        dve_took = sem("dve_took")
        tap_done = sem("tap_done")
        cv_mean = sem("cv_mean")
        cv_centred = sem("cv_centred")
        cv_squared = sem("cv_squared")
        cv_var = sem("cv_var")
        cv_varsb = sem("cv_varsb")
        cv_rstd = sem("cv_rstd")
        cv_normed = sem("cv_normed")
        cv_out = sem("cv_out")
        dn_tapped = sem("dn_tapped")
        dn_silu = sem("dn_silu")
        qk_sq = sem("qk_sq")
        qk_ss = sem("qk_ss")
        qk_rs = sem("qk_rs")
        qk_normed = sem("qk_normed")
        qk_turned = sem("qk_turned")
        qk_out = sem("qk_out")
        zg_done = sem("zg_done")
        gate_a = sem("gate_a")
        gate_v = sem("gate_v")
        gate_p = sem("gate_p")
        s_scores = sem("s_scores")
        s_max = sem("s_max")
        s_exp = sem("s_exp")
        s_turn = sem("s_turn")
        s_turned_a = sem("s_turned_a")
        s_turned_v = sem("s_turned_v")
        s_values = sem("s_values")
        s_att = sem("s_att")
        s_attT = sem("s_attT")
        s_attT_out = sem("s_attT_out")
        d_pe = sem("d_pe")
        d_act = sem("d_act")
        d_dve = sem("d_dve")
        d_pool = sem("d_pool")

        w_out_in = sem("w_out_in")
        ffn_in = sem("ffn_in")
        xs_in = [sem(f"xs_in{n}") for n in range(2)]
        out_mm = sem("out_mm")
        x2_done = sem("x2_done")
        x2_sq = sem("x2_sq")
        x2_ms = sem("x2_ms")
        x2_rs = sem("x2_rs")
        h2_done = sem("h2_done")
        x2_out = [sem(f"x2_out{n}") for n in range(2)]
        h2_out = [sem(f"h2_out{n}") for n in range(2)]
        h2_turned = sem("h2_turned")
        h2T_done = sem("h2T_done")
        logit_mm = sem("logit_mm")
        logit_sb = sem("logit_sb")
        route_v = sem("route_v")
        route_a = sem("route_a")
        rank_mm = sem("rank_mm")
        hots_done = sem("hots_done")
        list_v = sem("list_v")
        list_mm = sem("list_mm")
        slots_ready = sem("slots_ready")
        extras_ready = sem("extras_ready")
        hg_zero = sem("hg_zero")
        gu_in = [sem(f"gu_in{n}") for n in range(2)]
        down_in = [sem(f"down_in{n}") for n in range(2)]
        rows_in = [sem(f"rows_in{n}") for n in range(2)]
        idx_copied = sem("idx_copied")
        rows_turned = sem("rows_turned")
        rowsT_a = sem("rowsT_a")
        rowsT_v = sem("rowsT_v")
        gu_mm = sem("gu_mm")
        silu_done = sem("silu_done")
        act_done = sem("act_done")
        act_turned = sem("act_turned")
        actT_done = sem("actT_done")
        down_mm = sem("down_mm")
        y_a = sem("y_a")
        y_v = sem("y_v")
        y_out = [sem(f"y_out{n}") for n in range(2)]
        final_in = [sem(f"final_in{n}") for n in range(TILES)]
        y_all_out = sem("y_all_out")
        final_v = sem("final_v")
        final_out = sem("final_out")
        x2_back = sem("x2_back")

        def at_least(eng, s, value):
            if not isinstance(value, int) or value > 0:
                eng.wait_ge(s, value)

        def experts_loop(eng, body):
            for u in range(2):
                body(u, u, 0)
            with eng.Fori(1, EXPERTS // 2) as pair:
                for u in range(2):
                    body(2 * pair + u, u, pair)

        def extras_loop(eng, body, finish=None):
            more = eng.value_load(n_ov[0:1, 0:1], min_val=0, max_val=EXTRA)
            if finish:
                with eng.If(more < 1):
                    finish(EXPERTS - 1, 1, EXPERTS // 2 - 1)
            with eng.Fori(EXPERTS // 2, SLOTS // 2) as pair:
                for u in range(2):
                    slot = 2 * pair + u
                    with eng.If(more + EXPERTS > slot):
                        body(slot, u, pair)
                        if finish:
                            with eng.If(more + EXPERTS < slot + 2):
                                finish(slot, u, pair)

        def act_taken(step):
            glu = [n for n, s in enumerate(STEPS[:step + 1]) if s[1] == "glu"]
            return (dve_took, len(glu)) if STEPS[step][1] == "glu" else (act_took, step + 1 - len(glu))

        group_end = {g: max(n for n, s in enumerate(STEPS) if s[0] == g) + 1 for g in range(6)}

        pe_marks = {p: [p] for p in DN_PIECES if p not in ("ss", "qkn", "osum", "onorm")}
        pe_marks["split"] = ["split", "gb"]
        for lv in range(1, LEVELS - 1):
            pe_marks[f"y{lv}"] = [f"T{lv}", f"y{lv}"]
        act_marks = {"split": ["split", "decay"], "norm": ["norm"], "fresh": ["fresh"], "out": ["out"],
                     **{f"x{lv}": [f"x{lv}"] for lv in range(1, LEVELS)}}
        dve_marks = {**{p: [p] for p in ("ss", "qkn", "inv1", "carry", "emit", "osum", "onorm")}, "gram": ["gram", "am0", "qkD"],
                     **{f"y{lv}": ([f"T{lv}"] if lv < LEVELS - 1 else []) + [f"y{lv}"] for lv in range(1, LEVELS)}}
        pool_marks = {"split": ["tg", "sq"], "ss": ["rs"], "qkn": ["kb", "kdvb"], "gram": ["am1"],
                      **{f"x{lv}": [f"am{lv + 1}"] for lv in range(1, LEVELS - 1)}, "emit": ["osq"], "osum": ["ors"]}
        SCHEDULE = mixer_schedule()

        def in_order(marks):
            return [(ev[1], m) for ev in SCHEDULE if ev[0] == "dn" for m in marks.get(DN_PIECES[ev[2]], [])]

        PE_ORDER, ACT_ORDER, DVE_ORDER, POOL_ORDER = (in_order(m) for m in (pe_marks, act_marks, dve_marks, pool_marks))

        def pe_at(i, mark):
            return PE_ORDER.index((i, mark)) + 1

        def act_at(i, mark):
            return ACT_ORDER.index((i, mark)) + 1

        def dve_at(i, mark):
            return DVE_ORDER.index((i, mark)) + 1

        def pool_at(i, mark):
            return POOL_ORDER.index((i, mark)) + 1

        TURNS = []
        for ev in SCHEDULE:
            if ev[0] == "turn":
                TURNS += [("p", ev[1], g, c) for g, c in turn_groups(ev[1])]
            elif ev[0] == "att_out":
                TURNS.append(("o", ev[1], 0, 4))
        TAKER = ["v" if (n % 2) else "a" for n in range(len(TURNS))]

        def taken(idx):
            who = TAKER[idx]
            return (s_turned_a if who == "a" else s_turned_v), TAKER[:idx + 1].count(who)

        first_turn = {}
        last_turn = {}
        for n, (kind, m, g, c) in enumerate(TURNS):
            first_turn.setdefault((kind, m), n)
            last_turn[(kind, m)] = n

        def att_place(group):
            return mixT_at[:, group // 2, group % 2 * 512:(group % 2 + 1) * 512].rearrange("p (c n) -> p c n", c=4)

        block = ctx.enter_context(nc.Block())

        @block.sync
        def _(sp):
            sp.dma_start(cst, a["constants"]).then_inc(consts_in, 16)
            for t in range(TILES):
                sp.dma_start(x_all[:, t, :], a["x"][t * P:(t + 1) * P, :]).then_inc(x_in[t], 16)
            for g, (c0, width) in enumerate(WGROUPS):
                if g >= 2:
                    sp.wait_ge(proj_done, group_end[g - 2])
                sp.dma_start(wb[:, g % 2, :, 0:width],
                             a["w_in"][:, c0:c0 + width].rearrange("(k p) n -> p k n", p=P)).then_inc(w_in_sem[g % 2], 16)
                if g == 0:
                    sp.dma_start(tabE[0:N_BUCKETS + 1, :], a["distances"]).then_inc(onehot_in, 16)
            sp.wait_ge(proj_done, len(STEPS))
            sp.wait_ge(bias_out, 16)
            for pair in range(AT_HEADS // 2):
                if pair >= 2:
                    sp.wait_ge(s_max, 2 * TILES * (pair - 1))
                src = bass.AP(tensor=bias_dram.tensor, offset=2 * pair * NREL, ap=[[1, P], [NREL, 2], [1, SEQ]])
                sp.dma_start(slab[:, pair % 2], src).then_inc(slab_in[pair % 2], 16)

            n_att = TILES * AT_HEADS
            sp.wait_ge(s_max, 3 * 2 * TILES)
            for k in range(KC):
                sp.dma_start(w_out[k], a["w_out"][k * P:(k + 1) * P, :]).then_inc(w_out_in, 16)
            sp.wait_ge(s_values, n_att)
            sp.wait_ge(s_turned_a, TAKER.count("a"))
            sp.wait_ge(s_turned_v, TAKER.count("v"))
            sp.dma_start(g_ffn, a["norm_ffn"]).then_inc(ffn_in, 16)
            sp.dma_start(router, a["router"].rearrange("(k p) n -> p k n", p=P)).then_inc(ffn_in, 16)
            for t in range(2):
                sp.dma_start(xs[:, t, :], a["x"][t * P:(t + 1) * P, :]).then_inc(xs_in[t], 16)
            sp.wait_ge(d_dve, len(DVE_ORDER))
            sp.wait_ge(d_pe, len(PE_ORDER))

            def load_gate_up(slot, u, expert):
                at_least(sp, gu_mm, slot - 1)
                for w, name in ((w_gate, "ex_gate"), (w_up, "ex_up")):
                    sp.dma_start(w[u], a[name][bass.ds(expert, 1), :, :].rearrange("e (k p) n -> p (e k) n", p=P))\
                      .then_inc(gu_in[u], 16)

            def load_down(slot, u, expert):
                at_least(sp, down_mm, slot - 1)
                sp.dma_start(w_down[u], a["ex_down"][bass.ds(expert, 1), :, :].rearrange("e (k p) n -> p (e k) n", p=P))\
                  .then_inc(down_in[u], 16)

            load_gate_up(0, 0, 0)
            load_down(0, 0, 0)
            for t in range(TILES):
                sp.wait_ge(x2_done, t + 1)
                sp.dma_start(x2_dram[t * P:(t + 1) * P, :], xs[:, t % 2, :]).then_inc(x2_out[t % 2], 16)
                sp.wait_ge(h2_done, t + 1)
                sp.dma_start(h2_dram[t * P:(t + 1) * P, :], h2s[:, t % 2, :]).then_inc(h2_out[t % 2], 16)
                if t + 2 < TILES:
                    sp.wait_ge(x2_out[t % 2], 16 * (t // 2 + 1))
                    sp.wait_ge(x2_sq, t + 1)
                    sp.dma_start(xs[:, t % 2, :], a["x"][(t + 2) * P:(t + 3) * P, :]).then_inc(xs_in[t % 2], 16)
            sp.wait_ge(out_mm, TILES)
            load_gate_up(1, 1, 1)
            sp.wait_ge(slots_ready, 1)
            for u in range(2):
                sp.wait_ge(x2_out[u], 16 * TILES // 2)
            def load_next(pair):
                for u in range(2):
                    load_gate_up(2 * pair + u, u, 2 * pair + u)
                    load_down(2 * pair + u - 1, 1 - u, 2 * pair + u - 1)

            with sp.Fori(1, 1 + TILES) as pair:
                load_next(pair)
                sp.dma_start(fx[:, bass.ds(pair - 1, 1), :],
                             x2_dram.rearrange("(t p) d -> p t d", p=P)[:, bass.ds(pair - 1, 1), :]).then_inc(x2_back, 16)
            with sp.Fori(1 + TILES, EXPERTS // 2) as pair:
                load_next(pair)
            sp.wait_ge(extras_ready, 1)
            more = sp.value_load(n_ov[0:1, 0:1], min_val=0, max_val=EXTRA)
            with sp.If(more < 1):
                load_down(EXPERTS - 1, 1, EXPERTS - 1)
            with sp.Fori(0, EXTRA // 2) as pair:
                for u in range(2):
                    m = 2 * pair + u
                    with sp.If(more > m):
                        before_it = sp.value_load(ov_e[0:1, bass.ds(m, 1)], min_val=0, max_val=EXPERTS - 1)
                        expert = sp.value_load(ov_e[0:1, bass.ds(m + 1, 1)], min_val=0, max_val=EXPERTS - 1)
                        load_gate_up(m + EXPERTS, u, expert)
                        load_down(m + EXPERTS - 1, 1 - u, before_it)
                        with sp.If(more < m + 2):
                            load_down(m + EXPERTS, u, expert)
            sp.wait_ge(y_all_out, 1)
            for t in range(TILES):
                for c in range(2):
                    sp.dma_start(fy[c][:, t, :], y_dram[c * SEQ + t * P:c * SEQ + (t + 1) * P, :]).then_inc(final_in[t], 16)
            for t in range(TILES):
                sp.wait_ge(final_v, t + 1)
                sp.dma_start(out[t * P:(t + 1) * P, :], fx[:, t, :]).then_inc(final_out, 16)
            sp.wait_ge(final_out, 16 * TILES)

        @block.tensor
        def _(pe):
            mm, tr = nc.tensor.matmul, nc.tensor.transpose
            pe.wait_ge(consts_in, 16)
            for t in range(TILES):
                pe.wait_ge(h_scaled, t + 1)
                if t >= 2:
                    pe.wait_ge(hT_done, 2 * (t - 1))
                for half in range(2):
                    for c in range(4):
                        k = 4 * half + c
                        last = tr(ps[:, 2 * (t % 2) + half, c * P:(c + 1) * P], x_all[:, t, k * P:(k + 1) * P], ident)
                    last.then_inc(hT_turned, 1)
            pe.wait_ge(params_in, 16)
            pe.wait_ge(onehot_in, 16)
            for c in range(3):
                last = mm(ps[0:AT_HEADS, 5 + c, 0:384], par[0:N_BUCKETS + 1, P_RB:P_RB + AT_HEADS],
                          tabE[0:N_BUCKETS + 1, c * 384:(c + 1) * 384], start=True, stop=True)
            last.then_inc(table_mm, 1)
            pe.wait_ge(hT_done, 2 * TILES)

            def turn_qk(j):
                pe.wait_ge(qk_normed, j + 1)
                if j >= 2:
                    pe.wait_ge(qk_out, j - 1)
                for c in range(4):
                    last = tr(ps[:, 4 + j % 2, c * P:(c + 1) * P], stage[:, j % 2, c * P:(c + 1) * P], ident)
                last.then_inc(qk_turned, 1)

            def project(n):
                g, kind, c, m = STEPS[n]
                if g != STEPS[max(n - 1, 0)][0] or n == 0:
                    pe.wait_ge(w_in_sem[g % 2], 16 * (g // 2 + 1))
                if n < FIRST_V:
                    bank = n % 4
                    if n >= 4:
                        pe.wait_ge(*act_taken(n - 4))
                else:
                    bank = (6, 7, 3)[m % 3]
                    if m >= 2:
                        pe.wait_ge(*act_taken(n - 3))
                w = wb[:, g % 2]
                for k in range(KC):
                    f = dict(start=(k == 0), stop=(k == KC - 1))
                    if kind in ("gate", "glu", "dn"):
                        col = {"gate": 2 + c, "glu": c, "dn": c % 4}[kind] * P
                        last = mm(ps[:, bank, :], w[:, k, col:col + P], hT[:, k, m * 512:(m + 1) * 512], **f)
                    elif kind == "z":
                        last = mm(ps[:, bank, 0:264], hT[:, k, m * P:(m + 1) * P], w[:, k, 256:520], **f)
                    else:
                        last = mm(ps[:, bank, :], hT[:, k, m * P:(m + 1) * P], w[:, k, 0:512], **f)
                last.then_inc(proj_done, 1)

            for n in range(FIRST_V):
                project(n)
                if n == 19:
                    pe.wait_ge(tap_done, 2 * CV_TAPS)
                    for half in range(2):
                        for c2 in range(2):
                            last = mm(ps[:, 6 + half, :], ones, yc[:, c2, half * 512:(half + 1) * 512],
                                      start=(c2 == 0), stop=(c2 == 1))
                    last.then_inc(cv_mean, 1)
                if n == 22:
                    pe.wait_ge(cv_squared, 2)
                    for half in range(2):
                        for c2 in range(2):
                            last = mm(ps[:, 6 + half, :], ones, ypad[:, c2, half * 512:(half + 1) * 512],
                                      start=(c2 == 0), stop=(c2 == 1))
                    last.then_inc(cv_var, 1)
                if n > FIRST_QK and n - FIRST_QK - 1 < 16:
                    turn_qk(n - FIRST_QK - 1)
                if n == FIRST_QK + 7:
                    pe.wait_ge(gate_v, 4)
                    pe.wait_ge(cv_varsb, 1)
                    mm(ps[:, 6, 0:32], tri, g_col, start=True, stop=True)
                    mm(ps[:, 6, 32:64], ones, g_col, start=True, stop=True).then_inc(cv_mean, 1)

            D0, D1, D2, PV, TB = 0, 1, 2, 3, 4

            def dn(i, k):
                if k >= len(DN_PIECES):
                    return
                piece = DN_PIECES[k]
                if piece == "split":
                    if i == 0:
                        pe.wait_ge(dn_silu, 6)
                        pe.wait_ge(*act_taken(FIRST_V - 2))
                        pe.wait_ge(gate_a, 5)
                    else:
                        pe.wait_ge(d_dve, dve_at(i - 1, "y3"))
                    for c in range(6):
                        last = tr(ps[:, c // 4, (c % 4) * P:(c % 4 + 1) * P], dconv[:, c, i * P:(i + 1) * P], ident)
                    last.then_inc(d_pe, 1)
                    pe.wait_ge(d_pool, pool_at(i, "tg"))
                    if i:
                        pe.wait_ge(d_act, act_at(i - 1, "x4"))
                    mm(ps[:, D2, :], ones, Tg.rearrange("p h n -> p (h n)"), start=True, stop=False)
                    for h in range(4):
                        last = mm(ps[:, D2, h * P:(h + 1) * P], ident, negm, start=False, stop=(h == 3))
                    last.then_inc(d_pe, 1)
                elif piece == "norm":
                    pe.wait_ge(d_dve, dve_at(i, "qkn"))
                    pe.wait_ge(d_pool, pool_at(i, "kb"))
                    if i:
                        pe.wait_ge(d_dve, dve_at(i - 1, "y5"))
                    for pair in range(2):
                        cols = slice(pair * P, (pair + 1) * P)
                        for m, src in enumerate((kb[:, cols], tok[:, cols], tok[:, DN_W + pair * P:DN_W + (pair + 1) * P])):
                            last = tr(ps[:, pair, m * P:(m + 1) * P], src, ident)
                    last.then_inc(d_pe, 1)
                elif piece == "gram":
                    pe.wait_ge(d_act, act_at(i, "norm"))
                    for h in range(4):
                        rows = slice(HD * (h % 2), HD * (h % 2) + HD)
                        last = mm(ps[:, h % 2, (h // 2) * 256:(h // 2) * 256 + 256], tT[i % 2][rows, h // 2, 2, :],
                                  tT[i % 2][rows, h // 2, 0:2, :], start=True, stop=True)
                    last.then_inc(d_pe, 1)
                elif piece == "inv1":
                    pe.wait_ge(d_dve, dve_at(i, "am0"))
                    pe.wait_ge(d_act, act_at(i, "decay"))
                    if i:
                        pe.wait_ge(d_act, act_at(i - 1, "x6"))
                    for h in range(4):
                        last = tr(ps[:, D2, h * P:(h + 1) * P], AM[:, 0, h, :], ident)
                    last.then_inc(d_pe, 1)
                elif piece[0] == "x":
                    lv = int(piece[1:])
                    pe.wait_ge(d_pool, pool_at(i, f"am{lv}"))
                    pe.wait_ge(d_dve, dve_at(i, f"T{lv - 1}" if lv > 1 else "inv1"))
                    if lv == 1 and i:
                        pe.wait_ge(d_dve, dve_at(i - 1, "carry"))
                    if lv == 4 and i:
                        pe.wait_ge(d_act, act_at(i - 1, "out"))
                    if lv == 5 and i + 1 < TILES:
                        pe.wait_ge(d_act, act_at(i + 1, "decay"))
                    for h in range(4):
                        last = mm(ps[:, D2, h * P:(h + 1) * P], AM[:, lv % 2, h, :], T[:, h, :], start=True, stop=True)
                    last.then_inc(d_pe, 1)
                elif piece[0] == "y":
                    lv = int(piece[1:])
                    pe.wait_ge(d_act, act_at(i, f"x{lv}"))
                    pe.wait_ge(d_dve, dve_at(i, f"y{lv - 1}" if lv > 1 else "inv1"))
                    if lv == 1 and i:
                        pe.wait_ge(d_act, act_at(i - 1, "fresh"))
                        pe.wait_ge(d_dve, dve_at(i - 1, "y6"))
                    if lv == 2 and i:
                        pe.wait_ge(d_dve, dve_at(i - 1, "emit"))
                    if lv == 4 and i + 1 < TILES:
                        pe.wait_ge(d_act, act_at(i + 1, "split"))
                    if lv == 6 and i + 1 < TILES:
                        pe.wait_ge(d_dve, dve_at(i + 1, "qkD"))
                    if lv < LEVELS - 1:
                        for h in range(4):
                            last = mm(ps[:, D0, h * P:(h + 1) * P], Tt[i % 2][:, h, :], Xs[:, h, :], start=True, stop=True)
                        last.then_inc(d_pe, 1)
                    for h in range(4):
                        last = mm(ps[:, D1, h * P:(h + 1) * P], Xs[:, h, :], Tt[i % 2][:, h, :], start=True, stop=True)
                    last.then_inc(d_pe, 1)
                elif piece == "carry":
                    if i:
                        pe.wait_ge(d_dve, dve_at(i - 1, "emit"))
                    else:
                        pe.wait_ge(pads_zero, 2)
                    if i + 1 < TILES:
                        pe.wait_ge(d_dve, dve_at(i + 1, "inv1"))
                    for m in range(2):
                        for pair in range(2):
                            last = mm(ps[:, D2, m * 256 + pair * P:m * 256 + (pair + 1) * P], tT[i % 2][:, pair, m, :],
                                      Sst[:, pair, :], start=True, stop=True)
                    last.then_inc(d_pe, 1)
                elif piece == "fresh":
                    pe.wait_ge(d_dve, dve_at(i, "carry"))
                    if i + 1 < TILES:
                        pe.wait_ge(d_dve, dve_at(i + 1, "qkD"))
                    for h in range(4):
                        last = mm(ps[:, D0, h * HD:(h + 1) * HD], Tt[i % 2][:, h, :], R[:, h * HD:(h + 1) * HD],
                                  start=True, stop=True)
                    last.then_inc(d_pe, 1)
                elif piece == "emit":
                    pe.wait_ge(d_act, act_at(i, "fresh"))
                    pe.wait_ge(d_pool, pool_at(i, "kdvb"))
                    if i + 1 < TILES:
                        pe.wait_ge(d_dve, dve_at(i + 1, "y1"))
                    for h in range(4):
                        mm(ps[:, D1, h * HD:(h + 1) * HD], qkD[i % 2][:, h, :], vn[:, h * HD:(h + 1) * HD], start=True, stop=True)
                    for pair in range(2):
                        cols = slice(pair * P, (pair + 1) * P)
                        last = mm(ps[:, D0, pair * P:(pair + 1) * P], kd[i % 2][:, cols], vn[:, cols], start=True, stop=True)
                    last.then_inc(d_pe, 1)
                elif piece == "out":
                    pe.wait_ge(d_dve, dve_at(i, "onorm"))
                    if i + 1 < TILES:
                        pe.wait_ge(d_act, act_at(i + 1, "x3"))
                    for pair in range(2):
                        last = tr(ps[:, D2, pair * P:(pair + 1) * P], o1[:, pair * P:(pair + 1) * P], ident)
                    last.then_inc(d_pe, 1)

            idx = 0
            for ev in SCHEDULE:
                if ev[0] == "v":
                    project(FIRST_V + ev[1])
                    if ev[1] == 0:
                        turn_qk(15)
                elif ev[0] == "scores":
                    n = ev[1]
                    pair, i, hh = attention_step(n)
                    if n == 0:
                        pe.wait_ge(qk_out, 16)
                        pe.wait_ge(act_took, len(STEPS) - 4)
                    rows = slice(HD * hh, HD * hh + HD)
                    pe.wait_ge(s_max, n)
                    for c0 in range(0, (i + 1) * P, 512):
                        w = min(512, (i + 1) * P - c0)
                        last = mm(ps[:, 6 + c0 // 512, 0:w], qkT[rows, 0, pair, i * P:(i + 1) * P],
                                  qkT[rows, 1, pair, c0:c0 + w], start=True, stop=True)
                    last.then_inc(s_scores, 1)
                elif ev[0] == "dn":
                    dn(ev[1], ev[2])
                elif ev[0] == "turn":
                    n = ev[1]
                    pe.wait_ge(s_exp, n + 1)
                    for g, cnt in turn_groups(n):
                        if idx >= 2:
                            pe.wait_ge(*taken(idx - 2))
                        for c in range(cnt):
                            last = tr(ps[:, TB + idx % 2, c * P:(c + 1) * P], prob[:, n % 2, (g + c) * P:(g + c + 1) * P], ident)
                        last.then_inc(s_turn, 1)
                        idx += 1
                elif ev[0] == "values":
                    n = ev[1]
                    pair, i, hh = attention_step(n)
                    if n % 8 == 0 and n:
                        pe.wait_ge(s_att, n // 8)
                    for who in range(first_turn[("p", n)], last_turn[("p", n)] + 1):
                        pe.wait_ge(*taken(who))
                    for b in range(i + 1):
                        last = mm(ps[:, PV, n % 8 * HD:(n % 8 + 1) * HD], probT[:, n % 2, b * P:(b + 1) * P],
                                  v_tok[:, b, pair * P + hh * HD:pair * P + (hh + 1) * HD], start=(b == 0), stop=(b == i))
                    last.then_inc(s_values, 1)
                elif ev[0] == "att_out":
                    i = ev[1]
                    pe.wait_ge(s_att, i + 1)
                    pe.wait_ge(*taken(idx - 2))
                    for c in range(4):
                        last = tr(ps[:, TB + idx % 2, c * P:(c + 1) * P], att[:, c * P:(c + 1) * P], ident)
                    last.then_inc(s_turn, 1)
                    idx += 1

            pe.wait_ge(w_out_in, 16 * KC)
            pe.wait_ge(d_act, len(ACT_ORDER))
            pe.wait_ge(cv_out, 2)

            def out_rows(t):
                if t >= 2:
                    pe.wait_ge(x2_done, t - 1)
                for half in range(2):
                    for k in range(KC):
                        last = mm(ps[:, 2 * (t % 2) + half, :], mixT[k][:, t * P:(t + 1) * P],
                                  w_out[k][:, half * 512:(half + 1) * 512], start=(k == 0), stop=(k == KC - 1))
                last.then_inc(out_mm, 1)

            def turn_h2(t):
                pe.wait_ge(h2_done, t + 1)
                if t:
                    pe.wait_ge(h2T_done, t)
                for k in range(KC):
                    last = tr(ps[:, 4 + k // 4, (k % 4) * P:(k % 4 + 1) * P], h2s[:, t % 2, k * P:(k + 1) * P], ident)
                last.then_inc(h2_turned, 1)

            def logits_of(t):
                pe.wait_ge(h2T_done, t + 1)
                if t == 0:
                    pe.wait_ge(ffn_in, 32)
                if t >= 2:
                    pe.wait_ge(list_v, 2 * (t - 1))
                elif t:
                    pe.wait_ge(logit_sb, t)
                for k in range(KC):
                    last = mm(ps[:, 6, 0:36], h2T[:, t % 2, k, :], router[:, k, :], start=(k == 0), stop=(k == KC - 1))
                last.then_inc(logit_mm, 1)

            def ranks_of(t):
                pe.wait_ge(hots_done, t + 1)
                pe.wait_ge(logit_sb, min(t + 2, TILES))
                if t:
                    pe.wait_ge(list_v, 2 * t)
                mm(ps[:, 6, 64:96], tri, hots[:, t, :], start=True, stop=False)
                last = mm(ps[:, 6, 64:96], ones, before[:, t, :], start=False, stop=True)
                if t == TILES - 1:
                    mm(ps[:, 6, 96:128], ones, hots[:, t, :], start=True, stop=False)
                    last = mm(ps[:, 6, 96:128], ones, before[:, t, :], start=False, stop=True)
                last.then_inc(rank_mm, 1)

            def list_of(t):
                for m in (2 * t, 2 * t + 1):
                    pe.wait_ge(list_v, m + 1)
                    mm(ps[:, 7, 0:256], r_hot[:, m % 2, :], r_val[:, m % 2, :], start=(m == 0), stop=(m == 2 * TILES - 1))\
                        .then_inc(list_mm, 1)

            mixT = [mixT_dn[:, 0], mixT_dn[:, 1]] + [mixT_at[:, c] for c in range(4)] + [mixT_cv[:, 0], mixT_cv[:, 1]]
            for t in range(TILES + 4):
                for stage_of, behind in ((out_rows, 0), (logits_of, 2), (list_of, 4), (ranks_of, 3), (turn_h2, 1)):
                    if 0 <= t - behind < TILES:
                        stage_of(t - behind)

            def turn_rows(slot, u, pair):
                pe.wait_ge(rows_in[u], 16 * (pair + 1))
                at_least(pe, rowsT_a, slot)
                at_least(pe, rowsT_v, slot)
                for k in range(KC):
                    last = tr(ps[:, k // 4, (k % 4) * P:(k % 4 + 1) * P], hg[:, u, k * P:(k + 1) * P], ident)
                last.then_inc(rows_turned, 1)

            def gate_up(slot, u, pair):
                pe.wait_ge(rowsT_a, slot + 1)
                pe.wait_ge(rowsT_v, slot + 1)
                pe.wait_ge(gu_in[u], 32 * (pair + 1))
                at_least(pe, act_done, slot)
                for k in range(KC):
                    mm(ps[:, 2, :], hgT[:, u, k, :], w_gate[u][:, k, :], start=(k == 0), stop=(k == KC - 1))
                for k in range(KC):
                    last = mm(ps[:, 3, :], hgT[:, u, k, :], w_up[u][:, k, :], start=(k == 0), stop=(k == KC - 1))
                last.then_inc(gu_mm, 1)

            def turn_act(slot):
                pe.wait_ge(act_done, slot + 1)
                at_least(pe, actT_done, slot)
                for k in range(FC):
                    last = tr(ps[:, 4, k * P:(k + 1) * P], act_g[:, k * P:(k + 1) * P], ident)
                last.then_inc(act_turned, 1)

            def down(slot, u, pair):
                pe.wait_ge(actT_done, slot + 1)
                pe.wait_ge(down_in[u], 16 * (pair + 1))
                at_least(pe, y_a, slot)
                at_least(pe, y_v, slot)
                for half in range(2):
                    for k in range(FC):
                        last = mm(ps[:, 5 + half, :], actT[:, k, :], w_down[u][:, k, half * 512:(half + 1) * 512],
                                  start=(k == 0), stop=(k == FC - 1))
                last.then_inc(down_mm, 1)

            def expert(slot, u, pair):
                gate_up(slot, u, pair)
                turn_rows(slot + 1, 1 - u, pair + u)
                if not (isinstance(slot, int) and slot == 0):
                    down(slot - 1, 1 - u, pair + u - 1)
                turn_act(slot)

            pe.wait_ge(slots_ready, 1)
            turn_rows(0, 0, 0)
            experts_loop(pe, expert)
            pe.wait_ge(extras_ready, 1)
            extras_loop(pe, expert, down)

        @block.vector
        def _(v):
            tt, ts, stt = nc.vector.tensor_tensor, nc.vector.tensor_scalar, nc.vector.scalar_tensor_tensor
            nc.vector.memset(ypad[:, :, 0:30], 0.0)
            nc.vector.memset(dpad[:, :, 0:3], 0.0).then_inc(pads_zero, 1)

            def take_hT(t):
                for half in range(2):
                    v.wait_ge(hT_turned, 2 * t + half + 1)
                    k0 = 4 * half
                    tt(hT[:, k0:k0 + 4, t * P:(t + 1) * P], ps[:, 2 * (t % 2) + half, :].rearrange("p (k n) -> p k n", k=4),
                       bc_h(par[:, P_GMIX + k0:P_GMIX + k0 + 4], P), ALU.mult).then_inc(hT_done, 1)

            v.wait_ge(params_in, 16)
            v.wait_ge(consts_in, 16)
            for t in range(TILES):
                take_hT(t)

            for n, (g, kind, c, m) in enumerate(STEPS):
                if kind == "glu":
                    v.wait_ge(proj_done, n + 1)
                    v.wait_ge(act_took, 4)
                    tt(ypad[:, c, 30 + m * 512:30 + (m + 1) * 512], ps[:, n % 4, :], yc[:, c, m * 512:(m + 1) * 512],
                       ALU.mult).then_inc(dve_took, 1)
            v.wait_ge(dve_took, 4)
            for c in range(2):
                ts(yc[:, c, :], ypad[:, c, 0:SEQ], par[:, P_CVW + c * CV_TAPS:P_CVW + c * CV_TAPS + 1],
                   par[:, P_CVB + c:P_CVB + c + 1], ALU.mult, ALU.add).then_inc(tap_done, 1)
            for tap in range(1, CV_TAPS):
                for c in range(2):
                    v.wait_ge(tap_done, 2 * tap + c - 1)
                    col = P_CVW + c * CV_TAPS + tap
                    stt(yc[:, c, :], ypad[:, c, tap:tap + SEQ], par[:, col:col + 1], yc[:, c, :],
                        ALU.mult, ALU.add).then_inc(tap_done, 1)
            v.wait_ge(cv_mean, 1)
            for half in range(2):
                for c in range(2):
                    seg = yc[:, c, half * 512:(half + 1) * 512]
                    last = stt(seg, ps[:, 6 + half, :], -1.0 / CV_W, seg, ALU.mult, ALU.add)
            last.then_inc(cv_centred, 1)

            def dn_conv(c):
                v.wait_ge(*act_taken(8 + 2 * c + 1))
                v.wait_ge(bias_out, 16)
                w0 = P_DNW + c * DN_TAPS
                ts(dconv[:, c, :], dpad[:, c, 0:SEQ], par[:, w0:w0 + 1], None, ALU.mult)
                for tap in range(1, DN_TAPS):
                    nc.vector.drain()
                    last = stt(dconv[:, c, :], dpad[:, c, tap:tap + SEQ], par[:, w0 + tap:w0 + tap + 1], dconv[:, c, :],
                               ALU.mult, ALU.add)
                last.then_inc(dn_tapped, 1)

            dn_conv(0)
            dn_conv(1)
            v.wait_ge(cv_var, 1)
            for half in range(2):
                ts(junk[:, half * 512:(half + 1) * 512], ps[:, 6 + half, :], 1.0 / CV_W, EPS, ALU.mult, ALU.add)
            nc.vector.drain()
            nc.vector.reciprocal(junk, junk).then_inc(cv_varsb, 1)
            for c in range(2, 6):
                dn_conv(c)
            v.wait_ge(cv_rstd, 1)
            tt(yc, yc, bc_f(junk, 2), ALU.mult).then_inc(cv_normed, 1)
            v.wait_ge(act_took, 4 + 8 + 4 + 8)
            tt(zg.rearrange("p t (h d) -> p (t h) d", d=HD), zg.rearrange("p t (h d) -> p (t h) d", d=HD),
               bc_f(par[:, P_ON:P_ON + HD], TILES * DN_HEADS), ALU.mult).then_inc(zg_done, 1)
            a8 = ab[:, :, 0:4]
            b8 = ab[:, :, 4:8]
            g3, beta3, t13, t23, t33 = (x.rearrange("p (t h) -> p t h", h=4) for x in (g_col, beta, t1, t2, t3))
            tt(t13, a8, bc_f(par[:, P_DT:P_DT + 4], TILES), ALU.add)
            nc.vector.drain()
            stt(t23, t13, -1.0, t13, ALU.mult, ALU.min)
            v.wait_ge(act_took, 4 + 8 + 4 + 8)
            nc.vector.tensor_copy(t33, b8)
            nc.vector.drain().then_inc(gate_v, 1)
            for j in range(16):
                if j == 4:
                    v.wait_ge(gate_a, 2)
                    stt(t13, t13, 0.0, t23, ALU.max, ALU.add)
                    ts(t3, t3, 1.0, None, ALU.add)
                    nc.vector.drain().then_inc(gate_v, 1)
                    nc.vector.reciprocal(beta, t3)
                    stt(g3, t13, -1.0, bc_f(ea, TILES), ALU.mult, ALU.mult)
                    nc.vector.drain().then_inc(gate_v, 2)
                if j == 8:
                    v.wait_ge(cv_mean, 2)
                    nc.vector.tensor_copy(Gc, ps[:, 6, 0:32])
                    nc.vector.tensor_copy(Gtot, ps[:, 6, 32:64])
                    nc.vector.drain()
                    tt(ekd, Gtot, Gc, ALU.subtract)
                    ts(negG, Gc, -1.0, None, ALU.mult)
                    nc.vector.drain().then_inc(gate_v, 1)
                v.wait_ge(qk_sq, j + 1)
                nc.vector.tensor_reduce(ss2[:, j % 2, :], sqb.rearrange("p (h d) -> p h d", d=HD), AX.X, ALU.add)
                nc.vector.drain()
                if j < 8:
                    ts(ss2[:, j % 2, :], ss2[:, j % 2, :], HD * EPS, None, ALU.add).then_inc(qk_ss, 1)
                else:
                    ts(ss2[:, j % 2, :], ss2[:, j % 2, :], 1.0 / HD, EPS, ALU.mult, ALU.add).then_inc(qk_ss, 1)
                v.wait_ge(qk_rs, j + 1)
                s3 = stage[:, j % 2, :].rearrange("p (h d) -> p h d", d=HD)
                tt(s3, s3, bc_h(rs2[:, j % 2, :]), ALU.mult).then_inc(qk_normed, 1)
            v.wait_ge(gate_a, 5)
            e3 = egl_all.rearrange("p (t c two) -> p t c two", two=2, c=2)
            nc.vector.tensor_copy(egl[0:HD], e3[0:HD, :, :, 0])
            nc.vector.tensor_copy(egl[HD:P], e3[HD:P, :, :, 1])
            nc.vector.memset(Sst, 0.0)
            nc.vector.drain().then_inc(pads_zero, 1)

            def dn(i, k):
                if k >= len(DN_PIECES):
                    return
                piece = DN_PIECES[k]
                ti = slice(4 * i, 4 * i + 4)
                if piece == "ss":
                    v.wait_ge(d_pool, pool_at(i, "sq"))
                    nc.vector.tensor_reduce(dss, dsq.rearrange("p (h d) -> p h d", d=HD), AX.X, ALU.add)
                    nc.vector.drain()
                    ts(dss[:, 4:8], dss[:, 4:8], EPS, None, ALU.add)
                    ts(dss[:, 0:4], dss[:, 0:4], EPS, float(HD), ALU.add, ALU.mult)
                    nc.vector.drain().then_inc(d_dve, 1)
                elif piece == "qkn":
                    v.wait_ge(d_pool, pool_at(i, "rs"))
                    t8 = tok[:, 0:512].rearrange("p (h d) -> p h d", d=HD)
                    tt(t8, t8, bc_h(drs), ALU.mult).then_inc(d_dve, 1)
                elif piece == "gram":
                    v.wait_ge(d_pe, pe_at(i, "gram"))
                    v.wait_ge(d_act, act_at(i, "decay"))
                    if i:
                        v.wait_ge(d_pool, pool_at(i - 1, f"am{LEVELS - 1}"))
                    both = ps[:, 0:2, :].rearrange("p b (c m n) -> p b c m n", m=2, n=P)
                    of_bank = lambda x: x.rearrange("p (c b) n -> p b c n", b=2)
                    tt(of_bank(At), both[:, :, :, 0, :], of_bank(dI), ALU.mult)
                    nc.vector.drain().then_inc(d_dve, 1)
                    tt(AM[:, 0], At, bc_f(lvl(0), 4), ALU.mult).then_inc(d_dve, 1)
                    tt(of_bank(qkD[i % 2]), both[:, :, :, 1, :], of_bank(dI), ALU.mult)
                    nc.vector.drain().then_inc(d_dve, 1)
                elif piece == "inv1":
                    v.wait_ge(d_pe, pe_at(i, "inv1"))
                    tt(T, bc_f(ident, 4), ps[:, 2, :].rearrange("p (h n) -> p h n", h=4), ALU.subtract)
                    tt(Tt[i % 2], bc_f(ident, 4), AM[:, 0], ALU.subtract)
                    nc.vector.drain().then_inc(d_dve, 1)
                elif piece[0] == "y":
                    lv = int(piece[1:])
                    if lv < LEVELS - 1:
                        v.wait_ge(d_pe, pe_at(i, f"T{lv}"))
                        tt(T, T, ps[:, 0, :].rearrange("p (h n) -> p h n", h=4), ALU.subtract).then_inc(d_dve, 1)
                    v.wait_ge(d_pe, pe_at(i, piece))
                    tt(Tt[i % 2], Tt[i % 2], ps[:, 1, :].rearrange("p (h n) -> p h n", h=4), ALU.subtract)
                    nc.vector.drain().then_inc(d_dve, 1)
                elif piece == "carry":
                    v.wait_ge(d_pe, pe_at(i, "carry"))
                    v.wait_ge(d_pool, pool_at(i, "kdvb"))
                    h4 = lambda x: x.rearrange("p (h d) -> p h d", d=HD)
                    tt(h4(tmp), h4(ps[:, 2, 0:256]), bc_h(eG[:, ti]), ALU.mult)
                    tt(h4(o1), h4(ps[:, 2, 256:512]), bc_h(eG[:, ti]), ALU.mult)
                    nc.vector.drain()
                    tt(R, vb[i % 2], tmp, ALU.subtract).then_inc(d_dve, 1)
                elif piece == "emit":
                    v.wait_ge(d_pe, pe_at(i, "emit"))
                    tt(tmp.rearrange("p (c n) -> p c n", c=2), ps[:, 0, 0:256].rearrange("p (c n) -> p c n", c=2),
                       bc_f(bd, 2), ALU.mult)
                    tt(o1, ps[:, 1, 0:256], o1, ALU.add)
                    nc.vector.drain()
                    for pair in range(2):
                        stt(Sst[:, pair, :], Sst[:, pair, :], egl[:, i, pair:pair + 1], tmp[:, pair * P:(pair + 1) * P],
                            ALU.mult, ALU.add)
                    nc.vector.drain().then_inc(d_dve, 1)
                elif piece == "osum":
                    v.wait_ge(d_pool, pool_at(i, "osq"))
                    nc.vector.tensor_reduce(dss[:, 0:4], dsq[:, 0:256].rearrange("p (h d) -> p h d", d=HD), AX.X, ALU.add)
                    nc.vector.drain()
                    ts(dss[:, 0:4], dss[:, 0:4], 1.0 / HD, EPS, ALU.mult, ALU.add).then_inc(d_dve, 1)
                    tt(o1, o1, zg[:, i, :], ALU.mult)
                elif piece == "onorm":
                    nc.vector.drain()
                    v.wait_ge(d_pool, pool_at(i, "ors"))
                    o3 = o1.rearrange("p (h d) -> p h d", d=HD)
                    tt(o3, o3, bc_h(drs[:, 0:4]), ALU.mult).then_inc(d_dve, 1)

            v.wait_ge(qk_turned, 16)
            idx = 0
            for ev in SCHEDULE:
                if ev[0] == "scores":
                    n = ev[1]
                    pair, i, hh = attention_step(n)
                    L = (i + 1) * P
                    v.wait_ge(slab_in[pair % 2], 16 * (pair // 2 + 1))
                    if n == 0:
                        v.wait_ge(proj_done, len(STEPS))
                    v.wait_ge(s_scores, n + 1)
                    if n >= 2:
                        v.wait_ge(s_turn, first_turn[("p", n - 1)])
                        v.wait_ge(s_exp, n - 1)
                    scores = ps[:, 6:8, :].rearrange("p b n -> p (b n)")[:, 0:L]
                    nc.vector.tensor_tensor_reduce(prob[:, n % 2, 0:L], scores, slab[:, pair % 2, hh, 896 - i * P:896 - i * P + L],
                                                   1.0, -3e38, ALU.add, ALU.max, mx[:, n % 2:n % 2 + 1])
                    nc.vector.drain()
                    ts(nmx[:, n % 2:n % 2 + 1], mx[:, n % 2:n % 2 + 1], -1.0, None, ALU.mult).then_inc(s_max, 1)
                elif ev[0] == "dn":
                    dn(ev[1], ev[2])
                elif ev[0] == "turn":
                    n = ev[1]
                    for g, cnt in turn_groups(n):
                        if TAKER[idx] == "v":
                            v.wait_ge(s_turn, idx + 1)
                            if n >= 2:
                                v.wait_ge(s_values, n - 1)
                            nc.vector.tensor_copy(probT[:, n % 2, g * P:(g + cnt) * P], ps[:, 4 + idx % 2, 0:cnt * P])\
                                .then_inc(s_turned_v, 1)
                        idx += 1
                elif ev[0] == "values":
                    n = ev[1]
                    if n % 8 == 7:
                        v.wait_ge(s_values, n + 1)
                        v.wait_ge(s_exp, n + 1)
                        if n > 8:
                            v.wait_ge(s_turn, first_turn[("o", n // 8 - 1)] + 1)
                        nc.vector.reciprocal(rZ, Z[:, n // 8 % 2, :])
                        nc.vector.drain()
                        tt(att.rearrange("p (h d) -> p h d", d=HD), ps[:, 3, :].rearrange("p (h d) -> p h d", d=HD),
                           bc_h(rZ), ALU.mult).then_inc(s_att, 1)
                elif ev[0] == "att_out":
                    i = ev[1]
                    if TAKER[idx] == "v":
                        v.wait_ge(s_turn, idx + 1)
                        nc.vector.tensor_copy(att_place(i), flipped(ps[:, 4 + idx % 2, :].rearrange("p (c n) -> p c n", c=4)))\
                            .then_inc(s_turned_v, 1)
                    idx += 1

            v.wait_ge(ffn_in, 32)
            v.wait_ge(params_in, 16)

            def residual(t):
                v.wait_ge(out_mm, t + 1)
                v.wait_ge(xs_in[t % 2], 16 * (t // 2 + 1))
                tt(xs[:, t % 2, :], ps[:, 2 * (t % 2):2 * (t % 2) + 2, :].rearrange("p b n -> p (b n)"), xs[:, t % 2, :],
                   ALU.add).then_inc(x2_done, 1)

            def gained(t):
                v.wait_ge(x2_rs, t + 1)
                if t >= 2:
                    v.wait_ge(h2_turned, t - 1)
                    v.wait_ge(h2_out[t % 2], 16 * (t // 2))
                stt(h2s[:, t % 2, :], xs[:, t % 2, :], rs[:, t:t + 1], g_ffn, ALU.mult, ALU.mult).then_inc(h2_done, 1)

            def choose(t):
                v.wait_ge(logit_mm, t + 1)
                tt(logits[:, t, :], ps[:, 6, 0:36], par[:, P_RBIAS:P_RBIAS + 36], ALU.add)
                nc.vector.drain().then_inc(logit_sb, 1)
                nc.vector.tensor_copy(padded[:, t, 0:4], logits[:, t, 0:4])
                nc.vector.drain()
                nc.vector.max(gtop[:, t, :], padded[:, t, :])
                nc.vector.drain()
                nc.vector.max_index(gtop_i[:, t, :], gtop[:, t, :], padded[:, t, :])
                if t:
                    tt(before[:, t, :], before[:, t - 1, :], hots[:, t - 1, :], ALU.add)
                nc.vector.drain()
                nc.vector.tensor_copy(g_idx[:, t:t + 1], gtop_i[:, t, 0:1])
                nc.vector.drain()
                tt(g_hot[:, t, :], cst[:, C_J:C_J + 4], g_idx[:, t:t + 1].to_broadcast([P, 4]), ALU.is_equal)
                nc.vector.drain()
                ts(g_hot[:, t, :], g_hot[:, t, :], -1.0, -NEG, ALU.add, ALU.mult)
                nc.vector.drain()
                tt(em[:, t, :].rearrange("p (g e) -> p g e", g=4), logits[:, t, 4:36].rearrange("p (g e) -> p g e", g=4),
                   bc_h(g_hot[:, t, :], 8), ALU.add)
                nc.vector.drain()
                nc.vector.max(etop[:, t, :], em[:, t, :])
                nc.vector.drain()
                nc.vector.max_index(etop_i[:, t, :], etop[:, t, :], em[:, t, :])
                nc.vector.drain()
                nc.vector.tensor_copy(e_idx[:, :, t], etop_i[:, t, 0:2])
                nc.vector.drain()
                tt(hot[:, :, t, :], bc_f(cst[:, C_E:C_E + EXPERTS], 2), bc_h(e_idx[:, :, t], EXPERTS), ALU.is_equal)
                nc.vector.drain()
                tt(hots[:, t, :], hot[:, 0, t, :], hot[:, 1, t, :], ALU.add)
                nc.vector.drain().then_inc(hots_done, 1)

            def place(t):
                v.wait_ge(rank_mm, t + 1)
                tt(rtmp, bc_f(ps[:, 6, 64:96], 2), hot[:, :, t, :], ALU.mult)
                if t == TILES - 1:
                    nc.vector.tensor_copy(e_count, ps[:, 6, 96:128])
                nc.vector.drain()
                nc.vector.tensor_reduce(rk_k[:, :, t], rtmp, AX.X, ALU.add)
                nc.vector.drain()
                ts(rk_k[:, :, t], rk_k[:, :, t], -1.0, None, ALU.add)
                nc.vector.drain()
                tt(jhot[:, :, t, :], bc_h(rk_k[:, :, t], 8), bc_f(cst[:, C_J128:C_J128 + 8], 2), ALU.is_ge)
                nc.vector.drain()
                nc.vector.tensor_reduce(jn[:, :, t], jhot[:, :, t, :], AX.X, ALU.add)
                nc.vector.drain()
                ts(jn[:, :, t], jn[:, :, t], -1.0, None, ALU.add)
                nc.vector.drain()
                stt(rmod[:, :, t], jn[:, :, t], -float(P), rk_k[:, :, t], ALU.mult, ALU.add)
                tt(jhot[:, :, t, :], bc_h(jn[:, :, t], 8), bc_f(cst[:, C_J:C_J + 8], 2), ALU.is_equal)
                nc.vector.drain()
                for c in range(2):
                    stt(jhot[:, c, t, :], cst[:, C_TOK + t:C_TOK + t + 1].to_broadcast([P, 8]), float(c * SEQ + 1),
                        jhot[:, c, t, :], ALU.add, ALU.mult)
                nc.vector.drain()
                if t:
                    v.wait_ge(list_mm, 2 * t)
                for c in range(2):
                    ts(r_hot[:, c, :], cst[:, C_IOTA:C_IOTA + P], rmod[:, c, t:t + 1], None, ALU.is_equal)
                    tt(r_val[:, c, :].rearrange("p (e j) -> p e j", j=8), bc_h(hot[:, c, t, :], 8),
                       bc_f(jhot[:, c, t, :], EXPERTS), ALU.mult)
                    nc.vector.drain().then_inc(list_v, 1)

            nc.vector.memset(padded, -3e38)
            nc.vector.memset(before[:, 0, :], 0.0)
            nc.vector.memset(zero256, 0.0)
            nc.vector.drain()
            for t in range(TILES + 3):
                for stage_of, behind in ((residual, 0), (choose, 2), (place, 3), (gained, 0)):
                    if 0 <= t - behind < TILES:
                        stage_of(t - behind)
                if t == TILES - 1:
                    nc.vector.memset(hg, 0.0).then_inc(hg_zero, 1)
                if t == TILES + 1:
                    tt(gexp, logits[:, :, 0:4], gtop[:, :, 0:1].to_broadcast([P, TILES, 4]), ALU.subtract)
                    tt(e_diff, etop[:, :, 1], etop[:, :, 0], ALU.subtract)
                    nc.vector.drain().then_inc(route_v, 1)

            tt(active.rearrange("p (e j) -> p e j", j=8), bc_h(e_count, 8), bc_f(cst[:, C_THR:C_THR + 8], EXPERTS), ALU.is_gt)
            nc.vector.drain()
            nc.vector.tensor_tensor_scan(slot_of, active, zero256, 0.0, ALU.add, ALU.add)
            nc.vector.drain()
            nc.vector.tensor_copy(n_ov[:, 0:1], slot_of[:, 255:256])
            nc.vector.drain()
            tt(slot_of, slot_of, active, ALU.mult)

            def rows_of_blocks(first, last):
                b = slice(first, last)
                ts(slots[:, b], slots[:, b], -1.0, None, ALU.add)
                nc.vector.drain()
                ts(tok_f[:, b], slots[:, b], float(SEQ), -float(SEQ), ALU.is_ge, ALU.mult)
                ts(dst_f[:, b], slots[:, b], 0.0, 4.0 * SEQ, ALU.is_lt, ALU.mult)
                nc.vector.drain()
                tt(dst_f[:, b], dst_f[:, b], slots[:, b], ALU.add)
                nc.vector.drain()
                tt(tok_f[:, b], tok_f[:, b], dst_f[:, b], ALU.add)
                nc.vector.drain()
                nc.vector.tensor_copy(tok_of[:, b], tok_f[:, b])
                nc.vector.tensor_copy(dst_of[:, b], dst_f[:, b])

            v.wait_ge(list_mm, 2 * TILES)
            nc.vector.tensor_copy(code, ps[:, 7, 0:256])
            nc.vector.drain()
            nc.vector.tensor_copy(slots[:, 0:EXPERTS], code.rearrange("p (e j) -> p e j", j=8)[:, :, 0])
            nc.vector.drain()
            rows_of_blocks(0, EXPERTS)
            nc.vector.drain().then_inc(slots_ready, 1)

            def overflow():
                for m in range(EXTRA):
                    stt(otmp, slot_of, float(m + 1), code, ALU.is_equal, ALU.mult, accum_out=slots[:, EXPERTS + m:EXPERTS + m + 1])
                    nc.vector.drain()
                    stt(otmp, slot_of, float(m + 1), cst[:, C_EJ:C_EJ + 256], ALU.is_equal, ALU.mult, accum_out=ov_e_f[:, m + 1:m + 2])
                    nc.vector.drain()
                nc.vector.memset(ov_e_f[:, 0:1], float(EXPERTS - 1))
                nc.vector.drain()
                nc.vector.tensor_copy(ov_e, ov_e_f)
                rows_of_blocks(EXPERTS, SLOTS)
                nc.vector.drain().then_inc(extras_ready, 1)
                v.wait_ge(route_a, 1)
                nc.vector.tensor_reduce(p_grp, gexp, AX.X, ALU.add)
                ts(gates[:, 0, :], e_diff, 1.0, None, ALU.add)
                nc.vector.drain()
                tt(gates[:, 0, :], gates[:, 0, :], p_grp, ALU.mult)
                nc.vector.drain()
                nc.vector.reciprocal(gates[:, 0, :], gates[:, 0, :])
                nc.vector.drain()
                tt(gates[:, 1, :], gates[:, 0, :], e_diff, ALU.mult)

            def rowsT(slot, u):
                v.wait_ge(rows_turned, slot + 1)
                at_least(v, gu_mm, slot - 1)
                nc.vector.tensor_copy(hgT[:, u, 4:8, :], ps[:, 1, :].rearrange("p (k n) -> p k n", k=4)).then_inc(rowsT_v, 1)

            def product(slot):
                v.wait_ge(silu_done, slot + 1)
                at_least(v, act_turned, slot)
                tt(act_g, silu_g, ps[:, 3, :], ALU.mult).then_inc(act_done, 1)

            def result(slot, u, pair):
                v.wait_ge(down_mm, slot + 1)
                at_least(v, y_out[u], pair * 16)
                nc.vector.tensor_copy(ys[:, u, 512:1024], ps[:, 6, :]).then_inc(y_v, 1)

            def expert(slot, u, pair):
                product(slot)
                rowsT(slot + 1, 1 - u)
                if not (isinstance(slot, int) and slot == 0):
                    result(slot - 1, 1 - u, pair + u - 1)

            rowsT(0, 0)
            overflow()
            experts_loop(v, expert)
            extras_loop(v, expert, result)
            v.wait_ge(x2_back, 16 * TILES)
            for t in range(TILES):
                v.wait_ge(final_in[t], 32)
                x_t = fx[:, t, :]
                stt(x_t, fy[0][:, t, :], gates[:, 0, t:t + 1], x_t, ALU.mult, ALU.add)
                nc.vector.drain()
                stt(x_t, fy[1][:, t, :], gates[:, 1, t:t + 1], x_t, ALU.mult, ALU.add).then_inc(final_v, 1)

        @block.scalar
        def _(act):
            f = nc.scalar.activation
            act.dma_start(par, a["params"]).then_inc(params_in, 16)

            def scaled(t):
                act.wait_ge(rms_done, t + 1)
                f(x_all[:, t, :], x_all[:, t, :], ACT.Copy, scale=rs[:, t:t + 1]).then_inc(h_scaled, 1)

            for t in range(TILES):
                act.wait_ge(x_in[t], 16)
                act.wait_ge(sumsq_done, t)
                f(junk, x_all[:, t, :], ACT.Square, accum_out=ss[:, t:t + 1]).then_inc(sumsq_done, 1)
                if t >= 2:
                    scaled(t - 2)
            scaled(TILES - 2)
            scaled(TILES - 1)
            act.wait_ge(table_mm, 1)
            f(bvec[0:AT_HEADS, :].rearrange("p (c n) -> p c n", c=3), ps[0:AT_HEADS, 5:8, 0:384], ACT.Copy).then_inc(table_sb, 1)
            act.wait_ge(table_sb, 1)
            act.dma_start(bias_dram, bvec[0:AT_HEADS, :]).then_inc(bias_out, 16)

            def put_qk(j):
                act.wait_ge(qk_turned, j + 1)
                col = P_QN + j // 8
                turned = ps[:, 4 + j % 2, :].rearrange("p (c n) -> p c n", c=4)
                f(qkT[:, j // 8, :, (j % 8) * P:(j % 8 + 1) * P], flipped(turned) if j < TILES else turned,
                  ACT.Copy, scale=par[:, col:col + 1]).then_inc(qk_out, 1)

            def take_v(t):
                act.wait_ge(proj_done, FIRST_V + t + 1)
                f(v_tok[:, t, :], ps[:, (6, 7, 3)[t % 3], :], ACT.Copy).then_inc(act_took, 1)

            act.wait_ge(pads_zero, 1)
            for n, (g, kind, c, m) in enumerate(STEPS[:FIRST_V]):
                if kind == "glu":
                    continue
                act.wait_ge(proj_done, n + 1)
                bank = ps[:, n % 4, :]
                if kind == "gate":
                    last = f(yc[:, c, m * 512:(m + 1) * 512], bank, ACT.Sigmoid)
                elif kind == "dn":
                    last = f(dpad[:, c, 3 + m * 512:3 + (m + 1) * 512], bank, ACT.Copy)
                elif kind == "z":
                    f(ab[:, m, :], bank[:, 256:264], ACT.Copy)
                    last = f(zg[:, m, :], bank[:, 0:256], ACT.Silu)
                else:
                    j = n - FIRST_QK
                    if j >= 2:
                        act.wait_ge(qk_turned, j - 1)
                    last = f(stage[:, j % 2, :], bank, ACT.Copy)
                last.then_inc(act_took, 1)
                if n > FIRST_QK and n - FIRST_QK - 1 < 16:
                    put_qk(n - FIRST_QK - 1)
                if n == 20:
                    act.wait_ge(cv_centred, 1)
                    for c2 in range(2):
                        f(ypad[:, c2, 0:SEQ], yc[:, c2, :], ACT.Square).then_inc(cv_squared, 1)
                if n == 23:
                    act.wait_ge(cv_varsb, 1)
                    f(junk, junk, ACT.Sqrt).then_inc(cv_rstd, 1)
                if n == FIRST_QK + 2:
                    act.wait_ge(gate_v, 1)
                    f(t2, t2, ACT.Exp)
                    f(t3, t3, ACT.Exp, scale=-1.0)
                    f(ea, par[:, P_ALOG:P_ALOG + 4], ACT.Exp).then_inc(gate_a, 1)
                    act.wait_ge(gate_a, 1)
                    f(t2, t2, ACT.Ln, bias=1.0).then_inc(gate_a, 1)
                if n == FIRST_QK + 13:
                    act.wait_ge(gate_v, 5)
                    f(eG, Gc, ACT.Exp).then_inc(gate_a, 1)
                    f(ekd, ekd, ACT.Exp).then_inc(gate_a, 1)
                    f(egl_all, Gtot, ACT.Exp).then_inc(gate_a, 1)
                if FIRST_QK + 4 <= n < FIRST_QK + 10:
                    c2 = n - FIRST_QK - 4
                    act.wait_ge(dn_tapped, c2 + 1)
                    f(dconv[:, c2, :], dconv[:, c2, :], ACT.Silu).then_inc(dn_silu, 1)
                if n == FIRST_QK + 11:
                    act.wait_ge(cv_normed, 1)
                    for c2 in range(2):
                        f(yc[:, c2, :], yc[:, c2, :], ACT.Silu, scale=par[:, P_LNG + c2:P_LNG + c2 + 1],
                          bias=par[:, P_LNB + c2:P_LNB + c2 + 1]).then_inc(cv_out, 1)

            def dn(i, k):
                if k >= len(DN_PIECES):
                    return
                piece = DN_PIECES[k]
                if piece == "split":
                    act.wait_ge(d_pe, pe_at(i, "split"))
                    if i:
                        act.wait_ge(d_pe, pe_at(i - 1, "norm"))
                        act.wait_ge(d_pool, pool_at(i - 1, "kdvb"))
                    f(tok[:, 0:512], ps[:, 0, :], ACT.Copy)
                    f(tok[:, 512:768], ps[:, 1, 0:256], ACT.Copy).then_inc(d_act, 1)
                    act.wait_ge(d_pe, pe_at(i, "gb"))
                    if i:
                        act.wait_ge(d_dve, dve_at(i - 1, "qkD"))
                    for h in range(4):
                        last = f(dI[:, h, :], ps[:, 2, h * P:(h + 1) * P], ACT.Exp, bias=negG[:, 4 * i + h:4 * i + h + 1])
                    last.then_inc(d_act, 1)
                elif piece == "norm":
                    act.wait_ge(d_pe, pe_at(i, "norm"))
                    if i:
                        act.wait_ge(d_pe, pe_at(i - 1, "norm"))
                    if i >= 2:
                        act.wait_ge(d_pe, pe_at(i - 2, "carry"))
                    f(tT[i % 2].rearrange("p c m n -> p c (m n)"), ps[:, 0:2, 0:384], ACT.Copy).then_inc(d_act, 1)
                elif piece[0] == "x":
                    act.wait_ge(d_pe, pe_at(i, piece))
                    f(Xs.rearrange("p h n -> p (h n)"), ps[:, 2, :], ACT.Copy).then_inc(d_act, 1)
                elif piece == "fresh":
                    act.wait_ge(d_pe, pe_at(i, "fresh"))
                    f(vn, ps[:, 0, 0:256], ACT.Copy).then_inc(d_act, 1)
                elif piece == "out":
                    act.wait_ge(d_pe, pe_at(i, "out"))
                    f(mixT_dn[:, :, i * P:(i + 1) * P], ps[:, 2, 0:256].rearrange("p (c n) -> p c n", c=2),
                      ACT.Copy).then_inc(d_act, 1)

            idx = 0
            for ev in SCHEDULE:
                if ev[0] == "v":
                    take_v(ev[1])
                    if ev[1] == 0:
                        put_qk(15)
                elif ev[0] == "scores":
                    n = ev[1]
                    L = (attention_step(n)[1] + 1) * P
                    act.wait_ge(s_max, n + 1)
                    if n % 8 == 0 and n >= 16:
                        act.wait_ge(s_att, n // 8 - 1)
                    f(prob[:, n % 2, 0:L], prob[:, n % 2, 0:L], ACT.Exp, bias=nmx[:, n % 2:n % 2 + 1],
                      accum_out=Z[:, n // 8 % 2, n % 8:n % 8 + 1]).then_inc(s_exp, 1)
                elif ev[0] == "dn":
                    dn(ev[1], ev[2])
                elif ev[0] == "turn":
                    n = ev[1]
                    for g, cnt in turn_groups(n):
                        if TAKER[idx] == "a":
                            act.wait_ge(s_turn, idx + 1)
                            if n >= 2:
                                act.wait_ge(s_values, n - 1)
                            f(probT[:, n % 2, g * P:(g + cnt) * P], ps[:, 4 + idx % 2, 0:cnt * P], ACT.Copy)\
                                .then_inc(s_turned_a, 1)
                        idx += 1
                elif ev[0] == "att_out":
                    i = ev[1]
                    if TAKER[idx] == "a":
                        act.wait_ge(s_turn, idx + 1)
                        f(att_place(i), flipped(ps[:, 4 + idx % 2, :].rearrange("p (c n) -> p c n", c=4)),
                          ACT.Copy).then_inc(s_turned_a, 1)
                    idx += 1

            act.wait_ge(d_pe, len(PE_ORDER))
            act.wait_ge(d_dve, len(DVE_ORDER))

            def rows2(t):
                act.wait_ge(h2_turned, t + 1)
                if t >= 2:
                    act.wait_ge(logit_mm, t - 1)
                f(h2T[:, t % 2].rearrange("p k n -> p (k n)"), ps[:, 4:6, :].rearrange("p b n -> p (b n)"), ACT.Copy)\
                    .then_inc(h2T_done, 1)

            for t in range(TILES):
                act.wait_ge(x2_done, t + 1)
                act.wait_ge(x2_sq, t)
                f(junk3, xs[:, t % 2, :], ACT.Square, accum_out=ss[:, t:t + 1]).then_inc(x2_sq, 1)
                if t:
                    rows2(t - 1)
            rows2(TILES - 1)
            act.wait_ge(route_v, 1)
            f(gexp, gexp, ACT.Exp)
            f(e_diff, e_diff, ACT.Exp).then_inc(route_a, 1)

            def rowsT(slot, u):
                act.wait_ge(rows_turned, slot + 1)
                at_least(act, gu_mm, slot - 1)
                f(hgT[:, u, 0:4, :], ps[:, 0, :].rearrange("p (k n) -> p k n", k=4), ACT.Copy).then_inc(rowsT_a, 1)

            def gate(slot):
                act.wait_ge(gu_mm, slot + 1)
                at_least(act, act_done, slot)
                f(silu_g, ps[:, 2, :], ACT.Silu).then_inc(silu_done, 1)

            def put_act(slot):
                act.wait_ge(act_turned, slot + 1)
                at_least(act, down_mm, slot)
                f(actT.rearrange("p k n -> p (k n)"), ps[:, 4, :], ACT.Copy).then_inc(actT_done, 1)

            def result(slot, u, pair):
                act.wait_ge(down_mm, slot + 1)
                at_least(act, y_out[u], pair * 16)
                f(ys[:, u, 0:512], ps[:, 5, :], ACT.Copy).then_inc(y_a, 1)

            def expert(slot, u, pair):
                gate(slot)
                rowsT(slot + 1, 1 - u)
                if not (isinstance(slot, int) and slot == 0):
                    result(slot - 1, 1 - u, pair + u - 1)
                put_act(slot)

            act.wait_ge(slots_ready, 1)
            rowsT(0, 0)
            experts_loop(act, expert)
            act.wait_ge(extras_ready, 1)
            extras_loop(act, expert, result)

        @block.gpsimd
        def _(pool):
            tt, ts = nc.gpsimd.tensor_tensor, nc.gpsimd.tensor_scalar
            pool.wait_ge(consts_in, 16)
            for t in range(TILES):
                pool.wait_ge(sumsq_done, t + 1)
                ts(ss[:, t:t + 1], ss[:, t:t + 1], 1.0 / D, EPS, ALU.mult, ALU.add).then_inc(meansq_done, 1)
                pool.wait_ge(meansq_done, t + 1)
                tt(rs[:, t:t + 1], ss[:, t:t + 1], half_neg[:, 0:1], ALU.pow).then_inc(rms_done, 1)
            for j in range(16):
                pool.wait_ge(*act_taken(FIRST_QK + j))
                if j:
                    pool.wait_ge(qk_ss, j)
                tt(sqb, stage[:, j % 2, :], stage[:, j % 2, :], ALU.mult).then_inc(qk_sq, 1)
                pool.wait_ge(qk_ss, j + 1)
                if j >= 2:
                    pool.wait_ge(qk_normed, j - 1)
                tt(rs2[:, j % 2, :], ss2[:, j % 2, :], half_neg, ALU.pow).then_inc(qk_rs, 1)

            pool.wait_ge(qk_turned, 16)
            pool.wait_ge(gate_a, 5)

            def dn(i, k):
                if k >= len(DN_PIECES):
                    return
                piece = DN_PIECES[k]
                ti = slice(4 * i, 4 * i + 4)
                h4 = lambda x: x.rearrange("p (h d) -> p h d", d=HD)
                if piece == "split":
                    if i:
                        pool.wait_ge(d_pe, pe_at(i - 1, "gb"))
                    for h in range(4):
                        last = ts(Tg[:, h, :], tri, g_col[:, 4 * i + h:4 * i + h + 1], None, ALU.mult)
                    last.then_inc(d_pool, 1)
                    pool.wait_ge(d_act, act_at(i, "split"))
                    if i:
                        pool.wait_ge(d_dve, dve_at(i - 1, "ss"))
                    if i >= 2:
                        pool.wait_ge(d_dve, dve_at(i - 2, "osum"))
                    tt(dsq, tok[:, 0:512], tok[:, 0:512], ALU.mult).then_inc(d_pool, 1)
                elif piece == "ss":
                    pool.wait_ge(d_dve, dve_at(i, "ss"))
                    tt(drs, dss, half_neg, ALU.pow).then_inc(d_pool, 1)
                elif piece == "qkn":
                    pool.wait_ge(d_dve, dve_at(i, "qkn"))
                    if i:
                        pool.wait_ge(d_pe, pe_at(i - 1, "norm"))
                    if i >= 2:
                        pool.wait_ge(d_pe, pe_at(i - 2, "emit"))
                    tt(h4(kb), h4(tok[:, 256:512]), bc_h(beta[:, ti]), ALU.mult).then_inc(d_pool, 1)
                    tt(h4(kd[i % 2]), h4(tok[:, 256:512]), bc_h(ekd[:, ti]), ALU.mult)
                    tt(h4(vb[i % 2]), h4(tok[:, 512:768]), bc_h(beta[:, ti]), ALU.mult)
                    nc.gpsimd.drain().then_inc(d_pool, 1)
                elif piece == "gram":
                    pool.wait_ge(d_dve, dve_at(i, "gram"))
                    if i:
                        pool.wait_ge(d_pe, pe_at(i - 1, f"x{LEVELS - 1}"))
                    tt(AM[:, 1], At, bc_f(lvl(1), 4), ALU.mult).then_inc(d_pool, 1)
                elif piece[0] == "x" and int(piece[1:]) < LEVELS - 1:
                    lv = int(piece[1:]) + 1
                    if lv == 2:
                        pool.wait_ge(d_dve, dve_at(i, "inv1"))
                    else:
                        pool.wait_ge(d_pe, pe_at(i, f"x{lv - 2}"))
                    tt(AM[:, lv % 2], At, bc_f(lvl(lv), 4), ALU.mult).then_inc(d_pool, 1)
                elif piece == "emit":
                    pool.wait_ge(d_dve, dve_at(i, "emit"))
                    tt(dsq[:, 0:256], o1, o1, ALU.mult).then_inc(d_pool, 1)
                elif piece == "osum":
                    pool.wait_ge(d_dve, dve_at(i, "osum"))
                    tt(drs[:, 0:4], dss[:, 0:4], half_neg[:, 0:4], ALU.pow).then_inc(d_pool, 1)

            for ev in SCHEDULE:
                if ev[0] == "dn":
                    dn(ev[1], ev[2])

            pool.wait_ge(d_dve, len(DVE_ORDER))
            for t in range(TILES):
                pool.wait_ge(x2_sq, t + 1)
                ts(ss[:, t:t + 1], ss[:, t:t + 1], 1.0 / D, EPS, ALU.mult, ALU.add).then_inc(x2_ms, 1)
                pool.wait_ge(x2_ms, t + 1)
                tt(rs[:, t:t + 1], ss[:, t:t + 1], half_neg[:, 0:1], ALU.pow).then_inc(x2_rs, 1)

            def gather(slot, u, pair):
                nc.gpsimd.tensor_copy(tok_b[:, u:u + 1], tok_of[:, bass.ds(slot, 1)])
                at_least(pool, rows_turned, slot - 1)
                tt(tok_t[:, u:u + 1], zero256[:, 0:1], zero256[:, 0:1], ALU.add)
                nc.gpsimd.drain()
                nc.gpsimd.indirect_dma_start(hg[:, u, :], None, h2_dram, bass.IndirectOffsetOnAxis(ap=tok_b[:, u:u + 1], axis=0),
                                             bounds_check=SEQ - 1, oob_is_err=False).then_inc(rows_in[u], 16)

            def scatter(slot, u, pair):
                nc.gpsimd.tensor_copy(dst_b[:, u:u + 1], dst_of[:, bass.ds(slot, 1)])
                pool.wait_ge(y_v, slot + 1)
                pool.wait_ge(y_a, slot + 1)
                tt(dst_t[:, u:u + 1], zero256[:, 0:1], zero256[:, 0:1], ALU.add)
                nc.gpsimd.drain()
                nc.gpsimd.tensor_copy(dst_i[:, u:u + 1], dst_b[:, u:u + 1])
                nc.gpsimd.drain()
                nc.gpsimd.indirect_dma_start(y_dram, bass.IndirectOffsetOnAxis(ap=dst_i[:, u:u + 1], axis=0), ys[:, u, :], None,
                                             bounds_check=2 * SEQ - 1, oob_is_err=False).then_inc(y_out[u], 16)

            def expert(slot, u, pair):
                gather(slot + 2, u, pair + 1)
                if not (isinstance(slot, int) and slot == 0):
                    scatter(slot - 1, 1 - u, pair + u - 1)

            pool.wait_ge(hg_zero, 1)
            pool.wait_ge(slots_ready, 1)
            for u in range(2):
                pool.wait_ge(h2_out[u], 16 * TILES // 2)
            gather(0, 0, 0)
            gather(1, 1, 0)
            pool.wait_ge(extras_ready, 1)
            experts_loop(pool, expert)

            def finish(slot, u, pair):
                scatter(slot, u, pair)
                pool.wait_ge(y_out[u], 16 * (pair + 1))
                pool.wait_ge(y_out[1 - u], 16 * (pair + u))

            extras_loop(pool, expert, finish)
            nc.gpsimd.drain().then_inc(y_all_out, 1)


def lay_out(inputs):
    f = {k: np.asarray(v) for k, v in inputs.items()}
    cols = [f["cv_dw"][0].T.reshape(2, P, CV_TAPS).transpose(1, 0, 2).reshape(P, -1),
            f["dn_conv"][0].T.reshape(6, P, DN_TAPS).transpose(1, 0, 2).reshape(P, -1),
            f["norm_mix"][0].reshape(KC, P).T,
            f["cv_dw_bias"][0].reshape(2, P).T, f["cv_ln_g"][0].reshape(2, P).T, f["cv_ln_b"][0].reshape(2, P).T,
            np.tile(f["at_q_norm"][0], 2)[:, None], np.tile(f["at_k_norm"][0], 2)[:, None],
            np.broadcast_to(f["dn_a_log"][0], (P, DN_HEADS)), np.broadcast_to(f["dn_dt_bias"][0], (P, DN_HEADS)),
            np.broadcast_to(f["dn_out_norm"][0], (P, HD))]
    table = np.ones((P, 36), np.float32)
    table[:N_BUCKETS, :AT_HEADS] = f["rel_bias"]
    cols.append(table)
    cols.append(np.broadcast_to(np.concatenate([f["router_group_b"][0], f["router_expert_b"][0]]), (P, GROUPS + EXPERTS)))
    return {
        "x": f["x"].reshape(SEQ, D), "constants": shape_constants(), "distances": distance_constants(),
        "params": np.ascontiguousarray(np.concatenate(cols, 1)),
        "w_in": f["w_in"].reshape(D, N_IN), "w_out": f["w_out"].reshape(D, D),
        "norm_ffn": np.ascontiguousarray(np.broadcast_to(f["norm_ffn"][0], (P, D))),
        "router": np.ascontiguousarray(np.concatenate([f["router_group_w"][0], f["router_expert_w"][0]], 1)),
        "ex_gate": f["ex_gate"][0], "ex_up": f["ex_up"][0], "ex_down": f["ex_down"][0],
    }


def kernel(**inputs):
    import concourse.bacc as _bacc
    from concourse.bass_utils import run_bass_kernel_spmd as _run

    arrays = lay_out(inputs)
    nc = _bacc.Bacc("TRN2", target_bir_lowering=False, num_devices=1)
    args = {k: nc.dram_tensor(f"in_{k}", v.shape, mybir.dt.from_np(v.dtype), kind="ExternalInput").ap()
            for k, v in arrays.items()}
    out = nc.dram_tensor("out", [SEQ, D], F32, kind="ExternalOutput").ap()
    build(nc, args, out)
    r = _run(nc, [{f"in_{k}": v for k, v in arrays.items()}], core_ids=[0])
    return r.results[0]["out"].reshape(1, SEQ, D)
```
